# Optimizing a Trainium2 kernel written in Bass

```python
import jax
import jax.numpy as jnp
from jax import lax
import numpy as np

"""Two-layer hybrid decoder trunk.

Layer 0 (even): parallel head groups mLSTM (xLSTM matrix memory) + HGRN2 (gated linear
recurrence with state expansion) behind one combined input projection and one output
projection; layer 1 (odd): FoX forgetting attention. Every layer then cross-attends into
256 memory tokens and applies a squared-ReLU MLP; pre-RMSNorm everywhere, final RMSNorm.
Inputs: x (BATCH, SEQ, D_MODEL), mem (BATCH, 256, D_MODEL) + weights.
Output: (BATCH, SEQ, D_MODEL).
"""

D_MODEL = 1024
BATCH = 1
SEQ = 256
DEPTH = 2

MEM_LEN = 256
A_HEADS = 4
A_DIM = 128
B_HEADS = 4
B_DK = 128
B_DV = 128
CONV_W = 4
CHUNK = 64
C_HEADS = 8
C_DIM = D_MODEL // C_HEADS
Q_BLOCK = 128
X_HEADS = 4
X_DIM = D_MODEL // X_HEADS
D_FF = 4 * D_MODEL
EPS = 1e-6
N_EVEN = (DEPTH + 1) // 2
N_ODD = DEPTH // 2
A_W = A_HEADS * A_DIM
B_KW = B_HEADS * B_DK
B_VW = B_HEADS * B_DV
AB_SIZES = (A_W, A_W, A_W, A_W, A_HEADS, A_HEADS, B_KW, B_KW, B_VW, B_VW)
AB_IN = 4 * A_W + 2 * A_HEADS + 2 * B_KW + 2 * B_VW
C_SIZES = (D_MODEL, D_MODEL, D_MODEL, D_MODEL, C_HEADS)
C_IN = 4 * D_MODEL + C_HEADS

kernel_name = 'hybrid_mlstm_hgrn2_fox_trunk'

def _split(z, sizes):
    offs = [int(o) for o in np.cumsum(sizes)[:-1]]
    return jnp.split(z, offs, axis=-1)

def rmsnorm(x, g):
    xf = x.astype(jnp.float32)
    y = xf * lax.rsqrt(jnp.mean(xf * xf, axis=-1, keepdims=True) + EPS)
    return (y * g.astype(jnp.float32)).astype(x.dtype)

def _heads(a, h):
    return a.reshape(a.shape[0], a.shape[1], h, -1)

def _to_chunks(a):
    b, s, h = a.shape[:3]
    a = a.reshape((b, s // CHUNK, CHUNK, h) + a.shape[3:])
    return jnp.moveaxis(a, (1, 3), (0, 2))

def _from_chunks(a):
    a = jnp.moveaxis(a, (0, 2), (1, 3))
    return a.reshape((a.shape[0], a.shape[1] * a.shape[2]) + a.shape[3:])

def causal_conv_silu(u, w):
    s = u.shape[1]
    up = jnp.pad(u, ((0, 0), (CONV_W - 1, 0), (0, 0)))
    y = up[:, 0:s] * w[0]
    for j in range(1, CONV_W):
        y = y + up[:, j:j + s] * w[j]
    return jax.nn.silu(y)

def mlstm_chunkwise(q, k, v, i_pre, f_pre):
    bn, s, h, d = q.shape
    q = q.astype(jnp.float32)
    k = k.astype(jnp.float32) * (d ** -0.5)
    v = v.astype(jnp.float32)
    logf = jax.nn.log_sigmoid(f_pre)
    xs = (_to_chunks(q), _to_chunks(k), _to_chunks(v), _to_chunks(i_pre), _to_chunks(logf))
    causal = jnp.tril(jnp.ones((CHUNK, CHUNK), dtype=bool))

    def step(carry, inp):
        cmat, nvec, m = carry
        qb, kb, vb, ib, fb = inp
        bcum = jnp.cumsum(fb, axis=-1)
        logd = bcum[..., :, None] - bcum[..., None, :] + ib[..., None, :]
        logd = jnp.where(causal, logd, -jnp.inf)
        inter = bcum + m[..., None]
        m_t = jnp.maximum(inter, jnp.max(logd, axis=-1))
        w_inter = jnp.exp(inter - m_t)
        sc = jnp.einsum('bhtd,bhsd->bhts', qb, kb) * jnp.exp(logd - m_t[..., None])
        num = (jnp.einsum('bhts,bhsd->bhtd', sc, vb)
               + w_inter[..., None] * jnp.einsum('bhtd,bhde->bhte', qb, cmat))
        den = jnp.sum(sc, axis=-1) + w_inter * jnp.einsum('bhtd,bhd->bht', qb, nvec)
        hout = num / jnp.maximum(jnp.abs(den), jnp.exp(-m_t))[..., None]
        b_last = bcum[..., -1]
        log_in = b_last[..., None] - bcum + ib
        m_new = jnp.maximum(b_last + m, jnp.max(log_in, axis=-1))
        w_s = jnp.exp(log_in - m_new[..., None])
        decay = jnp.exp(b_last + m - m_new)
        c_new = decay[..., None, None] * cmat + jnp.einsum('bhs,bhsd,bhse->bhde', w_s, kb, vb)
        n_new = decay[..., None] * nvec + jnp.einsum('bhs,bhsd->bhd', w_s, kb)
        return (c_new, n_new, m_new), hout

    init = (jnp.zeros((bn, h, d, d), jnp.float32), jnp.zeros((bn, h, d), jnp.float32),
            jnp.zeros((bn, h), jnp.float32))
    _, hs = lax.scan(step, init, xs)
    return _from_chunks(hs)

def hgrn2_chunkwise(q, k, v, logf):
    bn, s, h, dk = q.shape
    dv = v.shape[-1]
    xs = (_to_chunks(q), _to_chunks(k), _to_chunks(v), _to_chunks(logf))
    causal = jnp.tril(jnp.ones((CHUNK, CHUNK), dtype=bool))[:, :, None]

    def step(state, inp):
        qb, kb, vb, gb = inp
        bcum = jnp.cumsum(gb, axis=2)
        rel = bcum[:, :, :, None, :] - bcum[:, :, None, :, :]
        rel = jnp.where(causal, rel, -jnp.inf)
        a = jnp.einsum('bhtc,bhsc,bhtsc->bhts', qb, kb, jnp.exp(rel))
        o = (jnp.einsum('bhts,bhse->bhte', a, vb)
             + jnp.einsum('bhtc,bhce->bhte', qb * jnp.exp(bcum), state))
        b_last = bcum[:, :, -1]
        s_new = (jnp.exp(b_last)[..., None] * state
                 + jnp.einsum('bhsc,bhse->bhce', kb * jnp.exp(b_last[:, :, None] - bcum), vb))
        return s_new, o

    _, os_ = lax.scan(step, jnp.zeros((bn, h, dk, dv), jnp.float32), xs)
    return _from_chunks(os_)

def forgetting_attention(q, k, v, logf):
    bn, s, h, d = q.shape
    nb = s // Q_BLOCK
    c = jnp.moveaxis(jnp.cumsum(logf, axis=1), 1, 2)
    qb = q.reshape(bn, nb, Q_BLOCK, h, d).transpose(1, 0, 3, 2, 4)
    cq = c.reshape(bn, h, nb, Q_BLOCK).transpose(2, 0, 1, 3)
    kpos = jnp.arange(s)

    def block(args):
        qi, cqi, bidx = args
        qpos = bidx * Q_BLOCK + jnp.arange(Q_BLOCK)
        logits = (jnp.einsum('bhqd,bshd->bhqs', qi, k).astype(jnp.float32) * (d ** -0.5)
                  + cqi[..., None] - c[:, :, None, :])
        logits = jnp.where(kpos[None, :] <= qpos[:, None], logits, -jnp.inf)
        p = jax.nn.softmax(logits, axis=-1)
        return jnp.einsum('bhqs,bshd->bqhd', p.astype(v.dtype), v)

    out = lax.map(block, (qb, cq, jnp.arange(nb)))
    return out.transpose(1, 0, 2, 3, 4).reshape(bn, s, h, d)

def mixer_ab(u, w_in, conv_w, gate_b, lb, norm_a, norm_b, w_out):
    bn, s, _ = u.shape
    z = u @ w_in
    qa, ka, va, oa, ia, fa, qb, fb, ib, gb = _split(z, AB_SIZES)
    qa, ka = jnp.split(causal_conv_silu(jnp.concatenate([qa, ka], axis=-1), conv_w), 2, axis=-1)
    gates = jnp.concatenate([ia, fa], axis=-1).astype(jnp.float32) + gate_b
    i_pre, f_pre = jnp.split(gates, 2, axis=-1)
    ha = mlstm_chunkwise(_heads(qa, A_HEADS), _heads(ka, A_HEADS), _heads(va, A_HEADS), i_pre, f_pre)
    ha = jax.nn.sigmoid(_heads(oa, A_HEADS).astype(jnp.float32)) * ha
    ha = rmsnorm(ha, norm_a.reshape(A_HEADS, A_DIM)).reshape(bn, s, A_W)
    zf = fb.astype(jnp.float32)
    logf = jnp.log(lb + (1.0 - lb) * jax.nn.sigmoid(zf))
    kf = (1.0 - lb) * jax.nn.sigmoid(-zf)
    hb = hgrn2_chunkwise(_heads(jax.nn.silu(qb.astype(jnp.float32)), B_HEADS), _heads(kf, B_HEADS),
                         _heads(jax.nn.silu(ib.astype(jnp.float32)), B_HEADS), _heads(logf, B_HEADS))
    hb = rmsnorm(hb, norm_b.reshape(B_HEADS, B_DV)) * jax.nn.silu(_heads(gb, B_HEADS).astype(jnp.float32))
    hb = hb.reshape(bn, s, B_VW)
    y = jnp.concatenate([ha, hb], axis=-1).astype(u.dtype)
    return y @ w_out

def mixer_c(u, w_in, f_b, q_norm, k_norm, w_out):
    bn, s, _ = u.shape
    z = u @ w_in
    q, k, v, g, f = _split(z, C_SIZES)
    q = rmsnorm(_heads(q, C_HEADS), q_norm)
    k = rmsnorm(_heads(k, C_HEADS), k_norm)
    logf = jax.nn.log_sigmoid(f.astype(jnp.float32) + f_b)
    o = forgetting_attention(q, k, _heads(v, C_HEADS), logf).reshape(bn, s, D_MODEL)
    o = (o.astype(jnp.float32) * jax.nn.sigmoid(g.astype(jnp.float32))).astype(u.dtype)
    return o @ w_out

def memory_cross_attention(u, mem_k, mem_v, w_q, w_o):
    bn, s, _ = u.shape
    q = _heads(u @ w_q, X_HEADS)
    logits = jnp.einsum('bshd,bmhd->bhsm', q, mem_k).astype(jnp.float32) * (X_DIM ** -0.5)
    p = jax.nn.softmax(logits, axis=-1)
    o = jnp.einsum('bhsm,bmhd->bshd', p.astype(mem_v.dtype), mem_v).reshape(bn, s, D_MODEL)
    return o @ w_o

def squared_relu_mlp(u, w1, w2):
    return jnp.square(jax.nn.relu(u @ w1)) @ w2

def setup_inputs(seed: int = 0) -> dict:
    key = jax.random.key(seed)
    ks = jax.random.split(key, 32)

    def nrm(k, shape):
        return jax.random.normal(k, shape, jnp.float32)

    def dense(k, shape, fan_in):
        return nrm(k, shape) * (fan_in ** -0.5)

    def gain(k, shape):
        return 1.0 + 0.02 * nrm(k, shape)

    ab_gate_b = jnp.concatenate(
        [0.1 * nrm(ks[10], (N_EVEN, A_HEADS)),
         jnp.linspace(3.0, 6.0, A_HEADS)[None, :] + 0.1 * nrm(ks[11], (N_EVEN, A_HEADS))], axis=-1)
    c_fgate_b = jnp.linspace(1.0, 5.0, C_HEADS)[None, :] + 0.1 * nrm(ks[17], (N_ODD, C_HEADS))
    return {
        'x': nrm(ks[0], (BATCH, SEQ, D_MODEL)),
        'mem': nrm(ks[1], (BATCH, MEM_LEN, D_MODEL)),
        'norm_mix_g': gain(ks[2], (DEPTH, D_MODEL)),
        'norm_xattn_g': gain(ks[3], (DEPTH, D_MODEL)),
        'norm_mlp_g': gain(ks[4], (DEPTH, D_MODEL)),
        'final_norm_g': gain(ks[5], (D_MODEL,)),
        'ab_w_in': dense(ks[6], (N_EVEN, D_MODEL, AB_IN), D_MODEL),
        'ab_conv_w': dense(ks[7], (N_EVEN, CONV_W, 2 * A_W), CONV_W),
        'ab_gate_b': ab_gate_b,
        'hgrn_lb_logits': 0.1 * nrm(ks[8], (N_EVEN + 1, B_KW)),
        'mlstm_norm_g': gain(ks[9], (N_EVEN, A_W)),
        'hgrn_norm_g': gain(ks[12], (N_EVEN, B_VW)),
        'ab_w_out': dense(ks[13], (N_EVEN, A_W + B_VW, D_MODEL), A_W + B_VW),
        'c_w_in': dense(ks[14], (N_ODD, D_MODEL, C_IN), D_MODEL),
        'c_fgate_b': c_fgate_b,
        'c_qnorm_g': gain(ks[15], (N_ODD, C_DIM)),
        'c_knorm_g': gain(ks[16], (N_ODD, C_DIM)),
        'c_w_out': dense(ks[18], (N_ODD, D_MODEL, D_MODEL), D_MODEL),
        'mem_norm_g': gain(ks[19], (D_MODEL,)),
        'mem_w_kv': dense(ks[20], (D_MODEL, 2 * D_MODEL), D_MODEL),
        'xa_w_q': dense(ks[21], (DEPTH, D_MODEL, D_MODEL), D_MODEL),
        'xa_w_o': dense(ks[22], (DEPTH, D_MODEL, D_MODEL), D_MODEL),
        'mlp_w1': dense(ks[23], (DEPTH, D_MODEL, D_FF), D_MODEL),
        'mlp_w2': dense(ks[24], (DEPTH, D_FF, D_MODEL), D_FF),
    }

def reference(x, mem, norm_mix_g, norm_xattn_g, norm_mlp_g, final_norm_g,
              ab_w_in, ab_conv_w, ab_gate_b, hgrn_lb_logits, mlstm_norm_g, hgrn_norm_g, ab_w_out,
              c_w_in, c_fgate_b, c_qnorm_g, c_knorm_g, c_w_out,
              mem_norm_g, mem_w_kv, xa_w_q, xa_w_o, mlp_w1, mlp_w2):
    bn, m_len, _ = mem.shape
    mem_k, mem_v = jnp.split(rmsnorm(mem, mem_norm_g) @ mem_w_kv, 2, axis=-1)
    mem_k = mem_k.reshape(bn, m_len, X_HEADS, X_DIM)
    mem_v = mem_v.reshape(bn, m_len, X_HEADS, X_DIM)
    lb_all = jnp.cumsum(jax.nn.softmax(hgrn_lb_logits.astype(jnp.float32), axis=0), axis=0)
    h = x
    for layer in range(DEPTH):
        u = rmsnorm(h, norm_mix_g[layer])
        if layer % 2 == 0:
            e = layer // 2
            h = h + mixer_ab(u, ab_w_in[e], ab_conv_w[e], ab_gate_b[e], lb_all[e],
                             mlstm_norm_g[e], hgrn_norm_g[e], ab_w_out[e])
        else:
            o = layer // 2
            h = h + mixer_c(u, c_w_in[o], c_fgate_b[o], c_qnorm_g[o], c_knorm_g[o], c_w_out[o])
        h = h + memory_cross_attention(rmsnorm(h, norm_xattn_g[layer]), mem_k, mem_v,
                                       xa_w_q[layer], xa_w_o[layer])
        h = h + squared_relu_mlp(rmsnorm(h, norm_mlp_g[layer]), mlp_w1[layer], mlp_w2[layer])
    return rmsnorm(h, final_norm_g)


_drawn_inputs = setup_inputs


def setup_inputs(seed=0):
    import zlib

    import numpy as np

    out = dict(_drawn_inputs(seed))
    spreads = {}
    factors = {'norm_xattn_g': 8.0,
     'norm_mlp_g': 2.699,
     'final_norm_g': 7.326,
     'hgrn_lb_logits': 8.0,
     'mlstm_norm_g': 4.49,
     'hgrn_norm_g': 7.967,
     'c_qnorm_g': 8.0,
     'c_knorm_g': 28.654,
     'mem_norm_g': 8.0}
    for name, (base, spread) in spreads.items():
        noise = np.random.default_rng([zlib.crc32(name.encode()), seed]).standard_normal(out[name].shape)
        drawn = base * np.exp(spread * noise) if base else spread * noise
        out[name] = jnp.asarray(drawn.astype(out[name].dtype))
    for name, factor in factors.items():
        out[name] = (out[name] * factor).astype(out[name].dtype)
    return out
```

```python
from contextlib import ExitStack, contextmanager

import numpy as np

import concourse.bass as bass
from concourse import mybir

F32 = mybir.dt.float32
F32R = mybir.dt.float32r
U8 = mybir.dt.uint8
ALU = mybir.AluOpType
ACT = mybir.ActivationFunctionType
AX = mybir.AxisListType

P = 128
BANK = 512
T = 256
MT = T // P
D = 1024
KD = D // P
FF = 4 * D
NJ = FF // BANK
HM = 4
HC = 8
HX = 4
XD = D // HX
EPS = 1e-6
NEG = -(2.0 ** 100)
RING = 4
RAW = 2
KU = 4
LEVELS = [0, 64, 32, 16, 8, 4, 2, 1, 128]

PARAMS = [("norm_mix", 16), ("norm_xattn", 16), ("norm_mlp", 16), ("mem_norm", 8), ("mix_out", 8),
          ("conv", 32), ("lb", 8), ("qn", 1), ("kn", 1)]
PROW = {}
_n = 0
for _name, _rows in PARAMS:
    PROW[_name] = _n
    _n += _rows
NPAR = _n

TURN = {4: 1, 5: 1, 6: 1, 7: 1}
STAGES = [
    ("params", {7: 1}), ("turn_mem", TURN), ("kv", {0: 2, 2: 2}),
    ("turn_mix0", TURN), ("gate0", {4: 1}), ("in0", {0: 4, 2: 4}),
    ("mlstm", {0: 1, 1: 1, 2: 1, 3: 1, 4: 2, 5: 3, 6: 2, 7: 2}),
    ("hgrn", {0: 1, 1: 1, 4: 5, 5: 4, 6: 4, 7: 4}),
    ("turn_y0", TURN), ("out0", {0: 1, 2: 1}),
    ("turn_x0", TURN), ("xq0", {0: 1, 2: 1}), ("xattn0", {b: 2 for b in range(6)}),
    ("xo0", {0: 1, 2: 1}),
    ("turn_m0", TURN), ("mlp0", {0: 1, 2: 1, 4: NJ}),
    ("turn_mix1", TURN), ("gate1", {4: 1}), ("in1", {0: 4, 2: 4}),
    ("turn_q", TURN), ("turn_k", TURN), ("fox", {b: HC // 2 for b in range(6)}),
    ("turn_y1", TURN), ("out1", {0: 1, 2: 1}),
    ("turn_x1", TURN), ("xq1", {0: 1, 2: 1}), ("xattn1", {b: 2 for b in range(6)}),
    ("xo1", {0: 1, 2: 1}),
    ("turn_m1", TURN), ("mlp1", {0: 1, 2: 1, 4: NJ}),
]
FILLED = {}
_at = [0] * 8
for _name, _banks in STAGES:
    FILLED[_name] = list(_at)
    for _b, _k in _banks.items():
        _at[_b] += _k

UNITS = {}
_u = 0
for _name, _k in [("kv", 8), ("in0", 16), ("out0", 4), ("xq0", 4), ("xo0", 4), ("mlp0", 4 * NJ),
                  ("in1", 16), ("out1", 4), ("xq1", 4), ("xo1", 4), ("mlp1", 4 * NJ)]:
    UNITS[_name] = _u
    _u += _k
NU = _u

VERSION = {n: i for i, n in enumerate(["turn_mem", "turn_mix0", "turn_y0", "turn_x0", "xattn0", "turn_m0",
                                       "turn_mix1", "turn_y1", "turn_x1", "xattn1", "turn_m1"])}
SOURCE = {n: i for i, n in enumerate(["turn_mem", "turn_mix0", "turn_y0", "turn_x0", "turn_m0",
                                      "turn_mix1", "turn_x1", "turn_m1"])}
GAIN = {"turn_mem": PROW["mem_norm"], "turn_mix0": PROW["norm_mix"], "turn_mix1": PROW["norm_mix"] + 8,
        "turn_y0": PROW["mix_out"], "turn_y1": None, "turn_x0": PROW["norm_xattn"],
        "turn_x1": PROW["norm_xattn"] + 8, "turn_m0": PROW["norm_mlp"], "turn_m1": PROW["norm_mlp"] + 8}
NORMS = {n: i for i, n in enumerate(["turn_mem", "turn_mix0", "turn_x0", "turn_m0", "turn_mix1", "turn_x1",
                                     "turn_m1", "final"])}
ROOTS = {n: i for i, n in enumerate(["turn_mem", "turn_mix0", "mlstm", "hgrn", "turn_x0", "turn_m0", "turn_mix1",
                                     "q", "k", "turn_x1", "turn_m1", "final"])}
SUMS = {n: i for i, n in enumerate(["out0", "xo0", "mlp0", "out1", "xo1", "mlp1"])}
SUM_BEFORE = {"turn_mix0": 0, "turn_x0": 1, "turn_m0": 2, "turn_mix1": 3, "turn_x1": 4, "turn_m1": 5, "final": 6}

IN0 = [("qb", 2056, True), ("fb", 2568, True), ("qa", 0, True), ("ka", 512, True),
       ("va", 1024, False), ("oa", 1536, False), ("ib", 3080, False), ("gb", 3592, False)]
CONV0 = {"qa": 0, "ka": HM}
EXP_BEFORE = {}
for _name, _, _ in IN0:
    EXP_BEFORE[_name] = len([n for n in EXP_BEFORE if n != "va"])
GATE0, GATE1 = 2048, 4096


def trunk(nc, x, mem, norm_mix_g, norm_xattn_g, norm_mlp_g, final_norm_g, ab_w_in, ab_conv_w, ab_gate_b,
          hgrn_lb_logits, mlstm_norm_g, hgrn_norm_g, ab_w_out, c_w_in, c_fgate_b, c_qnorm_g, c_knorm_g,
          c_w_out, mem_norm_g, mem_w_kv, xa_w_q, xa_w_o, mlp_w1, mlp_w2, out):
    ctx = ExitStack()
    with ctx:
        place = [nc.sbuf_base + (-nc.sbuf_base) % 64]

        def sb(name, shape, dt=F32, at=None):
            size = int(np.prod(shape[1:])) * (1 if dt == U8 else 4)
            size += (-size) % 64
            where = place[0] if at is None else at[0]
            t = nc.alloc_sbuf_tensor_at(name, shape, dt, offset=where)
            if at is None:
                place[0] += size
            else:
                at[0] += size
            return t

        def sem(name):
            return ctx.enter_context(nc.semaphore(name))

        bank = [ctx.enter_context(nc.psum_tensor(f"bank{b}", [P, BANK], F32)) for b in range(8)]

        h = sb("h", [P, MT, D])
        u = sb("u", [P, MT, D])
        act_hi = sb("act_hi", [P, KD, T], F32R)
        act_lo = sb("act_lo", [P, KD, T], F32R)
        mem_kT = sb("mem_kT", [P, KD, T])
        mem_v = sb("mem_v", [P, MT, D])
        raw = sb("raw", [P, RAW, KU, BANK])
        w_hi = sb("w_hi", [P, RING, KU, BANK], F32R)
        w_lo = sb("w_lo", [P, RING, KU, BANK], F32R)
        ident = sb("ident", [P, P])
        after_T = sb("after_T", [P, P])
        after = sb("after", [P, P])
        select = sb("select", [HC, HC, P])
        ones_row = sb("ones_row", [HC, T])
        zeros_row = sb("zeros_row", [HC, T])
        pairs = sb("pairs", [P, len(LEVELS) - 1, P], U8)
        par = sb("par", [P, NPAR])
        gate_w = sb("gate_w", [P, KD, 8])
        gate_w1 = sb("gate_w1", [P, KD, 8])
        bias_i = sb("bias_i", [HM, 1])
        bias_f = sb("bias_f", [HM, 1])
        bias_c = sb("bias_c", [HC, 1])
        lb = sb("lb", [P, 6, HM])
        st = sb("st", [P, 8, 16])
        cols = sb("cols", [P, 2, MT * HM])
        q_gain = sb("q_gain", [P, 1])
        xs = sb("xs", [P, 4, 2 * MT])

        arena = place[0]
        a = [arena]
        qkT = sb("qkT", [P, 2 * HM, T], at=a)
        va = sb("va", [P, MT, HM, P + 1], at=a)
        oa = sb("oa", [P, MT, BANK], at=a)
        vb = sb("vb", [P, MT, BANK], at=a)
        gb = sb("gb", [P, MT, BANK], at=a)
        qb = sb("qb", [P, HM, T], at=a)
        kb = sb("kb", [P, HM, T], at=a)
        cum = sb("cum", [P, HM, T], at=a)
        dec = sb("dec", [P, 2, HM, T], at=a)
        pair_w = sb("pair_w", [P, MT, HM, P], at=a)
        pair_x = sb("pair_x", [P, HM, P], at=a)
        mix_end = a[0]
        qd = sb("qd", [P, 2, HM, T], at=a)
        kd = sb("kd", [P, 2, HM, T], at=a)
        a2 = [mix_end]
        decay = sb("decay", [P, 2, 3 * P], at=a2)
        weight = sb("weight", [P, 2, 3 * P], at=a2)
        rows = sb("rows", [HC, 8, T], at=a2)
        assert a[0] <= nc.sbuf_usable_end and a2[0] <= nc.sbuf_usable_end, (a[0], a2[0], nc.sbuf_usable_end)
        a = [arena]
        qc = sb("qc", [P, MT, D], at=a)
        kc = sb("kc", [P, MT, D], at=a)
        vc = sb("vc", [P, MT, D], at=a)
        gc = sb("gc", [P, MT, D], at=a)
        qcT = sb("qcT", [P, HC, T], at=a)
        kcT = sb("kcT", [P, HC, T], at=a)
        pc = sb("pc", [P, 2, 3 * P], at=a)
        pcT = sb("pcT", [P, 2, 3 * P], at=a)
        rows1 = sb("rows1", [HC, 6, T], at=a)
        csum = sb("csum", [P, 4, 2 * HC], at=a)
        a = [arena]
        xqT = sb("xqT", [P, KD, T], at=a)
        px = sb("px", [P, 2, MT, T], at=a)
        pxT = sb("pxT", [P, 2, MT, T], at=a)
        a = [arena]
        hid_hi = sb("hid_hi", [P, 2, KU, T], F32R, at=a)
        hid_lo = sb("hid_lo", [P, 2, KU, T], F32R, at=a)
        relu = sb("relu", [P, 2, BANK], at=a)
        hid = sb("hid", [P, 2, BANK], at=a)
        a = [arena]
        par_rows = sb("par_rows", [NPAR, P], at=a)
        pairs_f = sb("pairs_f", [P, len(LEVELS) - 1, P], at=a)
        a = [arena]
        final_g = sb("final_g", [P, D], at=a)
        squares = sb("squares", [P, MT, D], at=a)

        x_in, mem_in, par_in, small_in, gain_in, out_done = map(
            sem, ["x_in", "mem_in", "par_in", "small_in", "gain_in", "out_done"])
        raw_in = [sem(f"raw_in{i}") for i in range(RAW)]
        hi_ready, lo_ready, unit_used = sem("hi_ready"), sem("lo_ready"), sem("unit_used")
        full = [sem(f"bank_full{b}") for b in range(8)]
        consts, par_ready, lb_in, lb_exp = sem("consts"), sem("par_ready"), sem("lb_in"), sem("lb_exp")
        square_sum, root_in, root_seed = sem("square_sum"), sem("root_in"), sem("root_seed")
        source_ready, acthi_ready, actlo_ready = sem("source_ready"), sem("acthi_ready"), sem("actlo_ready")
        sum_done, kv_done, xq_done = sem("sum_done"), sem("kv_done"), sem("xq_done")
        dve_step, act_step, pool_step = sem("dve_step"), sem("act_step"), sem("pool_step")
        relu_ready, hid_ready, hidhi_ready, hidlo_ready = map(
            sem, ["relu_ready", "hid_ready", "hidhi_ready", "hidlo_ready"])
        in_done = [sem(f"in_done{b}") for b in range(4)]
        exp_ready, tap_ready, conv_done, forget_ready, log_forget = map(
            sem, ["exp_ready", "tap_ready", "conv_done", "forget_ready", "log_forget"])
        log_out, rows_ready, cols_ready = sem("log_out"), sem("rows_ready"), sem("cols_ready")
        decay_ready, weight_ready, y_ready, y_squared = map(
            sem, ["decay_ready", "weight_ready", "y_ready", "y_squared"])
        dist_ready, dec_ready, scaled_ready, selected, pairx_ready = map(
            sem, ["dist_ready", "dec_ready", "scaled_ready", "selected", "pairx_ready"])
        xmax, xexp, xnorm, xturned = map(sem, ["xmax", "xexp", "xnorm", "xturned"])
        squares_used, cnormed, qT_ready, kT_ready = map(sem, ["squares_used", "cnormed", "qT_ready", "kT_ready"])
        cmax, cexp, cturned, oc_done = map(sem, ["cmax", "cexp", "cturned", "oc_done"])
        fin_ready = sem("fin_ready")

        def wait_full(eng, stage, b, k=0):
            eng.wait_ge(full[b], FILLED[stage][b] + k + 1)

        def f(ap):
            return ap.bitcast(F32)

        def heads(ap, n=HM):
            return ap.rearrange("p (h d) -> p h d", h=n)

        def wait_chunk(eng, stage, c, i):
            if i == 0:
                wait_full(eng, stage, 2 * (c % 2), c // 2)
            else:
                eng.wait_ge(unit_used, UNITS[stage] + 2 * c + 2)

        def flat(ap):
            return ap.rearrange("p a b -> p (a b)")

        def spread(ap, n):
            return ap.unsqueeze(2).to_broadcast([P, ap.shape[1], n])

        def scratch(c, i):
            return u[:, i, (c % 2) * BANK:(c % 2 + 1) * BANK]

        def mlp_walk(eng, l, split, ahead, hidden):
            u0 = UNITS[f"mlp{l}"]

            def chunk(i, slot, which, j, buf):
                split(i + RING, slot % RING)
                if which == 1:
                    hidden(j, buf, i)
                split(i + 1 + RING, (slot + 1) % RING)

            for n, (which, j, buf) in enumerate([(1, 0, 0), (1, 1, 1), (2, 0, 0)]):
                chunk(u0 + 2 * n, u0 + 2 * n, which, j, buf)
            turns = (NJ - 2) // 2 - l
            with eng.Fori(0, turns) as it:
                for n, (which, j, buf) in enumerate(in_order(it)):
                    chunk(8 * it + (u0 + 6 + 2 * n), u0 + 6 + 2 * n, which, j, buf)
            if l == 1:
                for n, (which, j, buf) in enumerate(in_order(turns)):
                    i = u0 + 6 + 8 * turns + 2 * n
                    ahead(i)
                    if which == 1:
                        hidden(j, buf, i)
                    ahead(i + 1)
            ahead(u0 + 4 * NJ - 2)
            ahead(u0 + 4 * NJ - 1)

        def last_of_half(level):
            v = cum[:].rearrange("p h (b two l) -> p (h b) two l", two=2, l=level)
            return v, v[:, :, 0, level - 1:level].to_broadcast([P, HM * T // (2 * level), level])

        def halves(ap, level):
            return ap.rearrange("p h (b two l) -> p (h b) two l", two=2, l=level)

        def in_order(it, j0=2):
            j = j0 + 2 * it
            return [(1, j, 0), (2, j - 1, 1), (1, j + 1, 1), (2, j, 0)]

        block = ctx.enter_context(nc.Block())

        @block.sync
        def _(sp):
            def load(i, slot, src):
                if not (isinstance(i, int) and i < RAW):
                    sp.wait_ge(lo_ready, i - RAW + 1)
                sp.dma_start(raw[:, slot], src).then_inc(raw_in[slot], 16)

            def load_square(stage, w, columns):
                v = w.rearrange("(k p) n -> p k n", p=P)
                for c, n in enumerate(columns):
                    for half in range(2):
                        load(UNITS[stage] + 2 * c + half, half, v[:, KU * half:KU * (half + 1), n:n + BANK])

            def load_mlp(l):
                w1 = mlp_w1[l].rearrange("(k p) n -> p k n", p=P)
                w2 = mlp_w2[l].rearrange("(k p) n -> p k n", p=P)
                u0 = UNITS[f"mlp{l}"]

                def chunk(i, which, j):
                    for half in range(2):
                        if which == 1:
                            load(i + half, half, w1[:, KU * half:KU * (half + 1), bass.ds(BANK * j, BANK)])
                        else:
                            load(i + half, half, w2[:, bass.ds(KU * j, KU), BANK * half:BANK * (half + 1)])

                for n, (which, j) in enumerate([(1, 0), (1, 1), (2, 0)]):
                    chunk(u0 + 2 * n, which, j)
                with sp.Fori(0, (NJ - 2) // 2) as it:
                    for n, (which, j, _) in enumerate(in_order(it)):
                        chunk(8 * it + (u0 + 6 + 2 * n), which, j)
                chunk(u0 + 4 * NJ - 2, 2, NJ - 1)

            sp.dma_start(mem_v[:], mem[0].rearrange("(m p) d -> p m d", p=P)).then_inc(mem_in, 16)
            load_square("kv", mem_w_kv, range(0, BANK, BANK))
            sp.dma_start(h[:], x[0].rearrange("(m p) d -> p m d", p=P)).then_inc(x_in, 16)
            v = mem_w_kv.rearrange("(k p) n -> p k n", p=P)
            for c in range(1, 4):
                for half in range(2):
                    load(2 * c + half, half, v[:, KU * half:KU * (half + 1), c * BANK:(c + 1) * BANK])
            load_square("in0", ab_w_in[0], [n for _, n, _ in IN0])
            load_square("out0", ab_w_out[0], [0, BANK])
            load_square("xq0", xa_w_q[0], [0, BANK])
            load_square("xo0", xa_w_o[0], [0, BANK])
            load_mlp(0)
            load_square("in1", c_w_in[0], range(0, 4 * D, BANK))
            load_square("out1", c_w_out[0], [0, BANK])
            load_square("xq1", xa_w_q[1], [0, BANK])
            load_square("xo1", xa_w_o[1], [0, BANK])
            load_mlp(1)
            sp.wait_ge(sum_done, 4 * SUM_BEFORE["final"])
            sp.dma_start(final_g[:], final_norm_g.rearrange("(a d) -> a d", a=1).to_broadcast([P, D])).then_inc(gain_in, 16)
            for m in range(MT):
                sp.wait_ge(fin_ready, m + 1)
                sp.dma_start(out[0, m * P:(m + 1) * P, :], u[:, m]).then_inc(out_done, 16)
            sp.wait_ge(out_done, 16 * MT)

        @block.gpsimd
        def _(pool):
            step = [0]

            def then(ins):
                step[0] += 1
                ins.then_inc(pool_step, 1)
                pool.wait_ge(pool_step, step[0])

            pool.memset(ident[:], 0.0).then_inc(pool_step, 1)
            pool.memset(after[:], 0.0).then_inc(pool_step, 1)
            pool.memset(after_T[:], 0.0).then_inc(pool_step, 1)
            pool.memset(select[:], 0.0).then_inc(pool_step, 1)
            pool.memset(ones_row[:], 1.0).then_inc(pool_step, 1)
            pool.memset(zeros_row[:], 0.0).then_inc(pool_step, 1)
            step[0] = 6
            pool.wait_ge(pool_step, 6)
            then(pool.affine_select(out=ident[:], in_=ident[:], pattern=[[-1, P]], compare_op=ALU.not_equal,
                                    fill=1.0, base=0, channel_multiplier=1))
            then(pool.affine_select(out=after_T[:], in_=after_T[:], pattern=[[1, P]], compare_op=ALU.is_ge,
                                    fill=NEG, base=0, channel_multiplier=-1))
            then(pool.affine_select(out=after[:], in_=after[:], pattern=[[-1, P]], compare_op=ALU.is_ge,
                                    fill=NEG, base=0, channel_multiplier=1))
            pool.affine_select(out=select[:], in_=select[:], pattern=[[-1, HC], [0, P]], compare_op=ALU.not_equal,
                               fill=1.0, base=0, channel_multiplier=1).then_inc(consts, 1)
            for n, level in enumerate(LEVELS[:-1]):
                lv = pairs_f[:, n]
                then(pool.memset(lv, 0.0 if level == 0 else 1.0))
                if level == 0:
                    then(pool.affine_select(out=lv, in_=lv, pattern=[[-1, P]], compare_op=ALU.not_equal, fill=1.0,
                                            base=0, channel_multiplier=1))
                    continue
                nb = P // (2 * level)
                v = lv.rearrange("p (b two l) -> p b two l", two=2, l=level)
                then(pool.memset(v[:, :, 0, :], 0.0))
                second = v[:, :, 1, :]
                then(pool.affine_select(out=second, in_=second, pattern=[[-2 * level, nb], [0, level]],
                                        compare_op=ALU.is_ge, fill=0.0, base=0, channel_multiplier=1))
                then(pool.affine_select(out=second, in_=second, pattern=[[2 * level, nb], [0, level]],
                                        compare_op=ALU.is_ge, fill=0.0, base=level - 1, channel_multiplier=-1))
            pool.tensor_copy(pairs[:], pairs_f[:]).then_inc(consts, 1)
            pool.memset(pair_w[:], 0.0).then_inc(consts, 1)
            pool.memset(va[:, :, :, P:P + 1], 1.0).then_inc(consts, 1)

        @block.scalar
        def _(act):
            step = [0]

            def then(ins):
                step[0] += 1
                ins.then_inc(act_step, 1)
                act.wait_ge(act_step, step[0])

            def split(i, slot):
                act.wait_ge(raw_in[slot % RAW], (i - slot % RAW) * (16 // RAW) + 16)
                if not (isinstance(i, int) and i < RING):
                    act.wait_ge(unit_used, i - RING + 1)
                act.activation(flat(w_hi[:, slot]), flat(raw[:, slot % RAW]), ACT.Copy).then_inc(hi_ready, 1)

            def ahead(i):
                if i + RING < NU:
                    split(i + RING, i % RING)

            def root(name, w):
                act.wait_ge(root_in, ROOTS[name] + 1)
                then(act.activation(st[:, 1, 0:w], st[:, 0, 0:w], ACT.Ln))
                act.activation(st[:, 2, 0:w], st[:, 1, 0:w], ACT.Exp, scale=-0.5).then_inc(root_seed, 1)

            def norm(stage, src, junk):
                act.activation(junk[:, 0], src[:, 0], ACT.Square, accum_out=st[:, 4, 0:1]).then_inc(square_sum, 1)
                root(stage, MT)

            def turn(stage):
                g = GAIN[stage]
                for k in range(KD):
                    if k % 2 == 0:
                        wait_full(act, stage, 4 + k // 2)
                    act.activation(act_hi[:, k], bank[4 + k // 2][:, (k % 2) * T:(k % 2 + 1) * T], ACT.Copy,
                                   scale=1.0 if g is None else par[:, g + k:g + k + 1]).then_inc(acthi_ready, 1)

            def gemm(stage, n, evacuate):
                for c in range(n):
                    ahead(UNITS[stage] + 2 * c)
                    evacuate(c)
                    ahead(UNITS[stage] + 2 * c + 1)

            def load_rows(name, src, skip=0):
                act.dma_start(par_rows[PROW[name] + skip:PROW[name] + skip + src.shape[0], :], src).then_inc(par_in, 16)

            load_rows("norm_mix", norm_mix_g.rearrange("l (k p) -> (l k) p", p=P))
            load_rows("norm_xattn", norm_xattn_g.rearrange("l (k p) -> (l k) p", p=P))
            load_rows("norm_mlp", norm_mlp_g.rearrange("l (k p) -> (l k) p", p=P))
            load_rows("mem_norm", mem_norm_g.rearrange("(k p) -> k p", p=P))
            load_rows("mix_out", mlstm_norm_g[0].rearrange("(k p) -> k p", p=P))
            load_rows("mix_out", hgrn_norm_g[0].rearrange("(k p) -> k p", p=P), HM)
            load_rows("conv", ab_conv_w[0].rearrange("j (k p) -> (j k) p", p=P))
            load_rows("lb", hgrn_lb_logits.rearrange("l (k p) -> (l k) p", p=P))
            load_rows("qn", c_qnorm_g)
            load_rows("kn", c_knorm_g)
            act.dma_start(gate_w[:], ab_w_in[0].rearrange("(k p) n -> p k n", p=P)[:, :, GATE0:GATE0 + 8])\
               .then_inc(small_in, 16)
            act.dma_start(gate_w1[:], c_w_in[0].rearrange("(k p) n -> p k n", p=P)[:, :, GATE1:GATE1 + 8])\
               .then_inc(small_in, 16)
            act.dma_start(bias_i[:], ab_gate_b[0, 0:HM].rearrange("(p a) -> p a", a=1)).then_inc(small_in, 16)
            act.dma_start(bias_f[:], ab_gate_b[0, HM:2 * HM].rearrange("(p a) -> p a", a=1)).then_inc(small_in, 16)
            act.dma_start(bias_c[:], c_fgate_b[0].rearrange("(p a) -> p a", a=1)).then_inc(small_in, 16)

            act.wait_ge(mem_in, 16)
            norm("turn_mem", mem_v, u)
            split(0, 0)
            split(1, 1)
            act.wait_ge(lb_in, 1)
            act.activation(lb[:, 3:5], lb[:, 3:5], ACT.Exp).then_inc(lb_exp, 1)
            turn("turn_mem")
            split(2, 2)
            split(3, 3)

            def kv(c):
                for i in range(2):
                    b = 2 * (c % 2) + i
                    wait_chunk(act, "kv", c, i)
                    if c < 2:
                        dst = flat(mem_kT[:, 4 * c + 2 * i:4 * c + 2 * i + 2])
                    else:
                        dst = mem_v[:, i, (c - 2) * BANK:(c - 1) * BANK]
                    act.activation(dst, bank[b][:], ACT.Copy).then_inc(kv_done, 1)
            gemm("kv", 4, kv)

            act.wait_ge(x_in, 16)
            act.wait_ge(consts, 4)
            norm("turn_mix0", h, u)
            turn("turn_mix0")

            def log_gate(stage, r, n, bias, zf):
                wait_full(act, stage, 4)
                act.wait_ge(small_in, 16 * 5)
                then(act.activation(r[0:n, 0], zf, ACT.Abs, bias=bias[:]))
                then(act.activation(r[0:n, 0], r[0:n, 0], ACT.Exp, scale=-1.0))
                act.activation(r[0:n, 0], r[0:n, 0], ACT.Ln, bias=1.0).then_inc(log_out, 1)

            log_gate("gate0", rows, HM, bias_f, bank[4][0:HM, T:2 * T])

            def in0(c):
                name = IN0[c][0]
                for i in range(2):
                    b = 2 * (c % 2) + i
                    wait_chunk(act, "in0", c, i)
                    if name == "va":
                        act.activation(va[:, i, :, 0:P], heads(bank[b][:]), ACT.Copy).then_inc(in_done[b], 1)
                    elif name in CONV0:
                        for k in range(CONV0[name] + 2 * i, CONV0[name] + 2 * i + 2):
                            w = PROW["conv"] + 3 * KD + k
                            act.activation(qkT[:, k], bank[b][:, (k % 2) * T:(k % 2 + 1) * T], ACT.Copy,
                                           scale=par[:, w:w + 1]).then_inc(tap_ready, 1)
                    else:
                        act.activation(scratch(c, i), bank[b][:], ACT.Exp, scale=-1.0).then_inc(exp_ready, 1)
                for i in range(2):
                    if name in CONV0:
                        k = CONV0[name] + 2 * i
                        act.wait_ge(conv_done, k // 2 + 1)
                        act.activation(scratch(c, i), flat(qkT[:, k:k + 2]), ACT.Exp, scale=-1.0)\
                           .then_inc(exp_ready, 1)
                    if name == "fb":
                        act.wait_ge(forget_ready, i + 1)
                        act.activation(dec[:, 1, 2 * i:2 * i + 2], dec[:, 0, 2 * i:2 * i + 2], ACT.Ln)\
                           .then_inc(log_forget, 1)
            gemm("in0", 8, in0)

            wait_full(act, "mlstm", 5)
            act.activation(cols[:, 1], bank[5][:, MT * HM:2 * MT * HM], ACT.Exp)
            act.activation(cols[:, 0], bank[5][:, 0:MT * HM], ACT.Copy).then_inc(cols_ready, 1)
            act.wait_ge(cols_ready, 1)
            for hd in range(HM):
                wait_full(act, "mlstm", 4 + hd % 2, hd // 2 + hd % 2)
                if hd >= 2:
                    act.wait_ge(weight_ready, hd - 1)
                act.activation(decay[:, hd % 2, 0:T], bank[4 + hd % 2][:, 0:T], ACT.Exp, bias=cols[:, 0, hd:hd + 1])
                act.activation(decay[:, hd % 2, T:3 * P], bank[4 + hd % 2][:, T:3 * P], ACT.Exp,
                               bias=cols[:, 0, HM + hd:HM + hd + 1]).then_inc(decay_ready, 1)
            for m in range(MT):
                act.wait_ge(y_ready, m + 1)
                act.activation(flat(qkT[:, 2 * m:2 * m + 2]), u[:, m, 0:BANK], ACT.Square).then_inc(y_squared, 1)
            root("mlstm", MT * HM)

            for n in range(1, len(LEVELS)):
                act.wait_ge(dist_ready, n)
                act.activation(flat(dec[:, n % 2]), flat(dec[:, n % 2]), ACT.Exp).then_inc(dec_ready, 1)
            wait_full(act, "hgrn", 4, 4)
            act.activation(flat(pair_x[:]), bank[4][:], ACT.Copy).then_inc(pairx_ready, 1)
            for m in range(MT):
                wait_full(act, "hgrn", m)
                act.activation(flat(qkT[:, 2 * m:2 * m + 2]), bank[m][:], ACT.Square).then_inc(y_squared, 1)
            root("hgrn", MT * HM)
            turn("turn_y0")
            gemm("out0", 2, lambda c: None)

            def cross(l):
                act.wait_ge(sum_done, 4 * SUM_BEFORE[f"turn_x{l}"])
                norm(f"turn_x{l}", h, u)
                turn(f"turn_x{l}")

                def xq(c):
                    for i in range(2):
                        b = 2 * c + i
                        wait_chunk(act, f"xq{l}", c, i)
                        act.activation(flat(xqT[:, 2 * b:2 * b + 2]), bank[b][:], ACT.Copy, scale=XD ** -0.5)\
                           .then_inc(xq_done, 1)
                gemm(f"xq{l}", 2, xq)
                stage = f"xattn{l}"
                for i in range(HX + 2):
                    if i < HX:
                        act.wait_ge(xmax, HX * l + i + 1)
                        if i >= 2:
                            wait_full(act, stage, 2 + i % 2, i // 2 - 1)
                        for m in range(MT):
                            c = 2 * (i % 2) + m
                            ins = act.activation(px[:, i % 2, m], bank[i % 2][:, m * T:(m + 1) * T], ACT.Exp,
                                                 bias=xs[:, 1, c:c + 1], accum_out=xs[:, 2, c:c + 1])
                        ins.then_inc(xexp, 1)
                    if 1 <= i <= HX:
                        hd = i - 1
                        wait_full(act, stage, 2 + hd % 2, hd // 2)
                        if hd >= 2:
                            wait_full(act, stage, 4 + hd % 2, hd // 2 - 1)
                        act.activation(flat(pxT[:, hd % 2]), bank[2 + hd % 2][:], ACT.Copy).then_inc(xturned, 1)
                    if i >= 2:
                        hd = i - 2
                        wait_full(act, stage, 4 + hd % 2, hd // 2)
                        act.activation(flat(act_hi[:, 2 * hd:2 * hd + 2]), bank[4 + hd % 2][:], ACT.Copy)\
                           .then_inc(acthi_ready, 2)
                gemm(f"xo{l}", 2, lambda c: None)

            def mlp(l):
                act.wait_ge(sum_done, 4 * SUM_BEFORE[f"turn_m{l}"])
                norm(f"turn_m{l}", h, u)
                turn(f"turn_m{l}")
                stage = f"mlp{l}"

                def hidden(j, buf, unit):
                    for i in range(2):
                        if i == 0:
                            wait_full(act, stage, 4, j)
                        else:
                            act.wait_ge(unit_used, unit + 2)
                        act.activation(relu[:, i], bank[4 + i][:], ACT.Relu).then_inc(relu_ready, 1)
                    for i in range(2):
                        act.wait_ge(hid_ready, 2 * j + (2 * NJ * l + i + 1))
                        act.activation(flat(hid_hi[:, buf, 2 * i:2 * i + 2]), hid[:, i], ACT.Copy)\
                           .then_inc(hidhi_ready, 1)
                mlp_walk(act, l, split, ahead, hidden)

            cross(0)
            mlp(0)

            act.wait_ge(sum_done, 4 * SUM_BEFORE["turn_mix1"])
            norm("turn_mix1", h, u)
            turn("turn_mix1")
            log_gate("gate1", rows1, HC, bias_c, bank[4][0:HC, 0:T])

            def in1(c):
                which, n = c // 2, c % 2
                for m in range(2):
                    b = 2 * (c % 2) + m
                    wait_chunk(act, "in1", c, m)
                    part = slice(n * BANK, (n + 1) * BANK)
                    if which < 2:
                        act.activation((qc, kc)[which][:, m, part], bank[b][:], ACT.Copy)
                        if which == 1:
                            act.wait_ge(squares_used, 2 * n + m + 1)
                        act.activation(u[:, m, part], bank[b][:], ACT.Square).then_inc(in_done[b], 1)
                    elif which == 2:
                        act.activation(vc[:, m, part], bank[b][:], ACT.Copy).then_inc(in_done[b], 1)
                    else:
                        act.activation(gc[:, m, part], bank[b][:], ACT.Exp, scale=-1.0).then_inc(in_done[b], 1)
                if c == 1:
                    root("q", MT * HC)
                if c == 3:
                    root("k", MT * HC)
                    for k in range(HC):
                        if k % 2 == 0:
                            wait_full(act, "turn_q", 4 + k // 2)
                        act.activation(qcT[:, k], bank[4 + k // 2][:, (k % 2) * T:(k % 2 + 1) * T], ACT.Copy,
                                       scale=q_gain[:]).then_inc(qT_ready, 1)
            gemm("in1", 8, in1)

            for i in range(HC + 1):
                if i < HC:
                    act.wait_ge(cmax, i + 1)
                    if i >= 2:
                        wait_full(act, "fox", 2 + i % 2, i // 2 - 1)
                    for m in range(MT):
                        part = slice(m * P, (1 + 2 * m) * P)
                        ins = act.activation(pc[:, i % 2, part], bank[i % 2][:, part], ACT.Exp,
                                             bias=csum[:, 1, 2 * i + m:2 * i + m + 1],
                                             accum_out=csum[:, 2, 2 * i + m:2 * i + m + 1])
                    ins.then_inc(cexp, 1)
                if i >= 1:
                    hd = i - 1
                    wait_full(act, "fox", 2 + hd % 2, hd // 2)
                    if hd >= 2:
                        wait_full(act, "fox", 4 + hd % 2, hd // 2 - 1)
                    act.activation(pcT[:, hd % 2], bank[2 + hd % 2][:, 0:3 * P], ACT.Copy).then_inc(cturned, 1)
            turn("turn_y1")
            gemm("out1", 2, lambda c: None)
            cross(1)
            mlp(1)
            act.wait_ge(sum_done, 4 * SUM_BEFORE["final"])
            norm("final", h, squares)

        @block.vector
        def _(dve):
            step = [0]

            def then(ins):
                step[0] += 1
                ins.then_inc(dve_step, 1)
                dve.wait_ge(dve_step, step[0])

            def split(i, slot):
                dve.wait_ge(hi_ready, i + 1)
                dve.tensor_tensor(flat(w_lo[:, slot]), flat(raw[:, slot % RAW]), f(flat(w_hi[:, slot])),
                                  ALU.subtract).then_inc(lo_ready, 1)

            def ahead(i):
                if i + RING < NU:
                    split(i + RING, i % RING)

            def root(name, w, sums, n):
                dve.tensor_scalar(st[:, 0, 0:w], sums, 1.0 / n, EPS, ALU.mult, ALU.add).then_inc(root_in, 1)
                dve.wait_ge(root_seed, ROOTS[name] + 1)
                then(dve.tensor_tensor(st[:, 3, 0:w], st[:, 0, 0:w], st[:, 2, 0:w], ALU.mult))
                then(dve.tensor_tensor(st[:, 3, 0:w], st[:, 3, 0:w], st[:, 2, 0:w], ALU.mult))
                then(dve.tensor_scalar(st[:, 3, 0:w], st[:, 3, 0:w], -0.5, 1.5, ALU.mult, ALU.add))
                then(dve.tensor_tensor(st[:, 6, 0:w], st[:, 3, 0:w], st[:, 2, 0:w], ALU.mult))

            def norm_sums(stage, src, junk):
                then(dve.tensor_tensor_reduce(out=junk[:, 1], in0=src[:, 1], in1=src[:, 1], scale=1.0, scalar=0.0,
                                              op0=ALU.mult, op1=ALU.add, accum_out=st[:, 4, 1:2]))
                dve.wait_ge(square_sum, NORMS[stage] + 1)
                root(stage, MT, st[:, 4, 0:MT], D)

            def norm(stage, src):
                norm_sums(stage, src, u)
                for m in range(MT):
                    dve.tensor_scalar(u[:, m], src[:, m], st[:, 6, m:m + 1], None, ALU.mult).then_inc(source_ready, 1)

            def turn(stage):
                g = GAIN[stage]
                for k in range(KD):
                    if k % 2 == 0:
                        dve.wait_ge(acthi_ready, KD * VERSION[stage] + k + 2)
                    z = bank[4 + k // 2][:, (k % 2) * T:(k % 2 + 1) * T]
                    if g is None:
                        ins = dve.tensor_tensor(act_lo[:, k], z, f(act_hi[:, k]), ALU.subtract)
                    else:
                        ins = dve.scalar_tensor_tensor(out=act_lo[:, k], in0=z, scalar=par[:, g + k:g + k + 1],
                                                       in1=f(act_hi[:, k]), op0=ALU.mult, op1=ALU.subtract)
                    ins.then_inc(actlo_ready, 1)

            def gemm(stage, n, evacuate):
                for c in range(n):
                    ahead(UNITS[stage] + 2 * c)
                    evacuate(c)
                    ahead(UNITS[stage] + 2 * c + 1)

            def add_to_h(stage, c, last_unit=None):
                last_unit = UNITS[stage] + 2 * c + 1 if last_unit is None else last_unit
                for m in range(MT):
                    if m == 0:
                        wait_full(dve, stage, 2 * c)
                    else:
                        dve.wait_ge(unit_used, last_unit + 1)
                    part = h[:, m, c * BANK:(c + 1) * BANK]
                    dve.tensor_tensor(part, bank[2 * c + m][:], part, ALU.add).then_inc(sum_done, 1)

            wait_full(dve, "params", 7)
            then(dve.tensor_copy(par[:], bank[7][:, 0:NPAR]))
            dve.tensor_scalar(q_gain[:], par[:, PROW["qn"]:PROW["qn"] + 1], P ** -0.5, None, ALU.mult)\
               .then_inc(par_ready, 1)
            l0, l1 = par[:, PROW["lb"]:PROW["lb"] + HM], par[:, PROW["lb"] + HM:PROW["lb"] + 2 * HM]
            then(dve.tensor_tensor(lb[:, 2], l0, l1, ALU.max))
            dve.tensor_tensor(lb[:, 3], l0, lb[:, 2], ALU.subtract)
            dve.tensor_tensor(lb[:, 4], l1, lb[:, 2], ALU.subtract).then_inc(lb_in, 1)
            dve.wait_ge(mem_in, 16)
            norm("turn_mem", mem_v)
            split(0, 0)
            split(1, 1)
            turn("turn_mem")
            split(2, 2)
            split(3, 3)
            dve.wait_ge(lb_exp, 1)
            then(dve.tensor_tensor(lb[:, 2], lb[:, 3], lb[:, 4], ALU.add))
            then(dve.reciprocal(lb[:, 5], lb[:, 2]))
            dve.tensor_tensor(lb[:, 0], lb[:, 3], lb[:, 5], ALU.mult)
            then(dve.tensor_tensor(lb[:, 1], lb[:, 4], lb[:, 5], ALU.mult))
            gemm("kv", 4, lambda c: None)

            dve.wait_ge(x_in, 16)
            dve.wait_ge(consts, 4)
            norm("turn_mix0", h)
            turn("turn_mix0")

            def log_sigmoid_sum(r, n, bias, zf, count):
                dve.wait_ge(log_out, count)
                then(dve.tensor_scalar(r[0:n, 1], zf, bias[:], 0.0, ALU.add, ALU.min))
                then(dve.tensor_tensor(r[0:n, 1], r[0:n, 1], r[0:n, 0], ALU.subtract))
                then(dve.tensor_tensor_scan(r[0:n, 3], r[0:n, 1], r[0:n, 1], 0.0, ALU.add, ALU.bypass))

            wait_full(dve, "gate0", 4)
            dve.wait_ge(small_in, 16 * 5)
            dve.wait_ge(log_out, 1)
            then(dve.tensor_scalar(rows[0:HM, 2], bank[4][0:HM, 0:T], bias_i[:], None, ALU.add))
            log_sigmoid_sum(rows, HM, bias_f, bank[4][0:HM, T:2 * T], 1)
            then(dve.tensor_tensor(rows[0:HM, 4], rows[0:HM, 2], rows[0:HM, 3], ALU.subtract))
            then(dve.tensor_tensor_scan(rows[0:HM, 5], rows[0:HM, 4], rows[0:HM, 4], 0.0, ALU.max, ALU.bypass))
            dve.tensor_scalar(rows[0:HM, 6], rows[0:HM, 5], -1.0, None, ALU.mult)
            dve.scalar_tensor_tensor(out=rows[0:HM, 7], in0=rows[0:HM, 3], scalar=-1.0, in1=rows[0:HM, 5],
                                     op0=ALU.mult, op1=ALU.subtract).then_inc(rows_ready, 1)

            def in0(c):
                name = IN0[c][0]
                if name == "va":
                    return
                for i in range(2):
                    b = 2 * (c % 2) + i
                    if name in CONV0:
                        wait_chunk(dve, "in0", c, i)
                        for lag in range(1, 4):
                            for k in range(CONV0[name] + 2 * i, CONV0[name] + 2 * i + 2):
                                if lag == 1 and k % 2 == 0:
                                    dve.wait_ge(tap_ready, k + 2)
                                w = PROW["conv"] + (3 - lag) * KD + k
                                z = bank[b][:, (k % 2) * T:(k % 2 + 1) * T - lag]
                                ins = dve.scalar_tensor_tensor(out=qkT[:, k, lag:T], in0=z, scalar=par[:, w:w + 1],
                                                               in1=qkT[:, k, lag:T], op0=ALU.mult, op1=ALU.add)
                                if k % 2 and lag < 3:
                                    then(ins)
                        ins.then_inc(conv_done, 1)
                for i in range(2):
                    b = 2 * (c % 2) + i
                    e, z = scratch(c, i), bank[b][:]
                    dve.wait_ge(exp_ready, 2 * EXP_BEFORE[name] + i + 1)
                    if name == "fb":
                        both = slice(2 * i, 2 * i + 2)
                        r = flat(dec[:, 0, both])
                        then(dve.tensor_scalar(r, e, 1e30, 1.0, ALU.min, ALU.add))
                        then(dve.reciprocal(r, r))
                        then(dve.scalar_tensor_tensor(out=flat(kb[:, both]), in0=e, scalar=1e30, in1=r,
                                                      op0=ALU.min, op1=ALU.mult))
                        for hd in range(2 * i, 2 * i + 2):
                            ins = dve.tensor_scalar(dec[:, 0, hd], dec[:, 0, hd], lb[:, 1, hd:hd + 1],
                                                    lb[:, 0, hd:hd + 1], ALU.mult, ALU.add)
                        ins.then_inc(forget_ready, 1)
                        for hd in range(2 * i, 2 * i + 2):
                            ins = dve.tensor_scalar(kb[:, hd], kb[:, hd], lb[:, 1, hd:hd + 1], None, ALU.mult)
                        ins.then_inc(in_done[b], 1)
                        continue
                    then(dve.tensor_scalar(e, e, 1.0, None, ALU.add))
                    if name == "oa":
                        dve.reciprocal(oa[:, i], e).then_inc(in_done[b], 1)
                        continue
                    then(dve.reciprocal(e, e))
                    if name in CONV0:
                        y = flat(qkT[:, CONV0[name] + 2 * i:CONV0[name] + 2 * i + 2])
                        ins = dve.scalar_tensor_tensor(out=y, in0=y, scalar=1.0 if name == "qa" else P ** -0.5,
                                                       in1=e, op0=ALU.mult, op1=ALU.mult)
                    else:
                        dst = {"qb": flat(qb[:, 2 * i:2 * i + 2]), "ib": vb[:, i], "gb": gb[:, i]}[name]
                        ins = dve.tensor_tensor(dst, z, e, ALU.mult)
                    ins.then_inc(in_done[b], 1)
                if name == "fb":
                    for hd in range(HM):
                        if hd % 2 == 0:
                            dve.wait_ge(log_forget, hd // 2 + 1)
                        ins = dve.tensor_tensor_scan(cum[:, hd], dec[:, 1, hd], dec[:, 1, hd], 0.0,
                                                     ALU.add, ALU.bypass)
                    then(ins)
            gemm("in0", 8, in0)

            def finish_pair(hp):
                for m in range(MT):
                    b = 2 * hp + m
                    wait_full(dve, "mlstm", b)
                    v = bank[b][:, 0:2 * (P + 1)].rearrange("p (h d) -> p h d", d=P + 1)
                    den = v[:, :, P:P + 1].rearrange("p h d -> p (h d)")
                    floor = cols[:, 1, HM * m + 2 * hp:HM * m + 2 * hp + 2]
                    c = slice(4 * m + 2 * hp, 4 * m + 2 * hp + 2)
                    then(dve.scalar_tensor_tensor(out=st[:, 7, c], in0=den, scalar=-1.0, in1=floor,
                                                  op0=ALU.mult, op1=ALU.max))
                    then(dve.tensor_tensor(st[:, 7, c], den, st[:, 7, c], ALU.max))
                    then(dve.reciprocal(st[:, 7, c], st[:, 7, c]))
                    for k in range(2):
                        hd = 2 * hp + k
                        part = slice(hd * P, (hd + 1) * P)
                        ins = dve.scalar_tensor_tensor(out=u[:, m, part], in0=v[:, k, 0:P],
                                                       scalar=st[:, 7, 4 * m + hd:4 * m + hd + 1],
                                                       in1=oa[:, m, part], op0=ALU.mult, op1=ALU.mult)
                    if hp == 1:
                        ins.then_inc(y_ready, 1)

            dve.wait_ge(cols_ready, 1)
            dve.wait_ge(in_done[2], 4)
            dve.wait_ge(in_done[3], 4)
            for hd in range(HM):
                dve.wait_ge(decay_ready, hd + 1)
                wait_full(dve, "mlstm", 6 + hd % 2, hd // 2)
                dve.tensor_tensor(weight[:, hd % 2], bank[6 + hd % 2][:, 0:3 * P], decay[:, hd % 2], ALU.mult)\
                   .then_inc(weight_ready, 1)
                if hd == 2:
                    finish_pair(0)
            finish_pair(1)

            def head_sums(first):
                for m in range(MT):
                    dve.wait_ge(y_squared, first + m + 1)
                    then(dve.tensor_reduce(st[:, 5, HM * m:HM * (m + 1)], heads(flat(qkT[:, 2 * m:2 * m + 2])), AX.X,
                                           ALU.add))

            head_sums(0)
            root("mlstm", MT * HM, st[:, 5, 0:MT * HM], P)
            for m in range(MT):
                y = heads(u[:, m, 0:BANK])
                dve.tensor_tensor(y, y, spread(st[:, 6, HM * m:HM * (m + 1)], P), ALU.mult)

            def distance(n):
                level = LEVELS[n]
                if n >= 3:
                    dve.wait_ge(scaled_ready, n - 2)
                v, mid = last_of_half(level)
                d = halves(dec[:, n % 2], level)
                dve.tensor_tensor(d[:, :, 0, :], mid, v[:, :, 0, :], ALU.subtract)
                dve.tensor_tensor(d[:, :, 1, :], v[:, :, 1, :], mid, ALU.subtract).then_inc(dist_ready, 1)

            def scale(n):
                dve.wait_ge(dec_ready, n)
                if n <= 2:
                    dve.tensor_tensor(flat(qd[:, n % 2]), flat(qb[:]), flat(dec[:, n % 2]), ALU.mult)
                    dve.tensor_tensor(flat(kd[:, n % 2]), flat(kb[:]), flat(dec[:, n % 2]), ALU.mult)\
                       .then_inc(scaled_ready, 1)
                    return
                level = LEVELS[n]
                for to, of, which in ((qd, qb, 1), (kd, kb, 0)):
                    ins = dve.tensor_tensor(halves(to[:, n % 2], level)[:, :, which, :],
                                            halves(of[:], level)[:, :, which, :],
                                            halves(dec[:, n % 2], level)[:, :, which, :], ALU.mult)
                ins.then_inc(scaled_ready, 1)

            def choose(n):
                for tile in range(MT):
                    b = 4 + 2 * (n % 2) + tile
                    wait_full(dve, "hgrn", b, n // 2)
                    if n:
                        dve.wait_ge(selected, 2 * (n - 1) + tile + 1)
                    dve.copy_predicated(pair_w[:, tile], pairs[:, n].unsqueeze(1).to_broadcast([P, HM, P]),
                                        heads(bank[b][:])).then_inc(selected, 1)

            distance(1)
            for n in range(1, len(LEVELS)):
                if n + 1 < len(LEVELS):
                    distance(n + 1)
                scale(n)
                choose(n - 1)
            head_sums(2)
            root("hgrn", MT * HM, st[:, 5, 0:MT * HM], P)
            for m in range(MT):
                for hd in range(HM):
                    part = slice(hd * P, (hd + 1) * P)
                    ins = dve.scalar_tensor_tensor(out=u[:, m, BANK + hd * P:BANK + (hd + 1) * P],
                                                   in0=bank[m][:, part], scalar=st[:, 6, HM * m + hd:HM * m + hd + 1],
                                                   in1=gb[:, m, part], op0=ALU.mult, op1=ALU.mult)
                ins.then_inc(source_ready, 1)
            turn("turn_y0")
            gemm("out0", 2, lambda c: add_to_h("out0", c))

            def cross(l):
                dve.wait_ge(sum_done, 4 * SUM_BEFORE[f"turn_x{l}"])
                norm(f"turn_x{l}", h)
                turn(f"turn_x{l}")
                gemm(f"xq{l}", 2, lambda c: None)
                stage = f"xattn{l}"
                for i in range(HX + 2):
                    if i < HX:
                        c = slice(2 * (i % 2), 2 * (i % 2) + 2)
                        wait_full(dve, stage, i % 2, i // 2)
                        then(dve.tensor_reduce(xs[:, 0, c], bank[i % 2][:].rearrange("p (m t) -> p m t", m=MT), AX.X,
                                               ALU.max))
                        dve.tensor_scalar(xs[:, 1, c], xs[:, 0, c], -1.0, None, ALU.mult).then_inc(xmax, 1)
                    if 1 <= i <= HX:
                        hd = i - 1
                        c = slice(2 * (hd % 2), 2 * (hd % 2) + 2)
                        dve.wait_ge(xexp, HX * l + hd + 1)
                        then(dve.reciprocal(xs[:, 3, c], xs[:, 2, c]))
                        dve.tensor_tensor(px[:, hd % 2], px[:, hd % 2], spread(xs[:, 3, c], T), ALU.mult)\
                           .then_inc(xnorm, 1)
                    if i >= 2:
                        hd = i - 2
                        dve.wait_ge(acthi_ready, KD * VERSION[stage] + 2 * hd + 2)
                        both = slice(2 * hd, 2 * hd + 2)
                        dve.tensor_tensor(flat(act_lo[:, both]), bank[4 + hd % 2][:], f(flat(act_hi[:, both])),
                                          ALU.subtract).then_inc(actlo_ready, 2)
                gemm(f"xo{l}", 2, lambda c: add_to_h(f"xo{l}", c))

            def mlp(l):
                dve.wait_ge(sum_done, 4 * SUM_BEFORE[f"turn_m{l}"])
                norm(f"turn_m{l}", h)
                turn(f"turn_m{l}")

                def hidden(j, buf, unit):
                    for i in range(2):
                        if l or not isinstance(j, int) or j:
                            dve.wait_ge(hidlo_ready, 2 * j + (2 * NJ * l + i - 1))
                        dve.wait_ge(relu_ready, 2 * j + (2 * NJ * l + i + 1))
                        dve.scalar_tensor_tensor(out=hid[:, i], in0=bank[4 + i][:], scalar=0.0, in1=relu[:, i],
                                                 op0=ALU.max, op1=ALU.mult).then_inc(hid_ready, 1)
                    for i in range(2):
                        dve.wait_ge(hidhi_ready, 2 * j + (2 * NJ * l + i + 1))
                        dve.tensor_tensor(flat(hid_lo[:, buf, 2 * i:2 * i + 2]), hid[:, i],
                                          f(flat(hid_hi[:, buf, 2 * i:2 * i + 2])), ALU.subtract)\
                           .then_inc(hidlo_ready, 1)
                mlp_walk(dve, l, split, ahead, hidden)
                for c in range(2):
                    add_to_h(f"mlp{l}", c, UNITS[f"mlp{l}"] + 4 * NJ - 2 + c)

            cross(0)
            mlp(0)

            dve.wait_ge(sum_done, 4 * SUM_BEFORE["turn_mix1"])
            norm("turn_mix1", h)
            turn("turn_mix1")
            wait_full(dve, "gate1", 4)
            log_sigmoid_sum(rows1, HC, bias_c, bank[4][0:HC, 0:T], 2)
            dve.tensor_scalar(rows1[0:HC, 4], rows1[0:HC, 3], -1.0, None, ALU.mult).then_inc(rows_ready, 1)

            def in1(c):
                which, n = c // 2, c % 2
                for m in range(MT):
                    b = 2 * (c % 2) + m
                    part = slice(n * BANK, (n + 1) * BANK)
                    if which < 2:
                        dve.wait_ge(in_done[b], 4 + c // 2 + 1)
                        dve.tensor_reduce(st[:, 5, HC * m + HM * n:HC * m + HM * (n + 1)], heads(u[:, m, part]), AX.X,
                                          ALU.add).then_inc(squares_used, 1)
                    if which == 3:
                        dve.wait_ge(in_done[b], 4 + c // 2 + 1)
                        then(dve.tensor_scalar(gc[:, m, part], gc[:, m, part], 1.0, None, ALU.add))
                        ins = dve.reciprocal(gc[:, m, part], gc[:, m, part])
                        if m == 1:
                            then(ins)
                if which < 2 and n == 1:
                    dve.wait_ge(squares_used, 4 * (which + 1))
                    root("qk"[which], MT * HC, st[:, 5, 0:MT * HC], P)
                    z = (qc, kc)[which]
                    for m in range(MT):
                        zm = heads(z[:, m], HC)
                        dve.tensor_tensor(zm, zm, spread(st[:, 6, HC * m:HC * (m + 1)], P), ALU.mult)\
                           .then_inc(cnormed, 1)
                if c == 5:
                    for k in range(HC):
                        if k % 2 == 0:
                            wait_full(dve, "turn_k", 4 + k // 2)
                        dve.tensor_scalar(kcT[:, k], bank[4 + k // 2][:, (k % 2) * T:(k % 2 + 1) * T],
                                          par[:, PROW["kn"]:PROW["kn"] + 1], None, ALU.mult).then_inc(kT_ready, 1)
            gemm("in1", 8, in1)

            for i in range(HC + 2):
                if i < HC:
                    wait_full(dve, "fox", i % 2, i // 2)
                    for m in range(MT):
                        ins = dve.tensor_reduce(csum[:, 0, 2 * i + m:2 * i + m + 1],
                                                bank[i % 2][:, m * P:(1 + 2 * m) * P], AX.X, ALU.max)
                    then(ins)
                    dve.tensor_scalar(csum[:, 1, 2 * i:2 * i + 2], csum[:, 0, 2 * i:2 * i + 2], -1.0, None, ALU.mult)\
                       .then_inc(cmax, 1)
                if i >= 2:
                    hd = i - 2
                    dve.wait_ge(cexp, hd + 1)
                    then(dve.reciprocal(csum[:, 3, 2 * hd:2 * hd + 2], csum[:, 2, 2 * hd:2 * hd + 2]))
                    wait_full(dve, "fox", 4 + hd % 2, hd // 2)
                    part = slice(hd * P, (hd + 1) * P)
                    for m in range(MT):
                        ins = dve.scalar_tensor_tensor(out=u[:, m, part], in0=bank[4 + hd % 2][:, m * P:(m + 1) * P],
                                                       scalar=csum[:, 3, 2 * hd + m:2 * hd + m + 1],
                                                       in1=gc[:, m, part], op0=ALU.mult, op1=ALU.mult)
                    ins.then_inc(oc_done, 1)
            turn("turn_y1")
            gemm("out1", 2, lambda c: add_to_h("out1", c))
            cross(1)
            mlp(1)
            dve.wait_ge(sum_done, 4 * SUM_BEFORE["final"])
            norm_sums("final", h, squares)
            dve.wait_ge(gain_in, 16)
            for m in range(MT):
                dve.scalar_tensor_tensor(out=u[:, m], in0=h[:, m], scalar=st[:, 6, m:m + 1], in1=final_g[:],
                                         op0=ALU.mult, op1=ALU.mult).then_inc(fin_ready, 1)

        @block.tensor
        def _(pe):
            def three(o, a_hi, a_lo, b_hi, b_lo, start, stop, mark=False):
                pe.matmul(o, a_hi, b_hi, start=start, stop=False, skip_group_check=True)
                pe.matmul(o, a_hi, b_lo, start=False, stop=False, skip_group_check=True)
                return pe.matmul(o, a_lo, b_hi, start=False, stop=stop, skip_group_check=True)

            def unit(i, slot, k0, banks, transposed, first, last, x_hi, x_lo, opens=True):
                pe.wait_ge(lo_ready, i + 1)
                for g in range(2):
                    for k in range(KU):
                        begin, end = first and opens and k == 0, last and k == KU - 1
                        if transposed:
                            for q in range(2):
                                cut = slice((2 * g + q) * P, (2 * g + q + 1) * P)
                                ins = three(bank[banks + g][:, q * T:(q + 1) * T], w_hi[:, slot, k, cut],
                                            w_lo[:, slot, k, cut], x_hi[:, k0 + k], x_lo[:, k0 + k],
                                            begin and q == 0, end)
                        else:
                            cut = slice(g * P, (g + 1) * P)
                            ins = three(bank[banks + g][:], x_hi[:, k0 + k, cut], x_lo[:, k0 + k, cut],
                                        w_hi[:, slot, k], w_lo[:, slot, k], begin, end)
                    if g == 0 and last:
                        ins.then_inc(full[banks], 1)
                ins.then_inc(unit_used, 1)

            def turn(stage, src, version=None):
                for j in range(4):
                    for m in range(MT):
                        if j == 0 and stage in SOURCE:
                            pe.wait_ge(source_ready, MT * SOURCE[stage] + m + 1)
                        if j == 0 and version is not None:
                            pe.wait_ge(cnormed, MT * version + m + 1)
                        for k in (2 * j, 2 * j + 1):
                            ins = pe.transpose(bank[4 + j][:, (k % 2) * T + m * P:(k % 2) * T + (m + 1) * P],
                                               src[:, m, k * P:(k + 1) * P], ident[:])
                    ins.then_inc(full[4 + j], 1)

            def chunk(stage, c, transposed, version, done=None):
                for half in range(2):
                    i = UNITS[stage] + 2 * c + half
                    pe.wait_ge(actlo_ready, KD * version + KU * (half + 1))
                    if half == 0 and done is not None:
                        done(c)
                    unit(i, i % RING, KU * half, 2 * (c % 2), transposed, half == 0, half == 1, act_hi, act_lo)

            pe.wait_ge(consts, 1)
            pe.wait_ge(par_in, 16 * 10)
            pe.transpose(bank[7][:, 0:NPAR], par_rows[:], ident[0:NPAR, 0:NPAR]).then_inc(full[7], 1)
            pe.wait_ge(par_ready, 1)
            turn("turn_mem", u)

            def kv_free(c):
                if c >= 2:
                    pe.wait_ge(kv_done, 2 * (c - 1))
            for c in range(4):
                chunk("kv", c, c < 2, VERSION["turn_mem"], kv_free)

            turn("turn_mix0", u)
            pe.wait_ge(small_in, 16 * 5)
            v = VERSION["turn_mix0"]
            pe.wait_ge(actlo_ready, KD * (v + 1))

            def gate(o, w, n):
                for part in (act_hi, act_lo):
                    for k in range(KD):
                        ins = pe.matmul(o, w[:, k, n], f(part[:, k]), start=(k == 0 and part is act_hi),
                                        stop=(k == KD - 1 and part is act_lo))
                return ins

            gate(bank[4][0:HM, 0:T], gate_w, slice(0, HM))
            gate(bank[4][0:HM, T:2 * T], gate_w, slice(HM, 2 * HM)).then_inc(full[4], 1)

            def in0_free(c):
                for i in range(2):
                    if c >= 2:
                        pe.wait_ge(in_done[2 * (c % 2) + i], c // 2)
                    else:
                        pe.wait_ge(kv_done, 8)
            for c, (name, _, transposed) in enumerate(IN0):
                chunk("in0", c, transposed, v, in0_free)

            pe.wait_ge(rows_ready, 1)
            for q, r in enumerate((4, 7)):
                for m in range(MT):
                    at = (MT * q + m) * HM
                    ins = pe.transpose(bank[5][:, at:at + HM], rows[0:HM, r, m * P:(m + 1) * P], ident[0:HM, 0:HM])
            ins.then_inc(full[5], 1)
            for b in range(4):
                pe.wait_ge(in_done[b], 4)

            def mlstm_values(hd):
                pe.wait_ge(weight_ready, hd + 1)
                for m in range(MT):
                    o = bank[2 * (hd // 2) + m][:, (hd % 2) * (P + 1):(hd % 2 + 1) * (P + 1)]
                    for s in range(m + 1):
                        ins = pe.matmul(o, weight[:, hd % 2, (m + s) * P:(m + s + 1) * P], va[:, s, hd],
                                        start=(s == 0), stop=(s == m))
                    if hd % 2:
                        ins.then_inc(full[2 * (hd // 2) + m], 1)

            pe.wait_ge(cols_ready, 1)
            for hd in range(HM):
                if hd >= 2:
                    pe.wait_ge(weight_ready, hd - 1)
                b = bank[4 + hd % 2]
                for n, (to, t0, t1) in enumerate([(0, 0, T), (T, P, T)]):
                    pe.matmul(b[:, to:to + t1 - t0], select[0:HM, hd], rows[0:HM, 6, t0:t1], start=(n == 0),
                              stop=False, skip_group_check=True)
                    ins = pe.matmul(b[:, to:to + P], ident[:], after_T[:], start=False, stop=True,
                                    skip_group_check=True)
                ins.then_inc(full[4 + hd % 2], 1)
                b = bank[6 + hd % 2]
                pe.matmul(b[:, 0:T], qkT[:, HM + hd, 0:P], qkT[:, hd], start=True, stop=True)
                pe.matmul(b[:, T:3 * P], qkT[:, HM + hd, P:T], qkT[:, hd, P:T], start=True, stop=True)\
                  .then_inc(full[6 + hd % 2], 1)
                if hd:
                    mlstm_values(hd - 1)
            mlstm_values(HM - 1)

            for n, level in enumerate(LEVELS):
                if n:
                    pe.wait_ge(scaled_ready, n)
                if n >= 2:
                    pe.wait_ge(selected, MT * (n - 1))
                if n == 0:
                    pe.wait_ge(y_ready, 2)
                kk, qq = (kb[:], qb[:]) if n == 0 else (kd[:, n % 2], qd[:, n % 2])
                for tile in range(1 if level == 128 else MT):
                    b = 4 + 2 * (n % 2) + tile
                    to = 1 if level == 128 else tile
                    for hd in range(HM):
                        ins = pe.matmul(bank[b][:, hd * P:(hd + 1) * P], kk[:, hd, tile * P:(tile + 1) * P],
                                        qq[:, hd, to * P:(to + 1) * P], start=True, stop=True)
                    ins.then_inc(full[b], 1)
            pe.wait_ge(selected, MT * (len(LEVELS) - 1))
            for m in range(MT):
                if m:
                    pe.wait_ge(pairx_ready, 1)
                for hd in range(HM):
                    o, part = bank[m][:, hd * P:(hd + 1) * P], slice(hd * P, (hd + 1) * P)
                    if m:
                        pe.matmul(o, pair_x[:, hd], vb[:, 0, part], start=True, stop=False)
                    ins = pe.matmul(o, pair_w[:, m, hd], vb[:, m, part], start=(m == 0), stop=True)
                ins.then_inc(full[m], 1)
            turn("turn_y0", u)
            for c in range(2):
                chunk("out0", c, False, VERSION["turn_y0"])

            def cross(l):
                turn(f"turn_x{l}", u)
                for c in range(2):
                    chunk(f"xq{l}", c, True, VERSION[f"turn_x{l}"])
                stage = f"xattn{l}"
                for i in range(HX + 2):
                    if i < HX:
                        if i < 2:
                            pe.wait_ge(xq_done, 4 * (l + 1))
                        else:
                            pe.wait_ge(xexp, HX * l + i - 1)
                        for m in range(MT):
                            for k in range(2):
                                ins = pe.matmul(bank[i % 2][:, m * T:(m + 1) * T],
                                                xqT[:, 2 * i + k, m * P:(m + 1) * P], mem_kT[:, 2 * i + k],
                                                start=(k == 0), stop=(k == 1))
                        ins.then_inc(full[i % 2], 1)
                    if 1 <= i <= HX:
                        hd = i - 1
                        pe.wait_ge(xnorm, HX * l + hd + 1)
                        if hd >= 2:
                            pe.wait_ge(xturned, HX * l + hd - 1)
                        for m in range(MT):
                            for j in range(MT):
                                ins = pe.transpose(bank[2 + hd % 2][:, j * T + m * P:j * T + (m + 1) * P],
                                                   px[:, hd % 2, m, j * P:(j + 1) * P], ident[:])
                        ins.then_inc(full[2 + hd % 2], 1)
                    if i >= 2:
                        hd = i - 2
                        pe.wait_ge(xturned, HX * l + hd + 1)
                        if hd >= 2:
                            pe.wait_ge(actlo_ready, KD * VERSION[stage] + 2 * (hd - 1))
                        for k in range(2):
                            at = XD * hd + P * k
                            for j in range(MT):
                                ins = pe.matmul(bank[4 + hd % 2][:, k * T:(k + 1) * T], mem_v[:, j, at:at + P],
                                                pxT[:, hd % 2, j], start=(j == 0), stop=(j == MT - 1))
                        ins.then_inc(full[4 + hd % 2], 1)
                for c in range(2):
                    chunk(f"xo{l}", c, False, VERSION[stage])

            def mlp(l):
                stage = f"mlp{l}"
                turn(f"turn_m{l}", u)
                pe.wait_ge(actlo_ready, KD * (VERSION[f"turn_m{l}"] + 1))

                def w1(i, slot, j):
                    if not isinstance(j, int) or j:
                        pe.wait_ge(hid_ready, 2 * j + 2 * NJ * l)
                    for half in range(2):
                        unit(i + half, (slot + half) % RING, KU * half, 4, True, half == 0, half == 1, act_hi, act_lo)

                def w2(i, slot, j, buf, first, last):
                    pe.wait_ge(hidlo_ready, 2 * j + (2 * NJ * l + 2))
                    for n in range(2):
                        unit(i + n, (slot + n) % RING, 0, 2 * n, False, first, last, hid_hi[:, buf], hid_lo[:, buf])

                u0 = UNITS[stage]
                w1(u0, u0 % RING, 0)
                w1(u0 + 2, (u0 + 2) % RING, 1)
                w2(u0 + 4, (u0 + 4) % RING, 0, 0, True, False)
                with pe.Fori(0, (NJ - 2) // 2) as it:
                    for n, (which, j, buf) in enumerate(in_order(it)):
                        i, slot = 8 * it + (u0 + 6 + 2 * n), (u0 + 6 + 2 * n) % RING
                        if which == 1:
                            w1(i, slot, j)
                        else:
                            w2(i, slot, j, buf, False, False)
                w2(u0 + 4 * NJ - 2, (u0 + 4 * NJ - 2) % RING, NJ - 1, (NJ - 1) % 2, False, True)

            cross(0)
            mlp(0)

            turn("turn_mix1", u)
            v = VERSION["turn_mix1"]
            pe.wait_ge(actlo_ready, KD * (v + 1))
            gate(bank[4][0:HC, 0:T], gate_w1, slice(0, HC)).then_inc(full[4], 1)

            def in1_free(c):
                for i in range(2):
                    if c >= 2:
                        pe.wait_ge(in_done[2 * (c % 2) + i], 4 + c // 2)
            for c in range(8):
                chunk("in1", c, False, v, in1_free)
                if c == 3:
                    pe.wait_ge(rows_ready, 2)
                    turn("turn_q", qc, 0)
                if c == 5:
                    pe.wait_ge(qT_ready, HC)
                    turn("turn_k", kc, 1)

            pe.wait_ge(kT_ready, HC)
            for i in range(HC + 2):
                if i < HC:
                    if i < 2:
                        for b in (2 * (i % 2), 2 * (i % 2) + 1):
                            pe.wait_ge(in_done[b], 8)
                        pe.wait_ge(in_done[i], 8)
                    else:
                        pe.wait_ge(cexp, i - 1)
                    for m in range(MT):
                        w = (m + 1) * P
                        o = bank[i % 2][:, m * P:m * P + w]
                        pe.matmul(o, qcT[:, i, m * P:(m + 1) * P], kcT[:, i, 0:w], start=(m == 0), stop=False,
                                  skip_group_check=True)
                        pe.matmul(o, select[0:HC, i], rows1[0:HC, 4, 0:w], start=False, stop=False,
                                  skip_group_check=True)
                        ins = pe.matmul(bank[i % 2][:, 2 * m * P:(2 * m + 1) * P], ident[:], after[:], start=False,
                                        stop=True, skip_group_check=True)
                    ins.then_inc(full[i % 2], 1)
                if 1 <= i <= HC:
                    hd = i - 1
                    pe.wait_ge(cexp, hd + 1)
                    if hd >= 2:
                        pe.wait_ge(cturned, hd - 1)
                    else:
                        pe.wait_ge(in_done[2 + hd % 2], 8)
                    for n in range(3):
                        ins = pe.transpose(bank[2 + hd % 2][:, n * P:(n + 1) * P], pc[:, hd % 2, n * P:(n + 1) * P],
                                           ident[:])
                    ins.then_inc(full[2 + hd % 2], 1)
                if i >= 2:
                    hd = i - 2
                    pe.wait_ge(cturned, hd + 1)
                    if hd >= 2:
                        pe.wait_ge(oc_done, hd - 1)
                    for m in range(MT):
                        for s in range(m + 1):
                            ins = pe.matmul(bank[4 + hd % 2][:, m * P:(m + 1) * P],
                                            pcT[:, hd % 2, (m + s) * P:(m + s + 1) * P],
                                            vc[:, s, hd * P:(hd + 1) * P], start=(s == 0), stop=(s == m))
                    ins.then_inc(full[4 + hd % 2], 1)
            pe.wait_ge(oc_done, HC)
            turn("turn_y1", u)
            for c in range(2):
                chunk("out1", c, False, VERSION["turn_y1"])
            cross(1)
            mlp(1)


_INS = ["x", "mem", "norm_mix_g", "norm_xattn_g", "norm_mlp_g", "final_norm_g", "ab_w_in", "ab_conv_w",
        "ab_gate_b", "hgrn_lb_logits", "mlstm_norm_g", "hgrn_norm_g", "ab_w_out", "c_w_in", "c_fgate_b",
        "c_qnorm_g", "c_knorm_g", "c_w_out", "mem_norm_g", "mem_w_kv", "xa_w_q", "xa_w_o", "mlp_w1", "mlp_w2"]


def kernel(**inputs):
    import numpy as _np
    import concourse.bacc as _bacc
    from concourse import mybir as _mybir
    from concourse.bass_utils import run_bass_kernel_spmd as _run

    nc = _bacc.Bacc("TRN2", target_bir_lowering=False, num_devices=1)
    arrays, args = {}, []
    for name in _INS:
        a = _np.ascontiguousarray(inputs[name])
        arrays[f"in_{name}_dram"] = a
        args.append(nc.dram_tensor(f"in_{name}_dram", a.shape, _mybir.dt.from_np(a.dtype), kind="ExternalInput").ap())
    args.append(nc.dram_tensor("out_dram", (1, T, D), F32, kind="ExternalOutput").ap())
    trunk(nc, *args)
    r = _run(nc, [arrays], core_ids=[0])
    return r.results[0]["out_dram"]
```

```python
from contextlib import ExitStack, contextmanager

import numpy as np

import concourse.bass as bass
from concourse import mybir

F32 = mybir.dt.float32
F32R = mybir.dt.float32r
U8 = mybir.dt.uint8
ALU = mybir.AluOpType
ACT = mybir.ActivationFunctionType
AX = mybir.AxisListType

P = 128
BANK = 512
T = 256
MT = T // P
D = 1024
KD = D // P
FF = 4 * D
NJ = FF // BANK
HM = 4
HC = 8
HX = 4
XD = D // HX
EPS = 1e-6
NEG = -(2.0 ** 100)
RING = 4
RAW = 2
AHEAD = 3
KU = 4
LEVELS = [0, 64, 32, 16, 8, 4, 2, 1, 128]

PARAMS = [("norm_mix", 16), ("norm_xattn", 16), ("norm_mlp", 16), ("mem_norm", 8), ("mix_out", 8),
          ("conv", 32), ("lb", 8), ("qn", 1), ("kn", 1)]
PROW = {}
_n = 0
for _name, _rows in PARAMS:
    PROW[_name] = _n
    _n += _rows
NPAR = _n

TURN = {4: 1, 5: 1, 6: 1, 7: 1}
STAGES = [
    ("params", {7: 1}), ("turn_mix0", TURN), ("gate0", {4: 1}), ("in0", {0: 4, 2: 4}),
    ("mlstm", {4: 4, 5: 4, 6: 3, 7: 2}), ("turn_mem", TURN), ("kv", {0: 4}),
    ("hgrn", {2: 5, 3: 4, 4: 4, 5: 4, 6: 1, 7: 1}),
    ("turn_y0", TURN), ("out0", {0: 1, 2: 1}),
    ("turn_x0", TURN), ("xq0", {0: 1, 2: 1}), ("xattn0", {b: 2 for b in range(6)}),
    ("xo0", {0: 1, 2: 1}),
    ("turn_m0", TURN), ("mlp0", {0: 1, 2: 1, 4: NJ}),
    ("turn_mix1", TURN), ("gate1", {4: 1}), ("in1", {0: 4, 2: 4}),
    ("turn_q", TURN), ("turn_k", TURN), ("fox", {b: HC // 2 for b in range(6)}),
    ("turn_y1", TURN), ("out1", {0: 1, 2: 1}),
    ("turn_x1", TURN), ("xq1", {0: 1, 2: 1}), ("xattn1", {b: 2 for b in range(6)}),
    ("xo1", {0: 1, 2: 1}),
    ("turn_m1", TURN), ("mlp1", {0: 1, 2: 1, 4: NJ}),
]
FILLED = {}
_at = [0] * 8
for _name, _banks in STAGES:
    FILLED[_name] = list(_at)
    for _b, _k in _banks.items():
        _at[_b] += _k

UNITS = {}
_u = 0
for _name, _k in [("in0", 16), ("kv", 8), ("out0", 4), ("xq0", 4), ("xo0", 4), ("mlp0", 4 * NJ),
                  ("in1", 16), ("out1", 4), ("xq1", 4), ("xo1", 4), ("mlp1", 4 * NJ)]:
    UNITS[_name] = _u
    _u += _k
NU = _u

VERSION = {n: i for i, n in enumerate(["turn_mix0", "turn_mem", "turn_y0", "turn_x0", "xattn0", "turn_m0",
                                       "turn_mix1", "turn_y1", "turn_x1", "xattn1", "turn_m1"])}
SOURCE = {n: i for i, n in enumerate(["turn_mix0", "turn_mem", "turn_y0", "turn_x0", "turn_m0",
                                      "turn_mix1", "turn_x1", "turn_m1"])}
GAIN = {"turn_mem": PROW["mem_norm"], "turn_mix0": PROW["norm_mix"], "turn_mix1": PROW["norm_mix"] + 8,
        "turn_y0": PROW["mix_out"], "turn_y1": None, "turn_x0": PROW["norm_xattn"],
        "turn_x1": PROW["norm_xattn"] + 8, "turn_m0": PROW["norm_mlp"], "turn_m1": PROW["norm_mlp"] + 8}
NORMS = {n: i for i, n in enumerate(["turn_mix0", "turn_mem", "turn_x0", "turn_m0", "turn_mix1", "turn_x1",
                                     "turn_m1", "final"])}
ROOTS = {n: i for i, n in enumerate(["turn_mix0", "turn_mem", "mlstm", "hgrn", "turn_x0", "turn_m0", "turn_mix1",
                                     "q", "k", "turn_x1", "turn_m1", "final"])}
SUMS = {n: i for i, n in enumerate(["out0", "xo0", "mlp0", "out1", "xo1", "mlp1"])}
SUM_BEFORE = {"turn_mix0": 0, "turn_x0": 1, "turn_m0": 2, "turn_mix1": 3, "turn_x1": 4, "turn_m1": 5, "final": 6}

IN0 = [("oa", 1536, False), ("qa", 0, True), ("ka", 512, True), ("va", 1024, False),
       ("fb", 2568, True), ("qb", 2056, True), ("ib", 3080, False), ("gb", 3592, False)]
MLSTM_AT = 4
CONV0 = {"qa": 0, "ka": HM}
IN_DONE0 = [len([1 for q in range(b // 2, 8, 2) if IN0[q][0] not in CONV0]) for b in range(4)]
GATE0, GATE1 = 2048, 4096


def trunk(nc, x, mem, norm_mix_g, norm_xattn_g, norm_mlp_g, final_norm_g, ab_w_in, ab_conv_w, ab_gate_b,
          hgrn_lb_logits, mlstm_norm_g, hgrn_norm_g, ab_w_out, c_w_in, c_fgate_b, c_qnorm_g, c_knorm_g,
          c_w_out, mem_norm_g, mem_w_kv, xa_w_q, xa_w_o, mlp_w1, mlp_w2, out):
    ctx = ExitStack()
    with ctx:
        place = [nc.sbuf_base + (-nc.sbuf_base) % 64]

        def sb(name, shape, dt=F32, at=None):
            size = int(np.prod(shape[1:])) * (1 if dt == U8 else 4)
            size += (-size) % 64
            where = place[0] if at is None else at[0]
            t = nc.alloc_sbuf_tensor_at(name, shape, dt, offset=where)
            if at is None:
                place[0] += size
            else:
                at[0] += size
            return t

        def sem(name):
            return ctx.enter_context(nc.semaphore(name))

        bank = [ctx.enter_context(nc.psum_tensor(f"bank{b}", [P, BANK], F32)) for b in range(8)]

        h = sb("h", [P, MT, D])
        u = sb("u", [P, MT, D])
        act_hi = sb("act_hi", [P, KD, T], F32R)
        act_lo = sb("act_lo", [P, KD, T], F32R)
        mem_kT = sb("mem_kT", [P, KD, T])
        mem_v = sb("mem_v", [P, MT, D])
        raw = sb("raw", [P, RAW, KU, BANK])
        w_hi = sb("w_hi", [P, RING, KU, BANK], F32R)
        w_lo = sb("w_lo", [P, RING, KU, BANK], F32R)
        ident = sb("ident", [P, P])
        after_T = sb("after_T", [P, P])
        after = sb("after", [P, P])
        select = sb("select", [HC, HC, P])
        ones_row = sb("ones_row", [HC, T])
        zeros_row = sb("zeros_row", [HC, T])
        pairs = sb("pairs", [P, len(LEVELS) - 1, P], U8)
        par = sb("par", [P, NPAR])
        gate_w = sb("gate_w", [P, 2, KD, 8])
        gate_hi = sb("gate_hi", [P, 2, KD, 8], F32R)
        gate_lo = sb("gate_lo", [P, 2, KD, 8], F32R)
        bias_i = sb("bias_i", [HM, 1])
        bias_f = sb("bias_f", [HM, 1])
        bias_c = sb("bias_c", [HC, 1])
        lb = sb("lb", [P, 6, HM])
        st = sb("st", [P, 8, 16])
        cols = sb("cols", [P, 2, MT * HM])
        q_gain = sb("q_gain", [P, 1])
        xs = sb("xs", [P, 4, 2 * MT])

        arena = place[0]
        a = [arena]
        qkT = sb("qkT", [P, 2 * HM, T], at=a)
        va = sb("va", [P, MT, HM, P + 1], at=a)
        oa = sb("oa", [P, MT, BANK], at=a)
        vb = sb("vb", [P, MT, BANK], at=a)
        gb = sb("gb", [P, MT, BANK], at=a)
        qb = sb("qb", [P, HM, T], at=a)
        kb = sb("kb", [P, HM, T], at=a)
        cum = sb("cum", [P, HM, T], at=a)
        dec = sb("dec", [P, 2, HM, T], at=a)
        pair_w = sb("pair_w", [P, MT, HM, P], at=a)
        pair_x = sb("pair_x", [P, HM, P], at=a)
        mix_end = a[0]
        qd = sb("qd", [P, 2, HM, T], at=a)
        kd = sb("kd", [P, 2, HM, T], at=a)
        a2 = [mix_end]
        decay = sb("decay", [P, 2, 3 * P], at=a2)
        weight = sb("weight", [P, 2, 3 * P], at=a2)
        rows = sb("rows", [HC, 8, T], at=a2)
        assert a[0] <= nc.sbuf_usable_end and a2[0] <= nc.sbuf_usable_end, (a[0], a2[0], nc.sbuf_usable_end)
        a = [arena]
        qc = sb("qc", [P, MT, D], at=a)
        kc = sb("kc", [P, MT, D], at=a)
        vc = sb("vc", [P, MT, D], at=a)
        gc = sb("gc", [P, MT, D], at=a)
        qcT = sb("qcT", [P, HC, T], at=a)
        kcT = sb("kcT", [P, HC, T], at=a)
        pc = sb("pc", [P, 2, 3 * P], at=a)
        pcT = sb("pcT", [P, 2, 3 * P], at=a)
        rows1 = sb("rows1", [HC, 6, T], at=a)
        csum = sb("csum", [P, 4, 2 * HC], at=a)
        a = [arena]
        xqT = sb("xqT", [P, KD, T], at=a)
        px = sb("px", [P, 2, MT, T], at=a)
        pxT = sb("pxT", [P, 2, MT, T], at=a)
        a = [arena]
        hid_hi = sb("hid_hi", [P, 2, KU, T], F32R, at=a)
        hid_lo = sb("hid_lo", [P, 2, KU, T], F32R, at=a)
        relu = sb("relu", [P, 2, BANK], at=a)
        hid = sb("hid", [P, 2, BANK], at=a)
        a = [arena]
        par_rows = sb("par_rows", [NPAR, P], at=a)
        pairs_f = sb("pairs_f", [P, len(LEVELS) - 1, P], at=a)
        a = [arena]
        final_g = sb("final_g", [P, D], at=a)
        squares = sb("squares", [P, MT, D], at=a)

        x_in = [sem(f"x_in{m}") for m in range(MT)]
        mem_in, par_in, small_in, gain_in, out_done = map(
            sem, ["mem_in", "par_in", "small_in", "gain_in", "out_done"])
        gatehi_ready, gatelo_ready = sem("gatehi_ready"), sem("gatelo_ready")
        raw_in = [sem(f"raw_in{i}") for i in range(RAW)]
        hi_ready, lo_ready, unit_used = sem("hi_ready"), sem("lo_ready"), sem("unit_used")
        full = [sem(f"bank_full{b}") for b in range(8)]
        consts, par_ready, lb_in, lb_exp = sem("consts"), sem("par_ready"), sem("lb_in"), sem("lb_exp")
        square_sum, root_in, root_seed = sem("square_sum"), sem("root_in"), sem("root_seed")
        source_ready, acthi_ready, actlo_ready = sem("source_ready"), sem("acthi_ready"), sem("actlo_ready")
        sum_done, kv_done, xq_done = sem("sum_done"), sem("kv_done"), sem("xq_done")
        dve_step, act_step, pool_step = sem("dve_step"), sem("act_step"), sem("pool_step")
        relu_ready, hid_ready, hidhi_ready, hidlo_ready = map(
            sem, ["relu_ready", "hid_ready", "hidhi_ready", "hidlo_ready"])
        in_done = [sem(f"in_done{b}") for b in range(4)]
        tap_ready, conv_done, conv_silu, sigmoid_ready, forget_ready, keep_ready, log_forget = map(
            sem, ["tap_ready", "conv_done", "conv_silu", "sigmoid_ready", "forget_ready", "keep_ready", "log_forget"])
        log_out, rows_ready, cols_ready = sem("log_out"), sem("rows_ready"), sem("cols_ready")
        decay_ready, weight_ready, half_ready, y_ready, y_squared = map(
            sem, ["decay_ready", "weight_ready", "half_ready", "y_ready", "y_squared"])
        dist_ready, dec_ready, scaled_ready, selected, pairx_ready = map(
            sem, ["dist_ready", "dec_ready", "scaled_ready", "selected", "pairx_ready"])
        xmax, xexp, xnorm, xturned = map(sem, ["xmax", "xexp", "xnorm", "xturned"])
        squares_used, cnormed, qT_ready, kT_ready = map(sem, ["squares_used", "cnormed", "qT_ready", "kT_ready"])
        cmax, cexp, cturned, oc_done = map(sem, ["cmax", "cexp", "cturned", "oc_done"])
        fin_ready = sem("fin_ready")

        def wait_full(eng, stage, b, k=0):
            eng.wait_ge(full[b], FILLED[stage][b] + k + 1)

        def f(ap):
            return ap.bitcast(F32)

        def heads(ap, n=HM):
            return ap.rearrange("p (h d) -> p h d", h=n)

        def wait_chunk(eng, stage, c, i):
            if i == 0:
                wait_full(eng, stage, 2 * (c % 2), c // 2)
            else:
                eng.wait_ge(unit_used, UNITS[stage] + 2 * c + 2)

        def flat(ap):
            return ap.rearrange("p a b -> p (a b)")

        def flat3(ap):
            return ap.rearrange("p a b c -> p (a b c)")

        def spread(ap, n):
            return ap.unsqueeze(2).to_broadcast([P, ap.shape[1], n])

        def mlp_walk(eng, l, split, ahead, hidden):
            u0 = UNITS[f"mlp{l}"]

            def chunk(i, slot, which, j, buf):
                split(i + AHEAD, (slot + AHEAD) % RING)
                split(i + 1 + AHEAD, (slot + 1 + AHEAD) % RING)
                if which == 1:
                    hidden(j, buf, i)

            for n, (which, j, buf) in enumerate([(1, 0, 0), (1, 1, 1), (2, 0, 0)]):
                chunk(u0 + 2 * n, u0 + 2 * n, which, j, buf)
            turns = (NJ - 2) // 2 - l
            with eng.Fori(0, turns) as it:
                for n, (which, j, buf) in enumerate(in_order(it)):
                    chunk(8 * it + (u0 + 6 + 2 * n), u0 + 6 + 2 * n, which, j, buf)
            if l == 1:
                for n, (which, j, buf) in enumerate(in_order(turns)):
                    i = u0 + 6 + 8 * turns + 2 * n
                    ahead(i)
                    ahead(i + 1)
                    if which == 1:
                        hidden(j, buf, i)
            ahead(u0 + 4 * NJ - 2)
            ahead(u0 + 4 * NJ - 1)

        def last_of_half(level):
            v = cum[:].rearrange("p h (b two l) -> p (h b) two l", two=2, l=level)
            return v, v[:, :, 0, level - 1:level].to_broadcast([P, HM * T // (2 * level), level])

        def halves(ap, level):
            return ap.rearrange("p h (b two l) -> p (h b) two l", two=2, l=level)

        def in_order(it, j0=2):
            j = j0 + 2 * it
            return [(1, j, 0), (2, j - 1, 1), (1, j + 1, 1), (2, j, 0)]

        block = ctx.enter_context(nc.Block())

        @block.sync
        def _(sp):
            def load(i, slot, src):
                if not (isinstance(i, int) and i < RAW):
                    sp.wait_ge(lo_ready, i - RAW + 1)
                sp.dma_start(raw[:, slot], src).then_inc(raw_in[slot], 16)

            def load_square(stage, w, columns, c0=0):
                v = w.rearrange("(k p) n -> p k n", p=P)
                for c, n in enumerate(columns, c0):
                    for half in range(2):
                        load(UNITS[stage] + 2 * c + half, half, v[:, KU * half:KU * (half + 1), n:n + BANK])

            def load_mlp(l):
                w1 = mlp_w1[l].rearrange("(k p) n -> p k n", p=P)
                w2 = mlp_w2[l].rearrange("(k p) n -> p k n", p=P)
                u0 = UNITS[f"mlp{l}"]

                def chunk(i, which, j):
                    for half in range(2):
                        if which == 1:
                            load(i + half, half, w1[:, KU * half:KU * (half + 1), bass.ds(BANK * j, BANK)])
                        else:
                            load(i + half, half, w2[:, bass.ds(KU * j, KU), BANK * half:BANK * (half + 1)])

                for n, (which, j) in enumerate([(1, 0), (1, 1), (2, 0)]):
                    chunk(u0 + 2 * n, which, j)
                with sp.Fori(0, (NJ - 2) // 2) as it:
                    for n, (which, j, _) in enumerate(in_order(it)):
                        chunk(8 * it + (u0 + 6 + 2 * n), which, j)
                chunk(u0 + 4 * NJ - 2, 2, NJ - 1)

            for m in range(MT):
                sp.dma_start(h[:, m], x[0, m * P:(m + 1) * P, :]).then_inc(x_in[m], 16)
            load_square("in0", ab_w_in[0], [IN0[0][1]])
            sp.dma_start(mem_v[:], mem[0].rearrange("(m p) d -> p m d", p=P)).then_inc(mem_in, 16)
            load_square("in0", ab_w_in[0], [n for _, n, _ in IN0[1:]], 1)
            load_square("kv", mem_w_kv, range(0, 2 * D, BANK))
            load_square("out0", ab_w_out[0], [0, BANK])
            load_square("xq0", xa_w_q[0], [0, BANK])
            load_square("xo0", xa_w_o[0], [0, BANK])
            load_mlp(0)
            load_square("in1", c_w_in[0], range(0, 4 * D, BANK))
            load_square("out1", c_w_out[0], [0, BANK])
            load_square("xq1", xa_w_q[1], [0, BANK])
            load_square("xo1", xa_w_o[1], [0, BANK])
            load_mlp(1)
            sp.wait_ge(sum_done, 4 * SUM_BEFORE["final"])
            sp.dma_start(final_g[:], final_norm_g.rearrange("(a d) -> a d", a=1).to_broadcast([P, D])).then_inc(gain_in, 16)
            for m in range(MT):
                sp.wait_ge(fin_ready, m + 1)
                sp.dma_start(out[0, m * P:(m + 1) * P, :], u[:, m]).then_inc(out_done, 16)
            sp.wait_ge(out_done, 16 * MT)

        @block.gpsimd
        def _(pool):
            step = [0]

            def then(ins):
                step[0] += 1
                ins.then_inc(pool_step, 1)
                pool.wait_ge(pool_step, step[0])

            pool.memset(ident[:], 0.0).then_inc(pool_step, 1)
            pool.memset(after[:], 0.0).then_inc(pool_step, 1)
            pool.memset(after_T[:], 0.0).then_inc(pool_step, 1)
            pool.memset(select[:], 0.0).then_inc(pool_step, 1)
            pool.memset(ones_row[:], 1.0).then_inc(pool_step, 1)
            pool.memset(zeros_row[:], 0.0).then_inc(pool_step, 1)
            step[0] = 6
            pool.wait_ge(pool_step, 6)
            then(pool.affine_select(out=ident[:], in_=ident[:], pattern=[[-1, P]], compare_op=ALU.not_equal,
                                    fill=1.0, base=0, channel_multiplier=1))
            then(pool.affine_select(out=after_T[:], in_=after_T[:], pattern=[[1, P]], compare_op=ALU.is_ge,
                                    fill=NEG, base=0, channel_multiplier=-1))
            then(pool.affine_select(out=after[:], in_=after[:], pattern=[[-1, P]], compare_op=ALU.is_ge,
                                    fill=NEG, base=0, channel_multiplier=1))
            pool.affine_select(out=select[:], in_=select[:], pattern=[[-1, HC], [0, P]], compare_op=ALU.not_equal,
                               fill=1.0, base=0, channel_multiplier=1).then_inc(consts, 1)
            for n, level in enumerate(LEVELS[:-1]):
                lv = pairs_f[:, n]
                then(pool.memset(lv, 0.0 if level == 0 else 1.0))
                if level == 0:
                    then(pool.affine_select(out=lv, in_=lv, pattern=[[-1, P]], compare_op=ALU.not_equal, fill=1.0,
                                            base=0, channel_multiplier=1))
                    continue
                nb = P // (2 * level)
                v = lv.rearrange("p (b two l) -> p b two l", two=2, l=level)
                then(pool.memset(v[:, :, 0, :], 0.0))
                second = v[:, :, 1, :]
                then(pool.affine_select(out=second, in_=second, pattern=[[-2 * level, nb], [0, level]],
                                        compare_op=ALU.is_ge, fill=0.0, base=0, channel_multiplier=1))
                then(pool.affine_select(out=second, in_=second, pattern=[[2 * level, nb], [0, level]],
                                        compare_op=ALU.is_ge, fill=0.0, base=level - 1, channel_multiplier=-1))
            pool.tensor_copy(pairs[:], pairs_f[:]).then_inc(consts, 1)
            pool.memset(pair_w[:], 0.0).then_inc(consts, 1)
            pool.memset(va[:, :, :, P:P + 1], 1.0).then_inc(consts, 1)

        @block.scalar
        def _(act):
            step = [0]

            def then(ins):
                step[0] += 1
                ins.then_inc(act_step, 1)
                act.wait_ge(act_step, step[0])

            def split(i, slot):
                act.wait_ge(raw_in[slot % RAW], (i - slot % RAW) * (16 // RAW) + 16)
                if not (isinstance(i, int) and i < RING):
                    act.wait_ge(unit_used, i - RING + 1)
                act.activation(flat(w_hi[:, slot]), flat(raw[:, slot % RAW]), ACT.Copy).then_inc(hi_ready, 1)

            def ahead(i):
                if i + AHEAD < NU:
                    split(i + AHEAD, (i + AHEAD) % RING)

            def root(name, w):
                act.wait_ge(root_in, ROOTS[name] + 1)
                then(act.activation(st[:, 1, 0:w], st[:, 0, 0:w], ACT.Ln))
                act.activation(st[:, 2, 0:w], st[:, 1, 0:w], ACT.Exp, scale=-0.5).then_inc(root_seed, 1)

            def norm(stage, src, junk):
                act.activation(junk[:, 0], src[:, 0], ACT.Square, accum_out=st[:, 4, 0:1]).then_inc(square_sum, 1)
                root(stage, MT)

            def turn(stage):
                g = GAIN[stage]
                for k in range(KD):
                    if k % 2 == 0:
                        wait_full(act, stage, 4 + k // 2)
                    act.activation(act_hi[:, k], bank[4 + k // 2][:, (k % 2) * T:(k % 2 + 1) * T], ACT.Copy,
                                   scale=1.0 if g is None else par[:, g + k:g + k + 1]).then_inc(acthi_ready, 1)

            def gemm(stage, n, evacuate):
                for c in range(n):
                    ahead(UNITS[stage] + 2 * c)
                    ahead(UNITS[stage] + 2 * c + 1)
                    evacuate(c)

            def load_rows(name, src, skip=0):
                act.dma_start(par_rows[PROW[name] + skip:PROW[name] + skip + src.shape[0], :], src).then_inc(par_in, 16)

            load_rows("norm_mix", norm_mix_g.rearrange("l (k p) -> (l k) p", p=P))
            load_rows("norm_xattn", norm_xattn_g.rearrange("l (k p) -> (l k) p", p=P))
            load_rows("norm_mlp", norm_mlp_g.rearrange("l (k p) -> (l k) p", p=P))
            load_rows("mem_norm", mem_norm_g.rearrange("(k p) -> k p", p=P))
            load_rows("mix_out", mlstm_norm_g[0].rearrange("(k p) -> k p", p=P))
            load_rows("mix_out", hgrn_norm_g[0].rearrange("(k p) -> k p", p=P), HM)
            load_rows("conv", ab_conv_w[0].rearrange("j (k p) -> (j k) p", p=P))
            load_rows("lb", hgrn_lb_logits.rearrange("l (k p) -> (l k) p", p=P))
            load_rows("qn", c_qnorm_g)
            load_rows("kn", c_knorm_g)
            act.dma_start(gate_w[:, 0], ab_w_in[0].rearrange("(k p) n -> p k n", p=P)[:, :, GATE0:GATE0 + 8])\
               .then_inc(small_in, 16)
            act.dma_start(gate_w[:, 1], c_w_in[0].rearrange("(k p) n -> p k n", p=P)[:, :, GATE1:GATE1 + 8])\
               .then_inc(small_in, 16)
            act.dma_start(bias_i[:], ab_gate_b[0, 0:HM].rearrange("(p a) -> p a", a=1)).then_inc(small_in, 16)
            act.dma_start(bias_f[:], ab_gate_b[0, HM:2 * HM].rearrange("(p a) -> p a", a=1)).then_inc(small_in, 16)
            act.dma_start(bias_c[:], c_fgate_b[0].rearrange("(p a) -> p a", a=1)).then_inc(small_in, 16)

            def exp_and_ln():
                act.preload_act_table_set("natural_log_exp_and_others")

            exp_and_ln()
            act.wait_ge(x_in[0], 16)
            norm("turn_mix0", h, u)
            split(0, 0)
            split(1, 1)
            act.wait_ge(lb_in, 1)
            act.activation(lb[:, 3:5], lb[:, 3:5], ACT.Exp).then_inc(lb_exp, 1)
            act.wait_ge(small_in, 16 * 5)
            act.activation(flat3(gate_hi[:]), flat3(gate_w[:]), ACT.Copy).then_inc(gatehi_ready, 1)
            turn("turn_mix0")
            split(2, 2)
            act.wait_ge(mem_in, 16)
            norm("turn_mem", mem_v, u)

            act.wait_ge(consts, 4)

            def log_gate(stage, r, n, bias, zf):
                wait_full(act, stage, 4)
                then(act.activation(r[0:n, 0], zf, ACT.Abs, bias=bias[:]))
                then(act.activation(r[0:n, 0], r[0:n, 0], ACT.Exp, scale=-1.0))
                act.activation(r[0:n, 0], r[0:n, 0], ACT.Ln, bias=1.0).then_inc(log_out, 1)

            log_gate("gate0", rows, HM, bias_f, bank[4][0:HM, T:2 * T])

            def mlstm_decay(hd):
                wait_full(act, "mlstm", 4, hd)
                if hd >= 2:
                    act.wait_ge(weight_ready, hd - 1)
                act.activation(decay[:, hd % 2, 0:T], bank[4][:, 0:T], ACT.Exp, bias=cols[:, 0, hd:hd + 1])
                act.activation(decay[:, hd % 2, T:3 * P], bank[4][:, T:3 * P], ACT.Exp,
                               bias=cols[:, 0, HM + hd:HM + hd + 1]).then_inc(decay_ready, 1)

            def hgrn_decay(n):
                act.wait_ge(dist_ready, n)
                act.activation(flat(dec[:, n % 2]), flat(dec[:, n % 2]), ACT.Exp).then_inc(dec_ready, 1)

            def in0(c):
                name = IN0[c][0]
                for i in range(2):
                    b = 2 * (c % 2) + i
                    wait_chunk(act, "in0", c, i)
                    both = slice(2 * i, 2 * i + 2)
                    if name == "va":
                        act.activation(va[:, i, :, 0:P], heads(bank[b][:]), ACT.Copy).then_inc(in_done[b], 1)
                    elif name in CONV0:
                        for k in range(CONV0[name] + 2 * i, CONV0[name] + 2 * i + 2):
                            w = PROW["conv"] + 3 * KD + k
                            act.activation(qkT[:, k], bank[b][:, (k % 2) * T:(k % 2 + 1) * T], ACT.Copy,
                                           scale=par[:, w:w + 1]).then_inc(tap_ready, 1)
                    elif name == "fb":
                        act.activation(flat(dec[:, 0, both]), bank[b][:], ACT.Sigmoid).then_inc(sigmoid_ready, 1)
                        act.activation(flat(kb[:, both]), bank[b][:], ACT.Sigmoid, scale=-1.0).then_inc(in_done[b], 1)
                    elif name == "oa":
                        act.activation(oa[:, i], bank[b][:], ACT.Sigmoid).then_inc(in_done[b], 1)
                    else:
                        dst = {"qb": flat(qb[:, both]), "ib": vb[:, i], "gb": gb[:, i]}[name]
                        act.activation(dst, bank[b][:], ACT.Silu).then_inc(in_done[b], 1)
                if name in CONV0:
                    for i in range(2):
                        k = CONV0[name] + 2 * i
                        act.wait_ge(conv_done, k // 2 + 1)
                        act.activation(flat(qkT[:, k:k + 2]), flat(qkT[:, k:k + 2]), ACT.Silu).then_inc(conv_silu, 1)

            for c in range(8):
                if c == MLSTM_AT:
                    wait_full(act, "mlstm", 6)
                    exp_and_ln()
                    act.activation(cols[:, 1], bank[6][:, MT * HM:2 * MT * HM], ACT.Exp)
                    act.activation(cols[:, 0], bank[6][:, 0:MT * HM], ACT.Copy).then_inc(cols_ready, 1)
                    act.wait_ge(cols_ready, 1)
                if MLSTM_AT <= c < MLSTM_AT + 2:
                    if c > MLSTM_AT:
                        exp_and_ln()
                    mlstm_decay(2 * (c - MLSTM_AT))
                ahead(UNITS["in0"] + 2 * c)
                if MLSTM_AT <= c < MLSTM_AT + 2:
                    mlstm_decay(2 * (c - MLSTM_AT) + 1)
                ahead(UNITS["in0"] + 2 * c + 1)
                if c == MLSTM_AT + 1:
                    act.wait_ge(forget_ready, 2)
                    act.activation(flat(dec[:, 1]), flat(dec[:, 0]), ACT.Ln).then_inc(log_forget, 1)
                in0(c)
            exp_and_ln()
            hgrn_decay(1)

            act.wait_ge(unit_used, UNITS["in0"] + 16)
            turn("turn_mem")
            for m in range(MT):
                act.wait_ge(y_ready, m + 1)
                act.activation(flat(qkT[:, 2 * m:2 * m + 2]), u[:, m, 0:BANK], ACT.Square).then_inc(y_squared, 1)

            for n in range(1, len(LEVELS)):
                if n + 1 < len(LEVELS):
                    hgrn_decay(n + 1)
                if n == 2:
                    root("mlstm", MT * HM)
                unit = n - 1
                if unit % 2:
                    c = unit // 2
                    for i in range(2):
                        if i == 0:
                            wait_full(act, "kv", 0, c)
                        else:
                            act.wait_ge(unit_used, UNITS["kv"] + 2 * c + 2)
                        if c < 2:
                            dst = flat(mem_kT[:, 4 * c + 2 * i:4 * c + 2 * i + 2])
                        else:
                            dst = mem_v[:, i, (c - 2) * BANK:(c - 1) * BANK]
                        act.activation(dst, bank[i][:], ACT.Copy).then_inc(kv_done, 1)
                ahead(UNITS["kv"] + unit)
            wait_full(act, "hgrn", 2, 4)
            act.activation(flat(pair_x[:]), bank[2][:], ACT.Copy).then_inc(pairx_ready, 1)
            for m in range(MT):
                wait_full(act, "hgrn", 6 + m)
                act.activation(flat(qkT[:, 2 * m:2 * m + 2]), bank[6 + m][:], ACT.Square).then_inc(y_squared, 1)
            root("hgrn", MT * HM)
            turn("turn_y0")
            gemm("out0", 2, lambda c: None)

            def cross(l):
                act.wait_ge(sum_done, 4 * SUM_BEFORE[f"turn_x{l}"])
                norm(f"turn_x{l}", h, u)
                turn(f"turn_x{l}")

                def xq(c):
                    for i in range(2):
                        b = 2 * c + i
                        wait_chunk(act, f"xq{l}", c, i)
                        act.activation(flat(xqT[:, 2 * b:2 * b + 2]), bank[b][:], ACT.Copy, scale=XD ** -0.5)\
                           .then_inc(xq_done, 1)
                gemm(f"xq{l}", 2, xq)
                stage = f"xattn{l}"
                for i in range(HX + 2):
                    if i < HX:
                        act.wait_ge(xmax, HX * l + i + 1)
                        if i >= 2:
                            wait_full(act, stage, 2 + i % 2, i // 2 - 1)
                        for m in range(MT):
                            c = 2 * (i % 2) + m
                            ins = act.activation(px[:, i % 2, m], bank[i % 2][:, m * T:(m + 1) * T], ACT.Exp,
                                                 bias=xs[:, 1, c:c + 1], accum_out=xs[:, 2, c:c + 1])
                        ins.then_inc(xexp, 1)
                    if 1 <= i <= HX:
                        hd = i - 1
                        wait_full(act, stage, 2 + hd % 2, hd // 2)
                        if hd >= 2:
                            wait_full(act, stage, 4 + hd % 2, hd // 2 - 1)
                        act.activation(flat(pxT[:, hd % 2]), bank[2 + hd % 2][:], ACT.Copy).then_inc(xturned, 1)
                    if i >= 2:
                        hd = i - 2
                        wait_full(act, stage, 4 + hd % 2, hd // 2)
                        act.activation(flat(act_hi[:, 2 * hd:2 * hd + 2]), bank[4 + hd % 2][:], ACT.Copy)\
                           .then_inc(acthi_ready, 2)
                gemm(f"xo{l}", 2, lambda c: None)

            def mlp(l):
                act.wait_ge(sum_done, 4 * SUM_BEFORE[f"turn_m{l}"])
                norm(f"turn_m{l}", h, u)
                turn(f"turn_m{l}")
                stage = f"mlp{l}"

                def hidden(j, buf, unit):
                    for i in range(2):
                        if i == 0:
                            wait_full(act, stage, 4, j)
                        else:
                            act.wait_ge(unit_used, unit + 2)
                        act.activation(relu[:, i], bank[4 + i][:], ACT.Relu).then_inc(relu_ready, 1)
                    for i in range(2):
                        act.wait_ge(hid_ready, 2 * j + (2 * NJ * l + i + 1))
                        act.activation(flat(hid_hi[:, buf, 2 * i:2 * i + 2]), hid[:, i], ACT.Copy)\
                           .then_inc(hidhi_ready, 1)
                mlp_walk(act, l, split, ahead, hidden)

            cross(0)
            mlp(0)

            act.wait_ge(sum_done, 4 * SUM_BEFORE["turn_mix1"])
            norm("turn_mix1", h, u)
            turn("turn_mix1")
            log_gate("gate1", rows1, HC, bias_c, bank[4][0:HC, 0:T])

            def in1(c):
                which, n = c // 2, c % 2
                for m in range(2):
                    b = 2 * (c % 2) + m
                    wait_chunk(act, "in1", c, m)
                    part = slice(n * BANK, (n + 1) * BANK)
                    if which < 2:
                        act.activation((qc, kc)[which][:, m, part], bank[b][:], ACT.Copy)
                        if which == 1:
                            act.wait_ge(squares_used, 2 * n + m + 1)
                        act.activation(u[:, m, part], bank[b][:], ACT.Square).then_inc(in_done[b], 1)
                    elif which == 2:
                        act.activation(vc[:, m, part], bank[b][:], ACT.Copy).then_inc(in_done[b], 1)
                    else:
                        act.activation(gc[:, m, part], bank[b][:], ACT.Exp, scale=-1.0).then_inc(in_done[b], 1)
                if c == 1:
                    root("q", MT * HC)
                if c == 3:
                    root("k", MT * HC)
                    for k in range(HC):
                        if k % 2 == 0:
                            wait_full(act, "turn_q", 4 + k // 2)
                        act.activation(qcT[:, k], bank[4 + k // 2][:, (k % 2) * T:(k % 2 + 1) * T], ACT.Copy,
                                       scale=q_gain[:]).then_inc(qT_ready, 1)
            gemm("in1", 8, in1)

            for i in range(HC + 1):
                if i < HC:
                    act.wait_ge(cmax, i + 1)
                    if i >= 2:
                        wait_full(act, "fox", 2 + i % 2, i // 2 - 1)
                    for m in range(MT):
                        part = slice(m * P, (1 + 2 * m) * P)
                        ins = act.activation(pc[:, i % 2, part], bank[i % 2][:, part], ACT.Exp,
                                             bias=csum[:, 1, 2 * i + m:2 * i + m + 1],
                                             accum_out=csum[:, 2, 2 * i + m:2 * i + m + 1])
                    ins.then_inc(cexp, 1)
                if i >= 1:
                    hd = i - 1
                    wait_full(act, "fox", 2 + hd % 2, hd // 2)
                    if hd >= 2:
                        wait_full(act, "fox", 4 + hd % 2, hd // 2 - 1)
                    act.activation(pcT[:, hd % 2], bank[2 + hd % 2][:, 0:3 * P], ACT.Copy).then_inc(cturned, 1)
            turn("turn_y1")
            gemm("out1", 2, lambda c: None)
            cross(1)
            mlp(1)
            act.wait_ge(sum_done, 4 * SUM_BEFORE["final"])
            norm("final", h, squares)

        @block.vector
        def _(dve):
            step = [0]

            def then(ins):
                step[0] += 1
                ins.then_inc(dve_step, 1)
                dve.wait_ge(dve_step, step[0])

            def split(i, slot):
                dve.wait_ge(hi_ready, i + 1)
                dve.tensor_tensor(flat(w_lo[:, slot]), flat(raw[:, slot % RAW]), f(flat(w_hi[:, slot])),
                                  ALU.subtract).then_inc(lo_ready, 1)

            def ahead(i):
                if i + AHEAD < NU:
                    split(i + AHEAD, (i + AHEAD) % RING)

            def root(name, w, sums, n):
                dve.tensor_scalar(st[:, 0, 0:w], sums, 1.0 / n, EPS, ALU.mult, ALU.add).then_inc(root_in, 1)
                dve.wait_ge(root_seed, ROOTS[name] + 1)
                then(dve.tensor_tensor(st[:, 3, 0:w], st[:, 0, 0:w], st[:, 2, 0:w], ALU.mult))
                then(dve.tensor_tensor(st[:, 3, 0:w], st[:, 3, 0:w], st[:, 2, 0:w], ALU.mult))
                then(dve.tensor_scalar(st[:, 3, 0:w], st[:, 3, 0:w], -0.5, 1.5, ALU.mult, ALU.add))
                then(dve.tensor_tensor(st[:, 6, 0:w], st[:, 3, 0:w], st[:, 2, 0:w], ALU.mult))

            def norm_sums(stage, src, junk):
                then(dve.tensor_tensor_reduce(out=junk[:, 1], in0=src[:, 1], in1=src[:, 1], scale=1.0, scalar=0.0,
                                              op0=ALU.mult, op1=ALU.add, accum_out=st[:, 4, 1:2]))
                dve.wait_ge(square_sum, NORMS[stage] + 1)
                root(stage, MT, st[:, 4, 0:MT], D)

            def norm(stage, src, to=u):
                norm_sums(stage, src, u)
                for m in range(MT):
                    dve.tensor_scalar(to[:, m], src[:, m], st[:, 6, m:m + 1], None, ALU.mult).then_inc(source_ready, 1)

            def turn(stage):
                g = GAIN[stage]
                for k in range(KD):
                    if k % 2 == 0:
                        dve.wait_ge(acthi_ready, KD * VERSION[stage] + k + 2)
                    z = bank[4 + k // 2][:, (k % 2) * T:(k % 2 + 1) * T]
                    if g is None:
                        ins = dve.tensor_tensor(act_lo[:, k], z, f(act_hi[:, k]), ALU.subtract)
                    else:
                        ins = dve.scalar_tensor_tensor(out=act_lo[:, k], in0=z, scalar=par[:, g + k:g + k + 1],
                                                       in1=f(act_hi[:, k]), op0=ALU.mult, op1=ALU.subtract)
                    ins.then_inc(actlo_ready, 1)

            def gemm(stage, n, evacuate):
                for c in range(n):
                    ahead(UNITS[stage] + 2 * c)
                    ahead(UNITS[stage] + 2 * c + 1)
                    evacuate(c)

            def add_to_h(stage, c, last_unit=None):
                last_unit = UNITS[stage] + 2 * c + 1 if last_unit is None else last_unit
                for m in range(MT):
                    if m == 0:
                        wait_full(dve, stage, 2 * c)
                    else:
                        dve.wait_ge(unit_used, last_unit + 1)
                    part = h[:, m, c * BANK:(c + 1) * BANK]
                    dve.tensor_tensor(part, bank[2 * c + m][:], part, ALU.add).then_inc(sum_done, 1)

            wait_full(dve, "params", 7)
            then(dve.tensor_copy(par[:], bank[7][:, 0:NPAR]))
            dve.tensor_scalar(q_gain[:], par[:, PROW["qn"]:PROW["qn"] + 1], P ** -0.5, None, ALU.mult)\
               .then_inc(par_ready, 1)
            l0, l1 = par[:, PROW["lb"]:PROW["lb"] + HM], par[:, PROW["lb"] + HM:PROW["lb"] + 2 * HM]
            then(dve.tensor_tensor(lb[:, 2], l0, l1, ALU.max))
            dve.tensor_tensor(lb[:, 3], l0, lb[:, 2], ALU.subtract)
            dve.tensor_tensor(lb[:, 4], l1, lb[:, 2], ALU.subtract).then_inc(lb_in, 1)
            dve.wait_ge(x_in[0], 16)
            dve.wait_ge(x_in[1], 16)
            norm("turn_mix0", h)
            split(0, 0)
            split(1, 1)
            dve.wait_ge(gatehi_ready, 1)
            dve.tensor_tensor(flat3(gate_lo[:]), flat3(gate_w[:]), f(flat3(gate_hi[:])), ALU.subtract)\
               .then_inc(gatelo_ready, 1)
            turn("turn_mix0")
            split(2, 2)
            dve.wait_ge(lb_exp, 1)
            then(dve.tensor_tensor(lb[:, 2], lb[:, 3], lb[:, 4], ALU.add))
            then(dve.reciprocal(lb[:, 5], lb[:, 2]))
            dve.tensor_tensor(lb[:, 0], lb[:, 3], lb[:, 5], ALU.mult)
            then(dve.tensor_tensor(lb[:, 1], lb[:, 4], lb[:, 5], ALU.mult))
            dve.wait_ge(mem_in, 16)
            norm("turn_mem", mem_v, mem_v)

            dve.wait_ge(consts, 4)

            def log_sigmoid_sum(r, n, bias, zf, count):
                dve.wait_ge(log_out, count)
                then(dve.tensor_scalar(r[0:n, 1], zf, bias[:], 0.0, ALU.add, ALU.min))
                then(dve.tensor_tensor(r[0:n, 1], r[0:n, 1], r[0:n, 0], ALU.subtract))
                then(dve.tensor_tensor_scan(r[0:n, 3], r[0:n, 1], r[0:n, 1], 0.0, ALU.add, ALU.bypass))

            wait_full(dve, "gate0", 4)
            dve.wait_ge(small_in, 16 * 5)
            dve.wait_ge(log_out, 1)
            then(dve.tensor_scalar(rows[0:HM, 2], bank[4][0:HM, 0:T], bias_i[:], None, ALU.add))
            log_sigmoid_sum(rows, HM, bias_f, bank[4][0:HM, T:2 * T], 1)
            then(dve.tensor_tensor(rows[0:HM, 4], rows[0:HM, 2], rows[0:HM, 3], ALU.subtract))
            then(dve.tensor_tensor_scan(rows[0:HM, 5], rows[0:HM, 4], rows[0:HM, 4], 0.0, ALU.max, ALU.bypass))
            dve.tensor_scalar(rows[0:HM, 6], rows[0:HM, 5], -1.0, None, ALU.mult)
            dve.scalar_tensor_tensor(out=rows[0:HM, 7], in0=rows[0:HM, 3], scalar=-1.0, in1=rows[0:HM, 5],
                                     op0=ALU.mult, op1=ALU.subtract).then_inc(rows_ready, 1)

            def mlstm_weight(hd):
                dve.wait_ge(decay_ready, hd + 1)
                wait_full(dve, "mlstm", 5, hd)
                dve.scalar_tensor_tensor(out=weight[:, hd % 2], in0=bank[5][:, 0:3 * P], scalar=P ** -0.5,
                                         in1=decay[:, hd % 2], op0=ALU.mult, op1=ALU.mult).then_inc(weight_ready, 1)

            def finish_pair(hp):
                for m in range(MT):
                    b = 6 + m
                    wait_full(dve, "mlstm", b, hp + (b == 6))
                    v = bank[b][:, 0:2 * (P + 1)].rearrange("p (h d) -> p h d", d=P + 1)
                    den = v[:, :, P:P + 1].rearrange("p h d -> p (h d)")
                    floor = cols[:, 1, HM * m + 2 * hp:HM * m + 2 * hp + 2]
                    c = slice(4 * m + 2 * hp, 4 * m + 2 * hp + 2)
                    then(dve.scalar_tensor_tensor(out=st[:, 7, c], in0=den, scalar=-1.0, in1=floor,
                                                  op0=ALU.mult, op1=ALU.max))
                    then(dve.tensor_tensor(st[:, 7, c], den, st[:, 7, c], ALU.max))
                    then(dve.reciprocal(st[:, 7, c], st[:, 7, c]))
                    for k in range(2):
                        hd = 2 * hp + k
                        part = slice(hd * P, (hd + 1) * P)
                        ins = dve.scalar_tensor_tensor(out=u[:, m, part], in0=v[:, k, 0:P],
                                                       scalar=st[:, 7, 4 * m + hd:4 * m + hd + 1],
                                                       in1=oa[:, m, part], op0=ALU.mult, op1=ALU.mult)
                    ins.then_inc((half_ready, y_ready)[hp], 1)

            def in0(c):
                name = IN0[c][0]
                if name in CONV0:
                    for i in range(2):
                        b = 2 * (c % 2) + i
                        wait_chunk(dve, "in0", c, i)
                        for lag in range(1, 4):
                            for k in range(CONV0[name] + 2 * i, CONV0[name] + 2 * i + 2):
                                if lag == 1 and k % 2 == 0:
                                    dve.wait_ge(tap_ready, k + 2)
                                w = PROW["conv"] + (3 - lag) * KD + k
                                z = bank[b][:, (k % 2) * T:(k % 2 + 1) * T - lag]
                                ins = dve.scalar_tensor_tensor(out=qkT[:, k, lag:T], in0=z, scalar=par[:, w:w + 1],
                                                               in1=qkT[:, k, lag:T], op0=ALU.mult, op1=ALU.add)
                                if k % 2 and lag < 3:
                                    then(ins)
                        ins.then_inc(conv_done, 1)
                if name == "fb":
                    for i in range(2):
                        dve.wait_ge(sigmoid_ready, i + 1)
                        dve.wait_ge(in_done[2 * (c % 2) + i], c // 2)
                        for hd in range(2 * i, 2 * i + 2):
                            ins = dve.tensor_scalar(dec[:, 0, hd], dec[:, 0, hd], lb[:, 1, hd:hd + 1],
                                                    lb[:, 0, hd:hd + 1], ALU.mult, ALU.add)
                        ins.then_inc(forget_ready, 1)
                        for hd in range(2 * i, 2 * i + 2):
                            ins = dve.tensor_scalar(kb[:, hd], kb[:, hd], lb[:, 1, hd:hd + 1], None, ALU.mult)
                        ins.then_inc(keep_ready, 1)

            def distance(n):
                level = LEVELS[n]
                if n >= 3:
                    dve.wait_ge(scaled_ready, n - 2)
                v, mid = last_of_half(level)
                d = halves(dec[:, n % 2], level)
                dve.tensor_tensor(d[:, :, 0, :], mid, v[:, :, 0, :], ALU.subtract)
                dve.tensor_tensor(d[:, :, 1, :], v[:, :, 1, :], mid, ALU.subtract).then_inc(dist_ready, 1)

            def scale(n):
                dve.wait_ge(dec_ready, n)
                if n <= 2:
                    dve.tensor_tensor(flat(qd[:, n % 2]), flat(qb[:]), flat(dec[:, n % 2]), ALU.mult)
                    dve.tensor_tensor(flat(kd[:, n % 2]), flat(kb[:]), flat(dec[:, n % 2]), ALU.mult)\
                       .then_inc(scaled_ready, 1)
                    return
                level = LEVELS[n]
                for to, of, which in ((qd, qb, 1), (kd, kb, 0)):
                    ins = dve.tensor_tensor(halves(to[:, n % 2], level)[:, :, which, :],
                                            halves(of[:], level)[:, :, which, :],
                                            halves(dec[:, n % 2], level)[:, :, which, :], ALU.mult)
                ins.then_inc(scaled_ready, 1)

            for c in range(8):
                if c == MLSTM_AT:
                    dve.wait_ge(cols_ready, 1)
                    dve.wait_ge(in_done[0], 1)
                    dve.wait_ge(in_done[1], 1)
                if MLSTM_AT <= c < MLSTM_AT + 2:
                    mlstm_weight(2 * (c - MLSTM_AT))
                if c >= MLSTM_AT + 2:
                    finish_pair(c - MLSTM_AT - 2)
                ahead(UNITS["in0"] + 2 * c)
                if MLSTM_AT <= c < MLSTM_AT + 2:
                    mlstm_weight(2 * (c - MLSTM_AT) + 1)
                ahead(UNITS["in0"] + 2 * c + 1)
                in0(c)
                if c == MLSTM_AT + 2:
                    dve.wait_ge(log_forget, 1)
                    for hd in range(HM):
                        ins = dve.tensor_tensor_scan(cum[:, hd], dec[:, 1, hd], dec[:, 1, hd], 0.0, ALU.add,
                                                     ALU.bypass)
                    then(ins)
                    distance(1)
            for b in range(4):
                dve.wait_ge(in_done[b], IN_DONE0[b])
            dve.wait_ge(keep_ready, 2)
            distance(2)
            scale(1)

            def head_sums(first):
                for m in range(MT):
                    dve.wait_ge(y_squared, first + m + 1)
                    then(dve.tensor_reduce(st[:, 5, HM * m:HM * (m + 1)], heads(flat(qkT[:, 2 * m:2 * m + 2])), AX.X,
                                           ALU.add))

            def mlstm_norm():
                head_sums(0)
                root("mlstm", MT * HM, st[:, 5, 0:MT * HM], P)
                for m in range(MT):
                    y = heads(u[:, m, 0:BANK])
                    dve.tensor_tensor(y, y, spread(st[:, 6, HM * m:HM * (m + 1)], P), ALU.mult)

            def choose(n):
                for tile in range(MT):
                    b = 2 + 2 * (n % 2) + tile
                    wait_full(dve, "hgrn", b, n // 2)
                    if n:
                        dve.wait_ge(selected, 2 * (n - 1) + tile + 1)
                    dve.copy_predicated(pair_w[:, tile], pairs[:, n].unsqueeze(1).to_broadcast([P, HM, P]),
                                        heads(bank[b][:])).then_inc(selected, 1)

            turn("turn_mem")
            for n in range(1, len(LEVELS)):
                choose(n - 1)
                if n + 2 < len(LEVELS):
                    distance(n + 2)
                if n + 1 < len(LEVELS):
                    scale(n + 1)
                if n == 2:
                    mlstm_norm()
                ahead(UNITS["kv"] + n - 1)
            head_sums(2)
            root("hgrn", MT * HM, st[:, 5, 0:MT * HM], P)
            for m in range(MT):
                for hd in range(HM):
                    part = slice(hd * P, (hd + 1) * P)
                    ins = dve.scalar_tensor_tensor(out=u[:, m, BANK + hd * P:BANK + (hd + 1) * P],
                                                   in0=bank[6 + m][:, part], scalar=st[:, 6, HM * m + hd:HM * m + hd + 1],
                                                   in1=gb[:, m, part], op0=ALU.mult, op1=ALU.mult)
                ins.then_inc(source_ready, 1)
            turn("turn_y0")
            gemm("out0", 2, lambda c: add_to_h("out0", c))

            def cross(l):
                dve.wait_ge(sum_done, 4 * SUM_BEFORE[f"turn_x{l}"])
                norm(f"turn_x{l}", h)
                turn(f"turn_x{l}")
                gemm(f"xq{l}", 2, lambda c: None)
                stage = f"xattn{l}"
                for i in range(HX + 2):
                    if i < HX:
                        c = slice(2 * (i % 2), 2 * (i % 2) + 2)
                        wait_full(dve, stage, i % 2, i // 2)
                        then(dve.tensor_reduce(xs[:, 0, c], bank[i % 2][:].rearrange("p (m t) -> p m t", m=MT), AX.X,
                                               ALU.max))
                        dve.tensor_scalar(xs[:, 1, c], xs[:, 0, c], -1.0, None, ALU.mult).then_inc(xmax, 1)
                    if 1 <= i <= HX:
                        hd = i - 1
                        c = slice(2 * (hd % 2), 2 * (hd % 2) + 2)
                        dve.wait_ge(xexp, HX * l + hd + 1)
                        then(dve.reciprocal(xs[:, 3, c], xs[:, 2, c]))
                        dve.tensor_tensor(px[:, hd % 2], px[:, hd % 2], spread(xs[:, 3, c], T), ALU.mult)\
                           .then_inc(xnorm, 1)
                    if i >= 2:
                        hd = i - 2
                        dve.wait_ge(acthi_ready, KD * VERSION[stage] + 2 * hd + 2)
                        both = slice(2 * hd, 2 * hd + 2)
                        dve.tensor_tensor(flat(act_lo[:, both]), bank[4 + hd % 2][:], f(flat(act_hi[:, both])),
                                          ALU.subtract).then_inc(actlo_ready, 2)
                gemm(f"xo{l}", 2, lambda c: add_to_h(f"xo{l}", c))

            def mlp(l):
                dve.wait_ge(sum_done, 4 * SUM_BEFORE[f"turn_m{l}"])
                norm(f"turn_m{l}", h)
                turn(f"turn_m{l}")

                def hidden(j, buf, unit):
                    for i in range(2):
                        if l or not isinstance(j, int) or j:
                            dve.wait_ge(hidlo_ready, 2 * j + (2 * NJ * l + i - 1))
                        dve.wait_ge(relu_ready, 2 * j + (2 * NJ * l + i + 1))
                        dve.scalar_tensor_tensor(out=hid[:, i], in0=bank[4 + i][:], scalar=0.0, in1=relu[:, i],
                                                 op0=ALU.max, op1=ALU.mult).then_inc(hid_ready, 1)
                    for i in range(2):
                        dve.wait_ge(hidhi_ready, 2 * j + (2 * NJ * l + i + 1))
                        dve.tensor_tensor(flat(hid_lo[:, buf, 2 * i:2 * i + 2]), hid[:, i],
                                          f(flat(hid_hi[:, buf, 2 * i:2 * i + 2])), ALU.subtract)\
                           .then_inc(hidlo_ready, 1)
                mlp_walk(dve, l, split, ahead, hidden)
                for c in range(2):
                    add_to_h(f"mlp{l}", c, UNITS[f"mlp{l}"] + 4 * NJ - 2 + c)

            cross(0)
            mlp(0)

            dve.wait_ge(sum_done, 4 * SUM_BEFORE["turn_mix1"])
            norm("turn_mix1", h)
            turn("turn_mix1")
            wait_full(dve, "gate1", 4)
            log_sigmoid_sum(rows1, HC, bias_c, bank[4][0:HC, 0:T], 2)
            dve.tensor_scalar(rows1[0:HC, 4], rows1[0:HC, 3], -1.0, None, ALU.mult).then_inc(rows_ready, 1)

            def in1(c):
                which, n = c // 2, c % 2
                for m in range(MT):
                    b = 2 * (c % 2) + m
                    part = slice(n * BANK, (n + 1) * BANK)
                    if which < 2:
                        dve.wait_ge(in_done[b], IN_DONE0[b] + c // 2 + 1)
                        dve.tensor_reduce(st[:, 5, HC * m + HM * n:HC * m + HM * (n + 1)], heads(u[:, m, part]), AX.X,
                                          ALU.add).then_inc(squares_used, 1)
                    if which == 3:
                        dve.wait_ge(in_done[b], IN_DONE0[b] + c // 2 + 1)
                        then(dve.tensor_scalar(gc[:, m, part], gc[:, m, part], 1.0, None, ALU.add))
                        ins = dve.reciprocal(gc[:, m, part], gc[:, m, part])
                        if m == 1:
                            then(ins)
                if which < 2 and n == 1:
                    dve.wait_ge(squares_used, 4 * (which + 1))
                    root("qk"[which], MT * HC, st[:, 5, 0:MT * HC], P)
                    z = (qc, kc)[which]
                    for m in range(MT):
                        zm = heads(z[:, m], HC)
                        dve.tensor_tensor(zm, zm, spread(st[:, 6, HC * m:HC * (m + 1)], P), ALU.mult)\
                           .then_inc(cnormed, 1)
                if c == 5:
                    for k in range(HC):
                        if k % 2 == 0:
                            wait_full(dve, "turn_k", 4 + k // 2)
                        dve.tensor_scalar(kcT[:, k], bank[4 + k // 2][:, (k % 2) * T:(k % 2 + 1) * T],
                                          par[:, PROW["kn"]:PROW["kn"] + 1], None, ALU.mult).then_inc(kT_ready, 1)
            gemm("in1", 8, in1)

            for i in range(HC + 2):
                if i < HC:
                    wait_full(dve, "fox", i % 2, i // 2)
                    for m in range(MT):
                        ins = dve.tensor_reduce(csum[:, 0, 2 * i + m:2 * i + m + 1],
                                                bank[i % 2][:, m * P:(1 + 2 * m) * P], AX.X, ALU.max)
                    then(ins)
                    dve.tensor_scalar(csum[:, 1, 2 * i:2 * i + 2], csum[:, 0, 2 * i:2 * i + 2], -1.0, None, ALU.mult)\
                       .then_inc(cmax, 1)
                if i >= 2:
                    hd = i - 2
                    dve.wait_ge(cexp, hd + 1)
                    then(dve.reciprocal(csum[:, 3, 2 * hd:2 * hd + 2], csum[:, 2, 2 * hd:2 * hd + 2]))
                    wait_full(dve, "fox", 4 + hd % 2, hd // 2)
                    part = slice(hd * P, (hd + 1) * P)
                    for m in range(MT):
                        ins = dve.scalar_tensor_tensor(out=u[:, m, part], in0=bank[4 + hd % 2][:, m * P:(m + 1) * P],
                                                       scalar=csum[:, 3, 2 * hd + m:2 * hd + m + 1],
                                                       in1=gc[:, m, part], op0=ALU.mult, op1=ALU.mult)
                    ins.then_inc(oc_done, 1)
            turn("turn_y1")
            gemm("out1", 2, lambda c: add_to_h("out1", c))
            cross(1)
            mlp(1)
            dve.wait_ge(sum_done, 4 * SUM_BEFORE["final"])
            norm_sums("final", h, squares)
            dve.wait_ge(gain_in, 16)
            for m in range(MT):
                dve.scalar_tensor_tensor(out=u[:, m], in0=h[:, m], scalar=st[:, 6, m:m + 1], in1=final_g[:],
                                         op0=ALU.mult, op1=ALU.mult).then_inc(fin_ready, 1)

        @block.tensor
        def _(pe):
            def three(o, a_hi, a_lo, b_hi, b_lo, start, stop, mark=False):
                pe.matmul(o, a_hi, b_hi, start=start, stop=False, skip_group_check=True)
                pe.matmul(o, a_hi, b_lo, start=False, stop=False, skip_group_check=True)
                return pe.matmul(o, a_lo, b_hi, start=False, stop=stop, skip_group_check=True)

            def unit(i, slot, k0, banks, transposed, first, last, x_hi, x_lo, opens=True, between=None):
                pe.wait_ge(lo_ready, i + 1)
                for g in range(2):
                    if g and between is not None:
                        between()
                    for k in range(KU):
                        begin, end = first and opens and k == 0, last and k == KU - 1
                        if transposed:
                            for q in range(2):
                                cut = slice((2 * g + q) * P, (2 * g + q + 1) * P)
                                ins = three(bank[banks + g][:, q * T:(q + 1) * T], w_hi[:, slot, k, cut],
                                            w_lo[:, slot, k, cut], x_hi[:, k0 + k], x_lo[:, k0 + k],
                                            begin and q == 0, end)
                        else:
                            cut = slice(g * P, (g + 1) * P)
                            ins = three(bank[banks + g][:], x_hi[:, k0 + k, cut], x_lo[:, k0 + k, cut],
                                        w_hi[:, slot, k], w_lo[:, slot, k], begin, end)
                    if g == 0 and last:
                        ins.then_inc(full[banks], 1)
                ins.then_inc(unit_used, 1)

            def turn(stage, src, version=None):
                for j in range(4):
                    for m in range(MT):
                        if j == 0 and stage in SOURCE:
                            pe.wait_ge(source_ready, MT * SOURCE[stage] + m + 1)
                        if j == 0 and version is not None:
                            pe.wait_ge(cnormed, MT * version + m + 1)
                        for k in (2 * j, 2 * j + 1):
                            ins = pe.transpose(bank[4 + j][:, (k % 2) * T + m * P:(k % 2) * T + (m + 1) * P],
                                               src[:, m, k * P:(k + 1) * P], ident[:])
                    ins.then_inc(full[4 + j], 1)

            def chunk(stage, c, transposed, version, done=None):
                for half in range(2):
                    i = UNITS[stage] + 2 * c + half
                    pe.wait_ge(actlo_ready, KD * version + KU * (half + 1))
                    if half == 0 and done is not None:
                        done(c)
                    unit(i, i % RING, KU * half, 2 * (c % 2), transposed, half == 0, half == 1, act_hi, act_lo)

            pe.wait_ge(consts, 1)
            pe.wait_ge(par_in, 16 * 10)
            pe.transpose(bank[7][:, 0:NPAR], par_rows[:], ident[0:NPAR, 0:NPAR]).then_inc(full[7], 1)
            pe.wait_ge(par_ready, 1)
            turn("turn_mix0", u)
            v = VERSION["turn_mix0"]
            pe.wait_ge(gatelo_ready, 1)
            pe.wait_ge(actlo_ready, KD * (v + 1))

            def gate(o, l, n):
                for k in range(KD):
                    ins = three(o, gate_hi[:, l, k, n], gate_lo[:, l, k, n], act_hi[:, k], act_lo[:, k],
                                k == 0, k == KD - 1)
                return ins

            gate(bank[4][0:HM, 0:T], 0, slice(0, HM))
            gate(bank[4][0:HM, T:2 * T], 0, slice(HM, 2 * HM)).then_inc(full[4], 1)

            def mlstm_scores(hd):
                if hd == 0:
                    pe.wait_ge(rows_ready, 1)
                    for q, r in enumerate((4, 7)):
                        for m in range(MT):
                            at = (MT * q + m) * HM
                            ins = pe.transpose(bank[6][:, at:at + HM], rows[0:HM, r, m * P:(m + 1) * P],
                                               ident[0:HM, 0:HM])
                    ins.then_inc(full[6], 1)
                    pe.wait_ge(conv_silu, 4)
                else:
                    pe.wait_ge(weight_ready, hd)
                for n, (to, t0, t1) in enumerate([(0, 0, T), (T, P, T)]):
                    pe.matmul(bank[4][:, to:to + t1 - t0], select[0:HM, hd], rows[0:HM, 6, t0:t1], start=(n == 0),
                              stop=False, skip_group_check=True)
                    ins = pe.matmul(bank[4][:, to:to + P], ident[:], after_T[:], start=False, stop=True,
                                    skip_group_check=True)
                ins.then_inc(full[4], 1)
                pe.matmul(bank[5][:, 0:T], qkT[:, HM + hd, 0:P], qkT[:, hd], start=True, stop=True)
                pe.matmul(bank[5][:, T:3 * P], qkT[:, HM + hd, P:T], qkT[:, hd, P:T], start=True, stop=True)\
                  .then_inc(full[5], 1)

            def mlstm_values(hd):
                pe.wait_ge(weight_ready, hd + 1)
                if hd == 0:
                    pe.wait_ge(cols_ready, 1)
                    pe.wait_ge(in_done[2], 1)
                    pe.wait_ge(in_done[3], 1)
                if hd == 2:
                    pe.wait_ge(half_ready, MT)
                for m in range(MT):
                    o = bank[6 + m][:, (hd % 2) * (P + 1):(hd % 2 + 1) * (P + 1)]
                    for s in range(m + 1):
                        ins = pe.matmul(o, weight[:, hd % 2, (m + s) * P:(m + s + 1) * P], va[:, s, hd],
                                        start=(s == 0), stop=(s == m))
                    if hd % 2:
                        ins.then_inc(full[6 + m], 1)

            def mlstm_step(n):
                if n == 0:
                    mlstm_scores(0)
                if n == 2:
                    mlstm_scores(1)
                if n in (4, 6):
                    mlstm_values(n // 2 - 2)
                    mlstm_scores(n // 2)
                if n in (9, 10):
                    mlstm_values(n - 7)

            for c, (name, _, transposed) in enumerate(IN0):
                for half in range(2):
                    i = UNITS["in0"] + 2 * c + half
                    if half == 0 and c >= 2:
                        for b in (2 * (c % 2), 2 * (c % 2) + 1):
                            if IN0[c - 2][0] in CONV0:
                                pe.wait_ge(conv_done, CONV0[IN0[c - 2][0]] // 2 + b % 2 + 1)
                            else:
                                done = len([1 for q in range(c % 2, c, 2) if IN0[q][0] not in CONV0])
                                pe.wait_ge(in_done[b], done)
                    step = 4 * (c - MLSTM_AT) + 2 * half
                    mlstm_step(step)
                    unit(i, i % RING, KU * half, 2 * (c % 2), transposed, half == 0, half == 1, act_hi, act_lo,
                         between=lambda: mlstm_step(step + 1))

            def hgrn_level(n):
                level = LEVELS[n]
                if n:
                    pe.wait_ge(scaled_ready, n)
                else:
                    pe.wait_ge(keep_ready, 2)
                    for b in range(4):
                        pe.wait_ge(in_done[b], IN_DONE0[b])
                if n >= 2:
                    pe.wait_ge(selected, MT * (n - 1))
                kk, qq = (kb[:], qb[:]) if n == 0 else (kd[:, n % 2], qd[:, n % 2])
                for tile in range(1 if level == 128 else MT):
                    b = 2 + 2 * (n % 2) + tile
                    to = 1 if level == 128 else tile
                    for hd in range(HM):
                        ins = pe.matmul(bank[b][:, hd * P:(hd + 1) * P], kk[:, hd, tile * P:(tile + 1) * P],
                                        qq[:, hd, to * P:(to + 1) * P], start=True, stop=True)
                    ins.then_inc(full[b], 1)

            pe.wait_ge(y_ready, 2)
            turn("turn_mem", mem_v)
            hgrn_level(0)
            v = VERSION["turn_mem"]
            for n in range(1, len(LEVELS)):
                c, half = (n - 1) // 2, (n - 1) % 2
                if half == 0 and c:
                    pe.wait_ge(kv_done, 2 * c)
                if c == 0:
                    pe.wait_ge(actlo_ready, KD * v + KU * (half + 1))
                i = UNITS["kv"] + n - 1
                unit(i, i % RING, KU * half, 0, c < 2, half == 0, half == 1, act_hi, act_lo)
                if n == 1:
                    pe.wait_ge(actlo_ready, KD * v + KD)
                hgrn_level(n)
            pe.wait_ge(selected, MT * (len(LEVELS) - 1))
            for m in range(MT):
                if m:
                    pe.wait_ge(pairx_ready, 1)
                for hd in range(HM):
                    o, part = bank[6 + m][:, hd * P:(hd + 1) * P], slice(hd * P, (hd + 1) * P)
                    if m:
                        pe.matmul(o, pair_x[:, hd], vb[:, 0, part], start=True, stop=False)
                    ins = pe.matmul(o, pair_w[:, m, hd], vb[:, m, part], start=(m == 0), stop=True)
                ins.then_inc(full[6 + m], 1)
            pe.wait_ge(kv_done, 8)
            turn("turn_y0", u)
            for c in range(2):
                chunk("out0", c, False, VERSION["turn_y0"])

            def cross(l):
                turn(f"turn_x{l}", u)
                for c in range(2):
                    chunk(f"xq{l}", c, True, VERSION[f"turn_x{l}"])
                stage = f"xattn{l}"
                for i in range(HX + 2):
                    if i < HX:
                        if i < 2:
                            pe.wait_ge(xq_done, 4 * (l + 1))
                        else:
                            pe.wait_ge(xexp, HX * l + i - 1)
                        for m in range(MT):
                            for k in range(2):
                                ins = pe.matmul(bank[i % 2][:, m * T:(m + 1) * T],
                                                xqT[:, 2 * i + k, m * P:(m + 1) * P], mem_kT[:, 2 * i + k],
                                                start=(k == 0), stop=(k == 1))
                        ins.then_inc(full[i % 2], 1)
                    if 1 <= i <= HX:
                        hd = i - 1
                        pe.wait_ge(xnorm, HX * l + hd + 1)
                        if hd >= 2:
                            pe.wait_ge(xturned, HX * l + hd - 1)
                        for m in range(MT):
                            for j in range(MT):
                                ins = pe.transpose(bank[2 + hd % 2][:, j * T + m * P:j * T + (m + 1) * P],
                                                   px[:, hd % 2, m, j * P:(j + 1) * P], ident[:])
                        ins.then_inc(full[2 + hd % 2], 1)
                    if i >= 2:
                        hd = i - 2
                        pe.wait_ge(xturned, HX * l + hd + 1)
                        if hd >= 2:
                            pe.wait_ge(actlo_ready, KD * VERSION[stage] + 2 * (hd - 1))
                        for k in range(2):
                            at = XD * hd + P * k
                            for j in range(MT):
                                ins = pe.matmul(bank[4 + hd % 2][:, k * T:(k + 1) * T], mem_v[:, j, at:at + P],
                                                pxT[:, hd % 2, j], start=(j == 0), stop=(j == MT - 1))
                        ins.then_inc(full[4 + hd % 2], 1)
                for c in range(2):
                    chunk(f"xo{l}", c, False, VERSION[stage])

            def mlp(l):
                stage = f"mlp{l}"
                turn(f"turn_m{l}", u)
                pe.wait_ge(actlo_ready, KD * (VERSION[f"turn_m{l}"] + 1))

                def w1(i, slot, j):
                    if not isinstance(j, int) or j:
                        pe.wait_ge(hid_ready, 2 * j + 2 * NJ * l)
                    for half in range(2):
                        unit(i + half, (slot + half) % RING, KU * half, 4, True, half == 0, half == 1, act_hi, act_lo)

                def w2(i, slot, j, buf, first, last):
                    pe.wait_ge(hidlo_ready, 2 * j + (2 * NJ * l + 2))
                    for n in range(2):
                        unit(i + n, (slot + n) % RING, 0, 2 * n, False, first, last, hid_hi[:, buf], hid_lo[:, buf])

                u0 = UNITS[stage]
                w1(u0, u0 % RING, 0)
                w1(u0 + 2, (u0 + 2) % RING, 1)
                w2(u0 + 4, (u0 + 4) % RING, 0, 0, True, False)
                with pe.Fori(0, (NJ - 2) // 2) as it:
                    for n, (which, j, buf) in enumerate(in_order(it)):
                        i, slot = 8 * it + (u0 + 6 + 2 * n), (u0 + 6 + 2 * n) % RING
                        if which == 1:
                            w1(i, slot, j)
                        else:
                            w2(i, slot, j, buf, False, False)
                w2(u0 + 4 * NJ - 2, (u0 + 4 * NJ - 2) % RING, NJ - 1, (NJ - 1) % 2, False, True)

            cross(0)
            mlp(0)

            turn("turn_mix1", u)
            v = VERSION["turn_mix1"]
            pe.wait_ge(actlo_ready, KD * (v + 1))
            gate(bank[4][0:HC, 0:T], 1, slice(0, HC)).then_inc(full[4], 1)

            def in1_free(c):
                for i in range(2):
                    if c >= 2:
                        pe.wait_ge(in_done[2 * (c % 2) + i], IN_DONE0[2 * (c % 2) + i] + c // 2)
            for c in range(8):
                chunk("in1", c, False, v, in1_free)
                if c == 3:
                    pe.wait_ge(rows_ready, 2)
                    turn("turn_q", qc, 0)
                if c == 5:
                    pe.wait_ge(qT_ready, HC)
                    turn("turn_k", kc, 1)

            pe.wait_ge(kT_ready, HC)
            for i in range(HC + 2):
                if i < HC:
                    if i < 2:
                        for b in range(4):
                            pe.wait_ge(in_done[b], IN_DONE0[b] + 4)
                    else:
                        pe.wait_ge(cexp, i - 1)
                    for m in range(MT):
                        w = (m + 1) * P
                        o = bank[i % 2][:, m * P:m * P + w]
                        pe.matmul(o, qcT[:, i, m * P:(m + 1) * P], kcT[:, i, 0:w], start=(m == 0), stop=False,
                                  skip_group_check=True)
                        pe.matmul(o, select[0:HC, i], rows1[0:HC, 4, 0:w], start=False, stop=False,
                                  skip_group_check=True)
                        ins = pe.matmul(bank[i % 2][:, 2 * m * P:(2 * m + 1) * P], ident[:], after[:], start=False,
                                        stop=True, skip_group_check=True)
                    ins.then_inc(full[i % 2], 1)
                if 1 <= i <= HC:
                    hd = i - 1
                    pe.wait_ge(cexp, hd + 1)
                    if hd >= 2:
                        pe.wait_ge(cturned, hd - 1)
                    for n in range(3):
                        ins = pe.transpose(bank[2 + hd % 2][:, n * P:(n + 1) * P], pc[:, hd % 2, n * P:(n + 1) * P],
                                           ident[:])
                    ins.then_inc(full[2 + hd % 2], 1)
                if i >= 2:
                    hd = i - 2
                    pe.wait_ge(cturned, hd + 1)
                    if hd >= 2:
                        pe.wait_ge(oc_done, hd - 1)
                    for m in range(MT):
                        for s in range(m + 1):
                            ins = pe.matmul(bank[4 + hd % 2][:, m * P:(m + 1) * P],
                                            pcT[:, hd % 2, (m + s) * P:(m + s + 1) * P],
                                            vc[:, s, hd * P:(hd + 1) * P], start=(s == 0), stop=(s == m))
                    ins.then_inc(full[4 + hd % 2], 1)
            pe.wait_ge(oc_done, HC)
            turn("turn_y1", u)
            for c in range(2):
                chunk("out1", c, False, VERSION["turn_y1"])
            cross(1)
            mlp(1)


_INS = ["x", "mem", "norm_mix_g", "norm_xattn_g", "norm_mlp_g", "final_norm_g", "ab_w_in", "ab_conv_w",
        "ab_gate_b", "hgrn_lb_logits", "mlstm_norm_g", "hgrn_norm_g", "ab_w_out", "c_w_in", "c_fgate_b",
        "c_qnorm_g", "c_knorm_g", "c_w_out", "mem_norm_g", "mem_w_kv", "xa_w_q", "xa_w_o", "mlp_w1", "mlp_w2"]


def kernel(**inputs):
    import numpy as _np
    import concourse.bacc as _bacc
    from concourse import mybir as _mybir
    from concourse.bass_utils import run_bass_kernel_spmd as _run

    nc = _bacc.Bacc("TRN2", target_bir_lowering=False, num_devices=1)
    arrays, args = {}, []
    for name in _INS:
        a = _np.ascontiguousarray(inputs[name])
        arrays[f"in_{name}_dram"] = a
        args.append(nc.dram_tensor(f"in_{name}_dram", a.shape, _mybir.dt.from_np(a.dtype), kind="ExternalInput").ap())
    args.append(nc.dram_tensor("out_dram", (1, T, D), F32, kind="ExternalOutput").ap())
    trunk(nc, *args)
    r = _run(nc, [arrays], core_ids=[0])
    return r.results[0]["out_dram"]
```

```python
from contextlib import ExitStack

import numpy as np

import concourse.bass as bass
from concourse import mybir

F32 = mybir.dt.float32
F32R = mybir.dt.float32r
U8 = mybir.dt.uint8
ALU = mybir.AluOpType
ACT = mybir.ActivationFunctionType
AX = mybir.AxisListType

P = 128
BANK = 512
T = 256
MT = T // P
D = 1024
KD = D // P
FF = 4 * D
NJ = FF // BANK
HM = 4
HC = 8
HX = 4
XD = D // HX
EPS = 1e-6
NEG = -(2.0 ** 100)
RING = 4
RAW = 4
AHEAD = 3
KU = 4
LEVELS = [0, 64, 32, 16, 8, 4, 2, 1, 128]

PARAMS = [("norm_mix", 16), ("norm_xattn", 16), ("norm_mlp", 16), ("mem_norm", 8), ("mix_out", 8),
          ("conv", 32), ("lb", 8), ("qn", 1), ("kn", 1)]
PROW = {}
_n = 0
for _name, _rows in PARAMS:
    PROW[_name] = _n
    _n += _rows
NPAR = _n

TURN = {4: 1, 5: 1, 6: 1, 7: 1}
STAGES = [
    ("params", {7: 1}), ("turn_mix0", TURN), ("gate0", {4: 1, 5: 1}), ("in0", {0: 4, 2: 4}),
    ("mlstm", {4: 4, 5: 4, 6: 3, 7: 2}), ("turn_mem", TURN), ("kv", {0: 4}),
    ("hgrn", {2: 5, 3: 1, 4: 5, 5: 1}),
    ("turn_y0", {6: 2, 7: 2}), ("out0", {0: 1, 2: 1}),
    ("turn_x0", TURN), ("xq0", {0: 1, 2: 1}), ("xattn0", {4: 2, 5: 2, 6: HX, 7: HX}),
    ("xo0", {0: 1, 2: 1}),
    ("turn_m0", {4: 1, 5: 1, 0: 1, 1: 1}), ("mlp0", {0: 1, 2: 1, 4: NJ - 1, 6: 1}),
    ("turn_mix1", TURN), ("gate1", {4: 1}), ("in1", {0: 4, 2: 4}),
    ("turn_q", TURN), ("turn_k", TURN), ("fox", {4: HC // 2, 5: HC // 2, 6: HC, 7: HC}),
    ("turn_y1", {0: 1, 1: 1, 4: 1, 5: 1}), ("out1", {0: 1, 2: 1}),
    ("turn_x1", TURN), ("xq1", {0: 1, 2: 1}), ("xattn1", {4: 2, 5: 2, 6: HX, 7: HX}),
    ("xo1", {0: 1, 2: 1}),
    ("turn_m1", {4: 1, 5: 1, 0: 1, 1: 1}), ("mlp1", {0: 1, 2: 1, 4: NJ - 1, 6: 1}),
]
FILLED = {}
_at = [0] * 8
for _name, _banks in STAGES:
    FILLED[_name] = list(_at)
    for _b, _k in _banks.items():
        _at[_b] += _k

TURN_BANKS = {"turn_m0": [(4, 0), (5, 0), (0, 0), (1, 0)], "turn_m1": [(4, 0), (5, 0), (0, 0), (1, 0)],
              "turn_y0": [(6, 0), (7, 0), (6, 1), (7, 1)], "turn_y1": [(0, 0), (1, 0), (4, 0), (5, 0)]}


def turn_bank(stage, j):
    return TURN_BANKS[stage][j] if stage in TURN_BANKS else (4 + j, 0)


def crossed(stage, c):
    return c < 2 and stage not in ("in0", "kv")


def unit_order(stage, chunks):
    order = [(c, half) for c in range(chunks) for half in range(2)]
    if crossed(stage, 0):
        order[1], order[2] = order[2], order[1]
    return order


UNITS = {}
_u = 0
for _name, _k in [("in0", 16), ("kv", 8), ("out0", 4), ("xq0", 4), ("xo0", 4), ("mlp0", 4 * NJ),
                  ("in1", 16), ("out1", 4), ("xq1", 4), ("xo1", 4), ("mlp1", 4 * NJ)]:
    UNITS[_name] = _u
    _u += _k
NU = _u

VERSION = {n: i for i, n in enumerate(["turn_mix0", "turn_mem", "turn_y0", "turn_x0", "xattn0", "turn_m0",
                                       "turn_mix1", "turn_y1", "turn_x1", "xattn1", "turn_m1"])}
GAIN = {"turn_mem": PROW["mem_norm"], "turn_mix0": PROW["norm_mix"], "turn_mix1": PROW["norm_mix"] + 8,
        "turn_y0": PROW["mix_out"], "turn_y1": None, "turn_x0": PROW["norm_xattn"],
        "turn_x1": PROW["norm_xattn"] + 8, "turn_m0": PROW["norm_mlp"], "turn_m1": PROW["norm_mlp"] + 8}
NORMS = {n: i for i, n in enumerate(["turn_x0", "turn_m0", "turn_mix1", "turn_x1", "turn_m1", "final"])}
ROOTS = {n: i for i, n in enumerate(["turn_mix0", "turn_mem", "mlstm", "hgrn", "turn_x0", "turn_m0", "turn_mix1",
                                     "q", "k", "turn_x1", "turn_m1", "final"])}
SUMS = {n: i for i, n in enumerate(["out0", "xo0", "mlp0", "out1", "xo1", "mlp1"])}
SUM_BEFORE = {"turn_mix0": 0, "turn_x0": 1, "turn_m0": 2, "turn_mix1": 3, "turn_x1": 4, "turn_m1": 5, "final": 6}

IN0 = [("oa", 1536, False), ("qa", 0, True), ("ka", 512, True), ("va", 1024, False),
       ("fb", 2568, True), ("qb", 2056, True), ("ib", 3080, False), ("gb", 3592, False)]
MLSTM_AT = 4
CONV0 = {"qa": 0, "ka": HM}
IN1 = [("q", 0), ("q", 1), ("k", 0), ("k", 1), ("v", 0), ("g", 0), ("v", 1), ("g", 1)]
IN1_COLUMNS = ["qkvg".index(name) * D + n * BANK for name, n in IN1]
FOX_AT = 10
IN_DONE0 = [len([1 for q in range(b // 2, 8, 2) if IN0[q][0] not in CONV0]) for b in range(4)]
GATE0, GATE1 = 2048, 4096


def trunk(nc, x, mem, norm_mix_g, norm_xattn_g, norm_mlp_g, final_norm_g, ab_w_in, ab_conv_w, ab_gate_b,
          hgrn_lb_logits, mlstm_norm_g, hgrn_norm_g, ab_w_out, c_w_in, c_fgate_b, c_qnorm_g, c_knorm_g,
          c_w_out, mem_norm_g, mem_w_kv, xa_w_q, xa_w_o, mlp_w1, mlp_w2, out):
    ctx = ExitStack()
    with ctx:
        place = [nc.sbuf_base + (-nc.sbuf_base) % 64]

        def sb(name, shape, dt=F32, at=None):
            size = int(np.prod(shape[1:])) * (1 if dt == U8 else 4)
            size += (-size) % 64
            where = place[0] if at is None else at[0]
            t = nc.alloc_sbuf_tensor_at(name, shape, dt, offset=where)
            if at is None:
                place[0] += size
            else:
                at[0] += size
            return t

        def sem(name):
            return ctx.enter_context(nc.semaphore(name))

        bank = [ctx.enter_context(nc.psum_tensor(f"bank{b}", [P, BANK], F32)) for b in range(8)]

        h = sb("h", [P, MT, D])
        u = sb("u", [P, MT, D])
        act_hi = sb("act_hi", [P, KD, T], F32R)
        act_lo = sb("act_lo", [P, KD, T], F32R)
        mem_kT = sb("mem_kT", [P, KD, T])
        mem_v = sb("mem_v", [P, MT, D])
        raw = sb("raw", [P, RAW, KU, BANK])
        w_hi = sb("w_hi", [P, RING, KU, BANK], F32R)
        w_lo = sb("w_lo", [P, RING, KU, BANK], F32R)
        ident = sb("ident", [P, P])
        ident_r = sb("ident_r", [P, P], F32R)
        after_T = sb("after_T", [P, P], F32R)
        after = sb("after", [P, P], F32R)
        select = sb("select", [HC, HC, P], F32R)
        ones = sb("ones", [P, HC])
        pairs = sb("pairs", [P, len(LEVELS) - 1, P], U8)
        par = sb("par", [P, NPAR])
        gate_w = sb("gate_w", [P, 2, KD, 8])
        gate_hi = sb("gate_hi", [P, 2, KD, 8], F32R)
        gate_lo = sb("gate_lo", [P, 2, KD, 8], F32R)
        bias_i = sb("bias_i", [HM, 1])
        bias_f = sb("bias_f", [HM, 1])
        bias_c = sb("bias_c", [HC, 1])
        lb = sb("lb", [P, 6, HM])
        st = sb("st", [P, 9, 16])
        rs = sb("rs", [P, 2, MT])
        diag = sb("diag", [P, MT, P])
        cols = sb("cols", [P, 2, MT * HM])
        q_gain = sb("q_gain", [P, 1])
        xs = sb("xs", [P, 4, 2 * MT])

        arena = place[0]
        a = [arena]
        dec = sb("dec", [P, 2, HM, T], at=a)
        qkT = mem_kT
        after_va = [a[0]]
        va = sb("va", [P, MT, HM, P + 1], at=a)
        pair_x = sb("pair_x", [P, HM, P], at=after_va)
        after_oa = [a[0]]
        oa = sb("oa", [P, MT, BANK], at=a)
        gb = sb("gb", [P, MT, BANK], at=after_oa)
        vb = sb("vb", [P, MT, BANK], at=a)
        qb = sb("qb", [P, HM, T], at=a)
        kb = sb("kb", [P, HM, T], at=a)
        cum = sb("cum", [P, HM, T], at=a)
        pair_w = sb("pair_w", [P, MT, HM, P], at=a)
        mix_end = a[0]
        qd = sb("qd", [P, 2, HM, T], at=a)
        kd = sb("kd", [P, 2, HM, T], at=a)
        a2 = [mix_end]
        decay = sb("decay", [P, 2, 3 * P], at=a2)
        weight = sb("weight", [P, 2, 3 * P], at=a2)
        rows = sb("rows", [HC, 7, T], at=a2)
        max_hi = sb("max_hi", [HC, 3 * P], F32R, at=a2)
        max_lo = sb("max_lo", [HC, 3 * P], F32R, at=a2)
        assert a[0] <= nc.sbuf_usable_end and a2[0] <= nc.sbuf_usable_end, (a[0], a2[0], nc.sbuf_usable_end)
        a = [arena]
        qc = sb("qc", [P, MT, D], at=a)
        kc = sb("kc", [P, MT, D], at=a)
        vc, gc = qc, kc
        qcT = sb("qcT", [P, HC, T], at=a)
        kcT = sb("kcT", [P, HC, T], at=a)
        pc = sb("pc", [P, 2, 3 * P], at=a)
        pcT = sb("pcT", [P, 2, 3 * P], at=a)
        rows1 = sb("rows1", [HC, 6, T], at=a)
        csum = sb("csum", [P, 4, 2 * HC], at=a)
        forget_hi = sb("forget_hi", [HC, 3 * P], F32R, at=a)
        forget_lo = sb("forget_lo", [HC, 3 * P], F32R, at=a)
        a = [arena]
        xqT = sb("xqT", [P, KD, T], at=a)
        px = sb("px", [P, 2, MT, T], at=a)
        pxT = sb("pxT", [P, 2, MT, T], at=a)
        a = [arena]
        hid_hi = sb("hid_hi", [P, 2, KU, T], F32R, at=a)
        hid_lo = sb("hid_lo", [P, 2, KU, T], F32R, at=a)
        relu = sb("relu", [P, 2, BANK], at=a)
        hid = sb("hid", [P, 2, BANK], at=a)
        final_g = sb("final_g", [P, D], at=a)
        junk = sb("junk", [P, MT, D], at=a)
        a = [arena]
        par_rows = sb("par_rows", [NPAR, P], at=a)
        pairs_f = sb("pairs_f", [P, len(LEVELS) - 1, P], at=a)
        after_f = sb("after_f", [P, P], at=a)
        after_T_f = sb("after_T_f", [P, P], at=a)
        select_f = sb("select_f", [HC, HC, P], at=a)

        x_in = [sem(f"x_in{m}") for m in range(MT)]
        mem_in, par_in, small_in, gain_in, out_done = map(
            sem, ["mem_in", "par_in", "small_in", "gain_in", "out_done"])
        gatehi_ready, gatelo_ready = sem("gatehi_ready"), sem("gatelo_ready")
        raw_in = [sem(f"raw_in{i}") for i in range(RAW)]
        hi_ready, lo_ready, unit_used = sem("hi_ready"), sem("lo_ready"), sem("unit_used")
        full = [sem(f"bank_full{b}") for b in range(8)]
        consts, par_ready, lb_in, lb_exp = sem("consts"), sem("par_ready"), sem("lb_in"), sem("lb_exp")
        square_sum, root_in, root_seed = sem("square_sum"), sem("root_in"), sem("root_seed")
        diag_ready, memory_ready, y_normed, y_scaled = map(sem, ["diag_ready", "memory_ready", "y_normed", "y_scaled"])
        first_squares, norm_ready, gate_ready = sem("first_squares"), sem("norm_ready"), sem("gate_ready")
        acthi_ready, actlo_ready = sem("acthi_ready"), sem("actlo_ready")
        sum_done, kv_done, xq_done = sem("sum_done"), sem("kv_done"), sem("xq_done")
        dve_step, act_step, pool_step = sem("dve_step"), sem("act_step"), sem("pool_step")
        relu_ready, hid_ready, hidhi_ready, hidlo_ready = map(
            sem, ["relu_ready", "hid_ready", "hidhi_ready", "hidlo_ready"])
        in_done = [sem(f"in_done{b}") for b in range(4)]
        tap_ready, conv_done, conv_silu, sigmoid_ready, forget_ready, keep_ready, log_forget = map(
            sem, ["tap_ready", "conv_done", "conv_silu", "sigmoid_ready", "forget_ready", "keep_ready", "log_forget"])
        log_out, rows_ready, cols_ready = sem("log_out"), sem("rows_ready"), sem("cols_ready")
        decay_ready, weight_ready, half_ready, y_ready, y_squared = map(
            sem, ["decay_ready", "weight_ready", "half_ready", "y_ready", "y_squared"])
        dist_ready, dec_ready, scaled_ready, selected, pairx_ready = map(
            sem, ["dist_ready", "dec_ready", "scaled_ready", "selected", "pairx_ready"])
        xmax, xexp, xnorm, xturned = map(sem, ["xmax", "xexp", "xnorm", "xturned"])
        squares_used, cnormed, qT_ready, kT_ready = map(sem, ["squares_used", "cnormed", "qT_ready", "kT_ready"])
        cmax, cexp, cturned, oc_done = map(sem, ["cmax", "cexp", "cturned", "oc_done"])
        fin_ready = [sem(f"fin_ready{c}_{m}") for c in range(2) for m in range(MT)]

        def wait_full(eng, stage, b, k=0):
            eng.wait_ge(full[b], FILLED[stage][b] + k + 1)

        def f(ap):
            return ap.bitcast(F32)

        def heads(ap, n=HM):
            return ap.rearrange("p (h d) -> p h d", h=n)

        def wait_chunk(eng, stage, c, i):
            if i == 0:
                wait_full(eng, stage, 2 * (c % 2), c // 2)
            else:
                eng.wait_ge(unit_used, UNITS[stage] + (2 + c if crossed(stage, c) else 2 * c + 1) + 1)

        def flat(ap):
            return ap.rearrange("p a b -> p (a b)")

        def flat3(ap):
            return ap.rearrange("p a b c -> p (a b c)")

        def spread(ap, n):
            return ap.unsqueeze(2).to_broadcast([P, ap.shape[1], n])

        def mlp_walk(eng, l, split, ahead, hidden):
            u0 = UNITS[f"mlp{l}"]

            def chunk(i, slot, which, j, buf):
                split(i + AHEAD, (slot + AHEAD) % RING)
                split(i + 1 + AHEAD, (slot + 1 + AHEAD) % RING)
                if which == 1:
                    hidden(j, buf, i + 1 if isinstance(j, int) and j == 0 else i)

            for n, (which, j, buf) in enumerate([(1, 0, 0), (1, 1, 1), (2, 0, 0)]):
                chunk(u0 + 2 * n, u0 + 2 * n, which, j, buf)
            turns = (NJ - 2) // 2 - l
            with eng.Fori(0, turns) as it:
                for n, (which, j, buf) in enumerate(in_order(it)):
                    chunk(8 * it + (u0 + 6 + 2 * n), u0 + 6 + 2 * n, which, j, buf)
            if l == 1:
                for n, (which, j, buf) in enumerate(in_order(turns)):
                    i = u0 + 6 + 8 * turns + 2 * n
                    ahead(i)
                    ahead(i + 1)
                    if which == 1:
                        hidden(j, buf, i)

        def last_of_half(level):
            v = cum[:].rearrange("p h (b two l) -> p (h b) two l", two=2, l=level)
            return v, v[:, :, 0, level - 1:level].to_broadcast([P, HM * T // (2 * level), level])

        def halves(ap, level):
            return ap.rearrange("p h (b two l) -> p (h b) two l", two=2, l=level)

        def second_halves(ap, level):
            if len(ap.shape) == 2:
                return ap.rearrange("p (b two l) -> p b two l", two=2, l=level)[:, :, 1, :]
            return ap.rearrange("p h (b two l) -> p h b two l", two=2, l=level)[:, :, :, 1, :]

        def hidden_bank(j):
            return 6 if isinstance(j, int) and j == 1 else 4

        def in_order(it, j0=2):
            j = j0 + 2 * it
            return [(1, j, 0), (2, j - 1, 1), (1, j + 1, 1), (2, j, 0)]

        def load_rows(eng, name, src, skip=0):
            eng.dma_start(par_rows[PROW[name] + skip:PROW[name] + skip + src.shape[0], :], src).then_inc(par_in, 16)

        block = ctx.enter_context(nc.Block())

        @block.sync
        def _(sp):
            def load(i, slot, src):
                if not (isinstance(i, int) and i < RAW):
                    sp.wait_ge(lo_ready, i - RAW + 1)
                sp.dma_start(raw[:, slot], src).then_inc(raw_in[slot], 16)

            def load_square(stage, w, columns, skip=0, stop=None):
                v = w.rearrange("(k p) n -> p k n", p=P)
                for n, (c, half) in list(enumerate(unit_order(stage, len(columns))))[skip:stop]:
                    load(UNITS[stage] + n, (UNITS[stage] + n) % RAW, v[:, KU * half:KU * (half + 1), columns[c]:columns[c] + BANK])

            def load_mlp(l):
                w1 = mlp_w1[l].rearrange("(k p) n -> p k n", p=P)
                w2 = mlp_w2[l].rearrange("(k p) n -> p k n", p=P)
                u0 = UNITS[f"mlp{l}"]

                def unit(i, slot, which, j, half):
                    if which == 1:
                        src = w1[:, KU * half:KU * (half + 1), bass.ds(BANK * j, BANK)]
                    else:
                        src = w2[:, bass.ds(KU * j, KU), BANK * half:BANK * (half + 1)]
                    load(i, slot % RAW, src)

                start = [(1, 0, 0), (1, 1, 0), (1, 0, 1), (1, 1, 1), (2, 0, 0), (2, 0, 1)]
                for n, (which, j, half) in enumerate(start):
                    unit(u0 + n, u0 + n, which, j, half)
                with sp.Fori(0, (NJ - 2) // 2) as it:
                    for n, (which, j, _) in enumerate(in_order(it)):
                        for half in range(2):
                            i = u0 + 6 + 2 * n + half
                            unit(8 * it + i, i, which, j, half)
                for half in range(2):
                    i = u0 + 4 * NJ - 2 + half
                    unit(i, i, 2, NJ - 1, half)

            for m in range(MT):
                sp.dma_start(h[:, m], x[0, m * P:(m + 1) * P, :]).then_inc(x_in[m], 16)
            load_square("in0", ab_w_in[0], [n for _, n, _ in IN0], 0, 1)
            load_rows(sp, "conv", ab_conv_w[0].rearrange("j (k p) -> (j k) p", p=P))
            load_rows(sp, "lb", hgrn_lb_logits.rearrange("l (k p) -> (l k) p", p=P))
            load_rows(sp, "qn", c_qnorm_g)
            load_rows(sp, "kn", c_knorm_g)
            load_square("in0", ab_w_in[0], [n for _, n, _ in IN0], 1, 2)
            sp.dma_start(gate_w[:, 0], ab_w_in[0].rearrange("(k p) n -> p k n", p=P)[:, :, GATE0:GATE0 + 8])\
              .then_inc(small_in, 16)
            sp.dma_start(gate_w[:, 1], c_w_in[0].rearrange("(k p) n -> p k n", p=P)[:, :, GATE1:GATE1 + 8])\
              .then_inc(small_in, 16)
            sp.dma_start(bias_i[:], ab_gate_b[0, 0:HM].rearrange("(p a) -> p a", a=1)).then_inc(small_in, 16)
            sp.dma_start(bias_f[:], ab_gate_b[0, HM:2 * HM].rearrange("(p a) -> p a", a=1)).then_inc(small_in, 16)
            sp.dma_start(bias_c[:], c_fgate_b[0].rearrange("(p a) -> p a", a=1)).then_inc(small_in, 16)
            sp.dma_start(mem_v[:], mem[0].rearrange("(m p) d -> p m d", p=P)).then_inc(mem_in, 16)
            load_square("in0", ab_w_in[0], [n for _, n, _ in IN0], 2)
            load_square("kv", mem_w_kv, range(0, 2 * D, BANK))
            load_square("out0", ab_w_out[0], [0, BANK])
            load_square("xq0", xa_w_q[0], [0, BANK])
            load_square("xo0", xa_w_o[0], [0, BANK])
            load_mlp(0)
            load_square("in1", c_w_in[0], IN1_COLUMNS)
            load_square("out1", c_w_out[0], [0, BANK])
            load_square("xq1", xa_w_q[1], [0, BANK])
            load_square("xo1", xa_w_o[1], [0, BANK])
            load_mlp(1)
            sp.wait_ge(sum_done, 4 * SUM_BEFORE["turn_m1"])
            sp.dma_start(final_g[:], final_norm_g.rearrange("(a d) -> a d", a=1).to_broadcast([P, D]))\
              .then_inc(gain_in, 16)
            for m in range(MT):
                for c in range(2):
                    part = slice(c * BANK, (c + 1) * BANK)
                    sp.wait_ge(fin_ready[MT * c + m], 1)
                    sp.dma_start(out[0, m * P:(m + 1) * P, part], u[:, m, part]).then_inc(out_done, 16)
            sp.wait_ge(out_done, 16 * 2 * MT)

        @block.gpsimd
        def _(pool):
            step = [0]

            def then(ins):
                step[0] += 1
                ins.then_inc(pool_step, 1)
                pool.wait_ge(pool_step, step[0])

            pool.memset(ident[:], 0.0).then_inc(pool_step, 1)
            pool.memset(after_f[:], 0.0).then_inc(pool_step, 1)
            pool.memset(after_T_f[:], 0.0).then_inc(pool_step, 1)
            pool.memset(select_f[:], 0.0).then_inc(pool_step, 1)
            pool.memset(ones[:], 1.0).then_inc(pool_step, 1)
            step[0] = 5
            pool.wait_ge(pool_step, 5)
            pool.affine_select(out=ident[:], in_=ident[:], pattern=[[-1, P]], compare_op=ALU.not_equal,
                               fill=1.0, base=0, channel_multiplier=1).then_inc(consts, 1)
            then(pool.affine_select(out=after_T_f[:], in_=after_T_f[:], pattern=[[1, P]], compare_op=ALU.is_ge,
                                    fill=NEG, base=0, channel_multiplier=-1))
            then(pool.affine_select(out=after_f[:], in_=after_f[:], pattern=[[-1, P]], compare_op=ALU.is_ge,
                                    fill=NEG, base=0, channel_multiplier=1))
            then(pool.affine_select(out=select_f[:], in_=select_f[:], pattern=[[-1, HC], [0, P]],
                                    compare_op=ALU.not_equal, fill=1.0, base=0, channel_multiplier=1))
            pool.wait_ge(consts, 1)
            for to, of in ((ident_r, ident), (after_T, after_T_f), (after, after_f)):
                then(pool.tensor_copy(to[:], of[:]))
            then(pool.tensor_copy(flat(select[:]), flat(select_f[:])))
            for n, level in enumerate(LEVELS[:-1]):
                lv = pairs_f[:, n]
                then(pool.memset(lv, 0.0 if level == 0 else 1.0))
                if level == 0:
                    then(pool.affine_select(out=lv, in_=lv, pattern=[[-1, P]], compare_op=ALU.not_equal, fill=1.0,
                                            base=0, channel_multiplier=1))
                    continue
                nb = P // (2 * level)
                v = lv.rearrange("p (b two l) -> p b two l", two=2, l=level)
                then(pool.memset(v[:, :, 0, :], 0.0))
                second = v[:, :, 1, :]
                then(pool.affine_select(out=second, in_=second, pattern=[[-2 * level, nb], [0, level]],
                                        compare_op=ALU.is_ge, fill=0.0, base=0, channel_multiplier=1))
                then(pool.affine_select(out=second, in_=second, pattern=[[2 * level, nb], [0, level]],
                                        compare_op=ALU.is_ge, fill=0.0, base=level - 1, channel_multiplier=-1))
            then(pool.tensor_copy(pairs[:], pairs_f[:]))
            pool.memset(pair_w[:], 0.0).then_inc(consts, 2)
            pool.memset(va[:, :, :, P:P + 1], 1.0).then_inc(consts, 1)

        @block.scalar
        def _(act):
            step = [0]

            def then(ins):
                step[0] += 1
                ins.then_inc(act_step, 1)
                act.wait_ge(act_step, step[0])

            def split(i, slot):
                act.wait_ge(raw_in[slot % RAW], (i - slot % RAW) * (16 // RAW) + 16)
                if not (isinstance(i, int) and i < RING):
                    act.wait_ge(unit_used, i - RING + 1)
                act.activation(flat(w_hi[:, slot]), flat(raw[:, slot % RAW]), ACT.Copy).then_inc(hi_ready, 1)

            def ahead(i):
                if i + AHEAD < NU:
                    split(i + AHEAD, (i + AHEAD) % RING)

            def root(name, w):
                act.wait_ge(root_in, ROOTS[name] + 1)
                then(act.activation(st[:, 1, 0:w], st[:, 0, 0:w], ACT.Ln))
                act.activation(st[:, 2, 0:w], st[:, 1, 0:w], ACT.Exp, scale=-0.5).then_inc(root_seed, 1)

            def norm_first(stage, src, junk):
                act.activation(junk[:, 0], src[:, 0], ACT.Square, accum_out=st[:, 4, 0:1]).then_inc(first_squares, 1)
                root(stage, MT)

            def squares(stage, c, junk=u):
                for m in range(MT):
                    act.wait_ge(sum_done, 4 * (SUM_BEFORE[stage] - 1) + 2 * c + m + 1)
                    part = slice(c * BANK, (c + 1) * BANK)
                    act.activation(junk[:, m, part], h[:, m, part], ACT.Square,
                                   accum_out=st[:, 4, MT * c + m:MT * c + m + 1]).then_inc(square_sum, 1)

            def turn(stage, half):
                g = GAIN[stage]
                for k in range(KU * half, KU * (half + 1)):
                    b, fill = turn_bank(stage, k // 2)
                    if k % 2 == 0:
                        wait_full(act, stage, b, fill)
                    act.activation(act_hi[:, k], bank[b][:, (k % 2) * T:(k % 2 + 1) * T], ACT.Copy,
                                   scale=1.0 if g is None else par[:, g + k:g + k + 1]).then_inc(acthi_ready, 1)

            def onto_h(last, stage):
                squares(stage, 0)
                turn(stage, 0)
                ahead(last)
                squares(stage, 1)
                turn(stage, 1)
                root(stage, MT)

            def exp_and_ln():
                act.preload_act_table_set("natural_log_exp_and_others")

            exp_and_ln()
            load_rows(act, "norm_mix", norm_mix_g.rearrange("l (k p) -> (l k) p", p=P))
            load_rows(act, "norm_xattn", norm_xattn_g.rearrange("l (k p) -> (l k) p", p=P))
            load_rows(act, "norm_mlp", norm_mlp_g.rearrange("l (k p) -> (l k) p", p=P))
            load_rows(act, "mem_norm", mem_norm_g.rearrange("(k p) -> k p", p=P))
            load_rows(act, "mix_out", mlstm_norm_g[0].rearrange("(k p) -> k p", p=P))
            load_rows(act, "mix_out", hgrn_norm_g[0].rearrange("(k p) -> k p", p=P), HM)

            act.wait_ge(x_in[0], 16)
            norm_first("turn_mix0", h, u)
            split(0, 0)
            act.wait_ge(par_ready, 1)
            turn("turn_mix0", 0)
            turn("turn_mix0", 1)
            split(1, 1)
            act.wait_ge(lb_in, 1)
            act.activation(lb[:, 3:5], lb[:, 3:5], ACT.Exp).then_inc(lb_exp, 1)
            act.wait_ge(small_in, 16 * 5)
            act.activation(flat3(gate_hi[:]), flat3(gate_w[:]), ACT.Copy).then_inc(gatehi_ready, 1)
            split(2, 2)

            act.wait_ge(consts, 4)

            def log_gate(r, n, bias, zf):
                then(act.activation(r[0:n, 0], zf, ACT.Abs, bias=bias[:]))
                then(act.activation(r[0:n, 0], r[0:n, 0], ACT.Exp, scale=-1.0))
                act.activation(r[0:n, 0], r[0:n, 0], ACT.Ln, bias=1.0).then_inc(log_out, 1)

            ahead(UNITS["in0"])
            ahead(UNITS["in0"] + 1)
            wait_full(act, "gate0", 5)
            log_gate(rows, HM, bias_f, bank[5][0:HM, 0:T])

            def mlstm_decay(hd):
                wait_full(act, "mlstm", 4, hd)
                if hd >= 2:
                    act.wait_ge(weight_ready, hd - 1)
                act.activation(decay[:, hd % 2, 0:T], bank[4][:, 0:T], ACT.Exp, bias=cols[:, 0, hd:hd + 1])
                act.activation(decay[:, hd % 2, T:3 * P], bank[4][:, T:3 * P], ACT.Exp,
                               bias=cols[:, 0, HM + hd:HM + hd + 1]).then_inc(decay_ready, 1)

            def hgrn_decay(n):
                act.wait_ge(dist_ready, n)
                act.activation(flat(dec[:, n % 2]), flat(dec[:, n % 2]), ACT.Exp).then_inc(dec_ready, 1)

            def in0(c):
                name = IN0[c][0]
                for i in range(2):
                    b = 2 * (c % 2) + i
                    wait_chunk(act, "in0", c, i)
                    both = slice(2 * i, 2 * i + 2)
                    if name == "va":
                        act.activation(va[:, i, :, 0:P], heads(bank[b][:]), ACT.Copy).then_inc(in_done[b], 1)
                    elif name in CONV0:
                        for k in range(CONV0[name] + 2 * i, CONV0[name] + 2 * i + 2):
                            w = PROW["conv"] + 3 * KD + k
                            act.activation(qkT[:, k], bank[b][:, (k % 2) * T:(k % 2 + 1) * T], ACT.Copy,
                                           scale=par[:, w:w + 1]).then_inc(tap_ready, 1)
                    elif name == "fb":
                        act.activation(flat(dec[:, 0, both]), bank[b][:], ACT.Sigmoid).then_inc(sigmoid_ready, 1)
                        act.activation(flat(kb[:, both]), bank[b][:], ACT.Sigmoid, scale=-1.0).then_inc(in_done[b], 1)
                    elif name == "oa":
                        act.activation(oa[:, i], bank[b][:], ACT.Sigmoid).then_inc(in_done[b], 1)
                    else:
                        dst = {"qb": flat(qb[:, both]), "ib": vb[:, i], "gb": gb[:, i]}[name]
                        act.activation(dst, bank[b][:], ACT.Silu).then_inc(in_done[b], 1)
                if name in CONV0:
                    for i in range(2):
                        k = CONV0[name] + 2 * i
                        act.wait_ge(conv_done, k // 2 + 1)
                        act.activation(flat(qkT[:, k:k + 2]), flat(qkT[:, k:k + 2]), ACT.Silu).then_inc(conv_silu, 1)

            for c in range(8):
                if c == MLSTM_AT:
                    wait_full(act, "mlstm", 6)
                    exp_and_ln()
                    act.activation(cols[:, 1], bank[6][:, MT * HM:2 * MT * HM], ACT.Exp)
                    act.activation(cols[:, 0], bank[6][:, 0:MT * HM], ACT.Copy).then_inc(cols_ready, 1)
                    act.wait_ge(cols_ready, 1)
                if MLSTM_AT <= c < MLSTM_AT + 2:
                    if c > MLSTM_AT:
                        exp_and_ln()
                    mlstm_decay(2 * (c - MLSTM_AT))
                if c:
                    ahead(UNITS["in0"] + 2 * c)
                if MLSTM_AT <= c < MLSTM_AT + 2:
                    mlstm_decay(2 * (c - MLSTM_AT) + 1)
                if c == MLSTM_AT:
                    act.wait_ge(mem_in, 16)
                    norm_first("turn_mem", mem_v, u)
                if c:
                    ahead(UNITS["in0"] + 2 * c + 1)
                if c == MLSTM_AT + 1:
                    act.wait_ge(forget_ready, 2)
                    act.activation(flat(dec[:, 1]), flat(dec[:, 0]), ACT.Ln).then_inc(log_forget, 1)
                if c == 7:
                    act.wait_ge(unit_used, UNITS["in0"] + 15)
                    turn("turn_mem", 0)
                in0(c)
            act.wait_ge(unit_used, UNITS["in0"] + 16)
            turn("turn_mem", 1)
            exp_and_ln()
            hgrn_decay(1)

            for m in range(MT):
                act.wait_ge(y_ready, m + 1)
                act.activation(u[:, m, BANK:2 * BANK], u[:, m, 0:BANK], ACT.Square).then_inc(y_squared, 1)

            for n in range(1, len(LEVELS)):
                if n + 1 < len(LEVELS):
                    hgrn_decay(n + 1)
                unit = n - 1
                if unit == 7:
                    turn("turn_y0", 0)
                if unit % 2:
                    c = unit // 2
                    for i in range(2):
                        if i == 0:
                            wait_full(act, "kv", 0, c)
                        else:
                            act.wait_ge(unit_used, UNITS["kv"] + 2 * c + 2)
                        if c < 2:
                            dst = flat(mem_kT[:, 4 * c + 2 * i:4 * c + 2 * i + 2])
                        else:
                            dst = mem_v[:, i, (c - 2) * BANK:(c - 1) * BANK]
                        act.activation(dst, bank[i][:], ACT.Copy).then_inc(kv_done, 1)
                ahead(UNITS["kv"] + unit)
                if n == 2:
                    root("mlstm", MT * HM)
            wait_full(act, "hgrn", 2, 4)
            act.activation(flat(pair_x[:]), bank[2][:], ACT.Copy).then_inc(pairx_ready, 1)
            for m in range(MT):
                wait_full(act, "hgrn", 4 + m, 0 if m else 4)
                act.activation(u[:, m, BANK:2 * BANK], bank[4 + m][:], ACT.Square).then_inc(y_squared, 1)
                if m == 0:
                    ahead(UNITS["out0"])
            root("hgrn", MT * HM)
            turn("turn_y0", 1)
            ahead(UNITS["out0"] + 1)
            ahead(UNITS["out0"] + 2)
            onto_h(UNITS["out0"] + 3, "turn_x0")

            def cross(l):
                uq, uo = UNITS[f"xq{l}"], UNITS[f"xo{l}"]
                stage = f"xattn{l}"

                def xq(c):
                    for i in range(2):
                        b = 2 * c + i
                        wait_chunk(act, f"xq{l}", c, i)
                        act.activation(flat(xqT[:, 2 * b:2 * b + 2]), bank[b][:], ACT.Copy, scale=XD ** -0.5)\
                           .then_inc(xq_done, 1)

                def weights(i):
                    act.wait_ge(xmax, HX * l + i + 1)
                    if i >= 2:
                        wait_full(act, stage, 6, i - 2)
                    for m in range(MT):
                        c = 2 * (i % 2) + m
                        ins = act.activation(px[:, i % 2, m], bank[4 + i % 2][:, m * T:(m + 1) * T], ACT.Exp,
                                             bias=xs[:, 1, c:c + 1], scale=rs[:, 0, m:m + 1],
                                             accum_out=xs[:, 2, c:c + 1])
                    ins.then_inc(xexp, 1)

                def turned(i):
                    wait_full(act, stage, 6, i)
                    if i >= 2:
                        wait_full(act, stage, 7, i - 2)
                    act.activation(flat(pxT[:, i % 2]), bank[6][:], ACT.Copy).then_inc(xturned, 1)

                def output(i):
                    wait_full(act, stage, 7, i)
                    act.activation(flat(act_hi[:, 2 * i:2 * i + 2]), bank[7][:], ACT.Copy).then_inc(acthi_ready, 2)

                act.wait_ge(norm_ready, NORMS[f"turn_x{l}"] + 1)
                for n in range(3):
                    ahead(uq + n)
                xq(0)
                ahead(uq + 3)
                weights(0)
                xq(1)
                weights(1)
                turned(0)
                weights(2)
                output(0)
                turned(1)
                weights(3)
                output(1)
                turned(2)
                ahead(uo)
                output(2)
                turned(3)
                ahead(uo + 1)
                output(3)
                ahead(uo + 2)
                onto_h(uo + 3, f"turn_m{l}")

            def mlp(l):
                stage = f"mlp{l}"

                def hidden(j, buf, unit):
                    b = hidden_bank(j)
                    for i in range(2):
                        if i:
                            act.wait_ge(unit_used, unit + 2)
                        elif b == 6:
                            wait_full(act, stage, 6)
                        else:
                            wait_full(act, stage, 4, j - (0 if isinstance(j, int) and j == 0 else 1))
                        act.activation(relu[:, i], bank[b + i][:], ACT.Relu).then_inc(relu_ready, 1)
                    for i in range(2):
                        act.wait_ge(hid_ready, 2 * j + (2 * NJ * l + i + 1))
                        act.activation(flat(hid_hi[:, buf, 2 * i:2 * i + 2]), hid[:, i], ACT.Copy)\
                           .then_inc(hidhi_ready, 1)
                mlp_walk(act, l, split, ahead, hidden)

            cross(0)
            mlp(0)

            ahead(UNITS["mlp0"] + 4 * NJ - 2)
            onto_h(UNITS["mlp0"] + 4 * NJ - 1, "turn_mix1")
            act.wait_ge(norm_ready, NORMS["turn_mix1"] + 1)
            ahead(UNITS["in1"])
            ahead(UNITS["in1"] + 1)

            def in1(c):
                name, n = IN1[c]
                for m in range(2):
                    b = 2 * (c % 2) + m
                    wait_chunk(act, "in1", c, m)
                    part, scale = slice(n * BANK, (n + 1) * BANK), rs[:, 0, m:m + 1]
                    if name in "qk":
                        act.activation((qc if name == "q" else kc)[:, m, part], bank[b][:], ACT.Copy, scale=scale)
                        if name == "k":
                            act.wait_ge(squares_used, 2 * n + m + 1)
                        act.activation(u[:, m, part], bank[b][:], ACT.Square, scale=scale).then_inc(in_done[b], 1)
                    elif name == "v":
                        act.activation(vc[:, m, part], bank[b][:], ACT.Copy, scale=scale).then_inc(in_done[b], 1)
                    else:
                        act.activation(gc[:, m, part], bank[b][:], ACT.Sigmoid, scale=scale).then_inc(in_done[b], 1)

            def fox_weights(i):
                act.wait_ge(cmax, i + 1)
                if i >= 2:
                    wait_full(act, "fox", 6, i - 2)
                for m in range(MT):
                    part = slice(m * P, (1 + 2 * m) * P)
                    ins = act.activation(pc[:, i % 2, part], bank[4 + i % 2][:, part], ACT.Exp,
                                         bias=csum[:, 1, 2 * i + m:2 * i + m + 1],
                                         accum_out=csum[:, 2, 2 * i + m:2 * i + m + 1])
                ins.then_inc(cexp, 1)

            def fox_turned(i):
                wait_full(act, "fox", 6, i)
                if i >= 2:
                    wait_full(act, "fox", 7, i - 2)
                act.activation(pcT[:, i % 2], bank[6][:, 0:3 * P], ACT.Copy).then_inc(cturned, 1)

            def fox_step(i):
                fox_turned(i)
                if i + 2 < HC:
                    fox_weights(i + 2)

            for n in range(2, 16):
                if n >= FOX_AT:
                    fox_step(n - FOX_AT)
                ahead(UNITS["in1"] + n)
                if n == FOX_AT - 1:
                    fox_weights(0)
                    fox_weights(1)
                if n == 15:
                    turn("turn_y1", 0)
                for c in range(8):
                    if n == (2 + c if crossed("in1", c) else 2 * c + 1):
                        in1(c)
                        if IN1[c][0] == "g":
                            exp_and_ln()
                if n == 2:
                    act.wait_ge(gate_ready, 2)
                    log_gate(rows1, HC, bias_c, rows1[0:HC, 2])
                if n == 3:
                    root("q", MT * HC)
                if n == 7:
                    root("k", MT * HC)
                    for k in range(HC):
                        if k % 2 == 0:
                            wait_full(act, "turn_q", 4 + k // 2)
                        act.activation(qcT[:, k], bank[4 + k // 2][:, (k % 2) * T:(k % 2 + 1) * T], ACT.Copy,
                                       scale=q_gain[:]).then_inc(qT_ready, 1)
            for n in range(2):
                fox_step(16 - FOX_AT + n)
                ahead(UNITS["out1"] + n)
            turn("turn_y1", 1)
            ahead(UNITS["out1"] + 2)
            onto_h(UNITS["out1"] + 3, "turn_x1")
            cross(1)
            mlp(1)
            squares("final", 0, junk)
            squares("final", 1, junk)
            root("final", MT)
            act.wait_ge(norm_ready, NORMS["final"] + 1)
            for m in range(MT):
                act.activation(u[:, m, 0:BANK], u[:, m, 0:BANK], ACT.Copy, scale=rs[:, 0, m:m + 1])\
                   .then_inc(fin_ready[m], 1)

        @block.vector
        def _(dve):
            step = [0]

            def then(ins):
                step[0] += 1
                ins.then_inc(dve_step, 1)
                dve.wait_ge(dve_step, step[0])

            def split(i, slot):
                dve.wait_ge(hi_ready, i + 1)
                dve.tensor_tensor(flat(w_lo[:, slot]), flat(raw[:, slot % RAW]), f(flat(w_hi[:, slot])),
                                  ALU.subtract).then_inc(lo_ready, 1)

            def ahead(i):
                if i + AHEAD < NU:
                    split(i + AHEAD, (i + AHEAD) % RING)

            def root(name, w, sums, n):
                dve.tensor_scalar(st[:, 0, 0:w], sums, 1.0 / n, EPS, ALU.mult, ALU.add).then_inc(root_in, 1)
                dve.wait_ge(root_seed, ROOTS[name] + 1)
                then(dve.tensor_tensor(st[:, 3, 0:w], st[:, 0, 0:w], st[:, 2, 0:w], ALU.mult))
                then(dve.tensor_tensor(st[:, 3, 0:w], st[:, 3, 0:w], st[:, 2, 0:w], ALU.mult))
                then(dve.tensor_scalar(st[:, 3, 0:w], st[:, 3, 0:w], -0.5, 1.5, ALU.mult, ALU.add))
                then(dve.tensor_tensor(st[:, 6, 0:w], st[:, 3, 0:w], st[:, 2, 0:w], ALU.mult))

            def norm_first(stage, src, junk):
                then(dve.tensor_tensor_reduce(out=junk[:, 1], in0=src[:, 1], in1=src[:, 1], scale=1.0, scalar=0.0,
                                              op0=ALU.mult, op1=ALU.add, accum_out=st[:, 4, 1:2]))
                dve.wait_ge(first_squares, ("turn_mix0", "turn_mem").index(stage) + 1)
                root(stage, MT, st[:, 4, 0:MT], D)

            def norm(stage):
                dve.wait_ge(square_sum, 4 * (NORMS[stage] + 1))
                then(dve.tensor_tensor(st[:, 8, 0:MT], st[:, 4, 0:MT], st[:, 4, MT:2 * MT], ALU.add))
                root(stage, MT, st[:, 8, 0:MT], D)
                dve.tensor_copy(rs[:, 0], st[:, 6, 0:MT])
                dve.tensor_tensor(rs[:, 1], st[:, 6, 0:MT], st[:, 6, 0:MT], ALU.mult).then_inc(norm_ready, 1)

            def turn(stage, half):
                g = GAIN[stage]
                for k in range(KU * half, KU * (half + 1)):
                    if k % 2 == 0:
                        dve.wait_ge(acthi_ready, KD * VERSION[stage] + k + 2)
                    z = bank[turn_bank(stage, k // 2)[0]][:, (k % 2) * T:(k % 2 + 1) * T]
                    if g is None:
                        ins = dve.tensor_tensor(act_lo[:, k], z, f(act_hi[:, k]), ALU.subtract)
                    else:
                        ins = dve.scalar_tensor_tensor(out=act_lo[:, k], in0=z, scalar=par[:, g + k:g + k + 1],
                                                       in1=f(act_hi[:, k]), op0=ALU.mult, op1=ALU.subtract)
                    ins.then_inc(actlo_ready, 1)

            def add_to_h(stage, c, scaled=False):
                for m in range(MT):
                    if m == 0:
                        wait_full(dve, stage, 2 * c)
                    else:
                        dve.wait_ge(unit_used, UNITS[stage] + (4 * NJ - 1 if scaled else 3) + c)
                    part = h[:, m, c * BANK:(c + 1) * BANK]
                    if scaled:
                        ins = dve.scalar_tensor_tensor(out=part, in0=bank[2 * c + m][:], scalar=rs[:, 1, m:m + 1],
                                                       in1=part, op0=ALU.mult, op1=ALU.add)
                    else:
                        ins = dve.tensor_tensor(part, bank[2 * c + m][:], part, ALU.add)
                    ins.then_inc(sum_done, 1)

            def onto_h(prev, last, stage, scaled=False):
                add_to_h(prev, 0, scaled)
                turn(stage, 0)
                ahead(last)
                add_to_h(prev, 1, scaled)
                turn(stage, 1)
                norm(stage)

            dve.wait_ge(x_in[1], 16)
            norm_first("turn_mix0", h, u)
            dve.wait_ge(consts, 1)
            for m in range(MT):
                dve.tensor_scalar(diag[:, m], ident[:], st[:, 6, m:m + 1], None, ALU.mult).then_inc(diag_ready, 1)
            wait_full(dve, "params", 7)
            then(dve.tensor_copy(par[:], bank[7][:, 0:NPAR]))
            dve.tensor_scalar(q_gain[:], par[:, PROW["qn"]:PROW["qn"] + 1], P ** -0.5, None, ALU.mult)\
               .then_inc(par_ready, 1)
            l0, l1 = par[:, PROW["lb"]:PROW["lb"] + HM], par[:, PROW["lb"] + HM:PROW["lb"] + 2 * HM]
            then(dve.tensor_tensor(lb[:, 2], l0, l1, ALU.max))
            dve.tensor_tensor(lb[:, 3], l0, lb[:, 2], ALU.subtract)
            dve.tensor_tensor(lb[:, 4], l1, lb[:, 2], ALU.subtract).then_inc(lb_in, 1)
            split(0, 0)
            dve.wait_ge(par_ready, 1)
            turn("turn_mix0", 0)
            turn("turn_mix0", 1)
            split(1, 1)
            dve.wait_ge(gatehi_ready, 1)
            dve.tensor_tensor(flat3(gate_lo[:]), flat3(gate_w[:]), f(flat3(gate_hi[:])), ALU.subtract)\
               .then_inc(gatelo_ready, 1)
            split(2, 2)
            dve.wait_ge(lb_exp, 1)
            then(dve.tensor_tensor(lb[:, 2], lb[:, 3], lb[:, 4], ALU.add))
            then(dve.reciprocal(lb[:, 5], lb[:, 2]))
            dve.tensor_tensor(lb[:, 0], lb[:, 3], lb[:, 5], ALU.mult)
            then(dve.tensor_tensor(lb[:, 1], lb[:, 4], lb[:, 5], ALU.mult))

            dve.wait_ge(consts, 4)

            def log_sigmoid_sum(r, n, bias, zf, count):
                dve.wait_ge(log_out, count)
                then(dve.tensor_scalar(r[0:n, 1], zf, bias[:], 0.0, ALU.add, ALU.min))
                then(dve.tensor_tensor(r[0:n, 1], r[0:n, 1], r[0:n, 0], ALU.subtract))
                then(dve.tensor_tensor_scan(r[0:n, 3], r[0:n, 1], r[0:n, 1], 0.0, ALU.add, ALU.bypass))

            def parts(hi, lo, row, pieces):
                for to, t0, t1 in pieces:
                    ins = dve.tensor_scalar(hi[:, to:to + t1 - t0], row[:, t0:t1], -1.0, None, ALU.mult)
                then(ins)
                for to, t0, t1 in pieces:
                    ins = dve.scalar_tensor_tensor(out=lo[:, to:to + t1 - t0], in0=row[:, t0:t1], scalar=-1.0,
                                                   in1=f(hi[:, to:to + t1 - t0]), op0=ALU.mult, op1=ALU.subtract)
                return ins

            wait_full(dve, "gate0", 4)
            dve.tensor_copy(rows[0:2 * HM, 5], bank[4][0:2 * HM, 0:T]).then_inc(gate_ready, 1)
            ahead(UNITS["in0"])
            ahead(UNITS["in0"] + 1)
            dve.wait_ge(small_in, 16 * 5)
            dve.wait_ge(log_out, 1)
            then(dve.tensor_scalar(rows[0:HM, 2], bank[4][0:HM, 0:T], bias_i[:], None, ALU.add))
            log_sigmoid_sum(rows, HM, bias_f, bank[5][0:HM, 0:T], 1)
            then(dve.tensor_tensor(rows[0:HM, 4], rows[0:HM, 2], rows[0:HM, 3], ALU.subtract))
            then(dve.tensor_tensor_scan(rows[0:HM, 5], rows[0:HM, 4], rows[0:HM, 4], 0.0, ALU.max, ALU.bypass))
            parts(max_hi[0:HM], max_lo[0:HM], rows[0:HM, 5], ((0, 0, T), (T, P, T)))
            dve.scalar_tensor_tensor(out=rows[0:HM, 6], in0=rows[0:HM, 3], scalar=-1.0, in1=rows[0:HM, 5],
                                     op0=ALU.mult, op1=ALU.subtract).then_inc(rows_ready, 1)

            def mlstm_weight(hd):
                dve.wait_ge(decay_ready, hd + 1)
                wait_full(dve, "mlstm", 5, hd)
                dve.scalar_tensor_tensor(out=weight[:, hd % 2], in0=bank[5][:, 0:3 * P], scalar=P ** -0.5,
                                         in1=decay[:, hd % 2], op0=ALU.mult, op1=ALU.mult).then_inc(weight_ready, 1)

            def finish_pair(hp):
                for m in range(MT):
                    b = 6 + m
                    wait_full(dve, "mlstm", b, hp + (b == 6))
                    v = bank[b][:, 0:2 * (P + 1)].rearrange("p (h d) -> p h d", d=P + 1)
                    den = v[:, :, P:P + 1].rearrange("p h d -> p (h d)")
                    floor = cols[:, 1, HM * m + 2 * hp:HM * m + 2 * hp + 2]
                    c = slice(4 * m + 2 * hp, 4 * m + 2 * hp + 2)
                    then(dve.scalar_tensor_tensor(out=st[:, 7, c], in0=den, scalar=-1.0, in1=floor,
                                                  op0=ALU.mult, op1=ALU.max))
                    then(dve.tensor_tensor(st[:, 7, c], den, st[:, 7, c], ALU.max))
                    then(dve.reciprocal(st[:, 7, c], st[:, 7, c]))
                    for k in range(2):
                        hd = 2 * hp + k
                        part = slice(hd * P, (hd + 1) * P)
                        ins = dve.scalar_tensor_tensor(out=u[:, m, part], in0=v[:, k, 0:P],
                                                       scalar=st[:, 7, 4 * m + hd:4 * m + hd + 1],
                                                       in1=oa[:, m, part], op0=ALU.mult, op1=ALU.mult)
                    ins.then_inc((half_ready, y_ready)[hp], 1)

            def in0(c):
                name = IN0[c][0]
                if name in CONV0:
                    for i in range(2):
                        b = 2 * (c % 2) + i
                        wait_chunk(dve, "in0", c, i)
                        for lag in range(1, 4):
                            for k in range(CONV0[name] + 2 * i, CONV0[name] + 2 * i + 2):
                                if lag == 1 and k % 2 == 0:
                                    dve.wait_ge(tap_ready, k + 2)
                                w = PROW["conv"] + (3 - lag) * KD + k
                                z = bank[b][:, (k % 2) * T:(k % 2 + 1) * T - lag]
                                ins = dve.scalar_tensor_tensor(out=qkT[:, k, lag:T], in0=z, scalar=par[:, w:w + 1],
                                                               in1=qkT[:, k, lag:T], op0=ALU.mult, op1=ALU.add)
                                if k % 2 and lag < 3:
                                    then(ins)
                        ins.then_inc(conv_done, 1)
                if name == "fb":
                    for i in range(2):
                        dve.wait_ge(sigmoid_ready, i + 1)
                        dve.wait_ge(in_done[2 * (c % 2) + i], c // 2)
                        for hd in range(2 * i, 2 * i + 2):
                            ins = dve.tensor_scalar(dec[:, 0, hd], dec[:, 0, hd], lb[:, 1, hd:hd + 1],
                                                    lb[:, 0, hd:hd + 1], ALU.mult, ALU.add)
                        ins.then_inc(forget_ready, 1)
                        for hd in range(2 * i, 2 * i + 2):
                            ins = dve.tensor_scalar(kb[:, hd], kb[:, hd], lb[:, 1, hd:hd + 1], None, ALU.mult)
                        ins.then_inc(keep_ready, 1)

            def distance(n):
                level = LEVELS[n]
                if n >= 3:
                    dve.wait_ge(scaled_ready, n - 2)
                v, mid = last_of_half(level)
                d = halves(dec[:, n % 2], level)
                dve.tensor_tensor(d[:, :, 0, :], mid, v[:, :, 0, :], ALU.subtract)
                dve.tensor_tensor(d[:, :, 1, :], v[:, :, 1, :], mid, ALU.subtract).then_inc(dist_ready, 1)

            def scale(n):
                dve.wait_ge(dec_ready, n)
                level = LEVELS[n]
                for to, of, which in ((qd, qb, 1), (kd, kb, 0)):
                    if n <= 2 and to is kd:
                        ins = dve.tensor_tensor(flat(kd[:, n % 2]), flat(kb[:]), flat(dec[:, n % 2]), ALU.mult)
                        continue
                    ins = dve.tensor_tensor(halves(to[:, n % 2], level)[:, :, which, :],
                                            halves(of[:], level)[:, :, which, :],
                                            halves(dec[:, n % 2], level)[:, :, which, :], ALU.mult)
                ins.then_inc(scaled_ready, 1)

            for c in range(8):
                if c == MLSTM_AT:
                    dve.wait_ge(cols_ready, 1)
                    dve.wait_ge(in_done[0], 1)
                    dve.wait_ge(in_done[1], 1)
                if MLSTM_AT <= c < MLSTM_AT + 2:
                    mlstm_weight(2 * (c - MLSTM_AT))
                if c >= MLSTM_AT + 2:
                    finish_pair(c - MLSTM_AT - 2)
                if c:
                    ahead(UNITS["in0"] + 2 * c)
                if MLSTM_AT <= c < MLSTM_AT + 2:
                    mlstm_weight(2 * (c - MLSTM_AT) + 1)
                if c == MLSTM_AT:
                    dve.wait_ge(mem_in, 16)
                    norm_first("turn_mem", mem_v, u)
                    for m in range(MT):
                        dve.tensor_scalar(mem_v[:, m], mem_v[:, m], st[:, 6, m:m + 1], None, ALU.mult)\
                           .then_inc(memory_ready, 1)
                if c:
                    ahead(UNITS["in0"] + 2 * c + 1)
                in0(c)
                if c == MLSTM_AT + 2:
                    dve.wait_ge(log_forget, 1)
                    for hd in range(HM):
                        ins = dve.tensor_tensor_scan(cum[:, hd], dec[:, 1, hd], dec[:, 1, hd], 0.0, ALU.add,
                                                     ALU.bypass)
                    then(ins)
                    distance(1)
            turn("turn_mem", 0)
            turn("turn_mem", 1)
            for b in range(4):
                dve.wait_ge(in_done[b], IN_DONE0[b])
            dve.wait_ge(keep_ready, 2)
            distance(2)
            scale(1)

            def head_sums(first, between=lambda: None):
                for m in range(MT):
                    if m:
                        between()
                    dve.wait_ge(y_squared, first + m + 1)
                    then(dve.tensor_reduce(st[:, 5, HM * m:HM * (m + 1)], heads(u[:, m, BANK:2 * BANK]), AX.X,
                                           ALU.add))

            def mlstm_norm():
                head_sums(0)
                root("mlstm", MT * HM, st[:, 5, 0:MT * HM], P)
                for m in range(MT):
                    y = heads(u[:, m, 0:BANK])
                    dve.tensor_tensor(y, y, spread(st[:, 6, HM * m:HM * (m + 1)], P), ALU.mult).then_inc(y_normed, 1)

            def choose(n):
                if n == 0:
                    for tile in range(MT):
                        wait_full(dve, "hgrn", 2 + tile)
                        dve.copy_predicated(pair_w[:, tile], pairs[:, n].unsqueeze(1).to_broadcast([P, HM, P]),
                                            heads(bank[2 + tile][:])).then_inc(selected, 1)
                    return
                level = LEVELS[n]
                b = 2 + 2 * (n % 2)
                wait_full(dve, "hgrn", b, n // 2)
                dve.wait_ge(selected, n + 1)
                mask = second_halves(pairs[:, n], level).unsqueeze(1).to_broadcast([P, MT * HM, P // (2 * level), level])
                dve.copy_predicated(second_halves(pair_w[:].rearrange("p m h t -> p (m h) t"), level), mask,
                                    bank[b][:].rearrange("p (h b l) -> p h b l", h=MT * HM, l=level))\
                   .then_inc(selected, 1)

            for n in range(1, len(LEVELS)):
                choose(n - 1)
                if n + 2 < len(LEVELS):
                    distance(n + 2)
                if n + 1 < len(LEVELS):
                    scale(n + 1)
                if n == 8:
                    turn("turn_y0", 0)
                ahead(UNITS["kv"] + n - 1)
                if n == 2:
                    mlstm_norm()
            head_sums(2, lambda: ahead(UNITS["out0"]))
            root("hgrn", MT * HM, st[:, 5, 0:MT * HM], P)
            for m in range(MT):
                for hd in range(HM):
                    part = slice(hd * P, (hd + 1) * P)
                    ins = dve.scalar_tensor_tensor(out=u[:, m, BANK + hd * P:BANK + (hd + 1) * P],
                                                   in0=bank[4 + m][:, part], scalar=st[:, 6, HM * m + hd:HM * m + hd + 1],
                                                   in1=gb[:, m, part], op0=ALU.mult, op1=ALU.mult)
                ins.then_inc(y_scaled, 1)
            turn("turn_y0", 1)
            ahead(UNITS["out0"] + 1)
            ahead(UNITS["out0"] + 2)
            onto_h("out0", UNITS["out0"] + 3, "turn_x0")

            def cross(l):
                uq, uo = UNITS[f"xq{l}"], UNITS[f"xo{l}"]
                stage = f"xattn{l}"

                def maximum(i):
                    c = slice(2 * (i % 2), 2 * (i % 2) + 2)
                    wait_full(dve, stage, 4 + i % 2, i // 2)
                    then(dve.tensor_reduce(xs[:, 0, c], bank[4 + i % 2][:].rearrange("p (m t) -> p m t", m=MT), AX.X,
                                           ALU.max))
                    dve.scalar_tensor_tensor(out=xs[:, 1, c], in0=xs[:, 0, c], scalar=-1.0, in1=rs[:, 0],
                                             op0=ALU.mult, op1=ALU.mult).then_inc(xmax, 1)

                def normalize(i):
                    c = slice(2 * (i % 2), 2 * (i % 2) + 2)
                    dve.wait_ge(xexp, HX * l + i + 1)
                    then(dve.reciprocal(xs[:, 3, c], xs[:, 2, c]))
                    dve.tensor_tensor(px[:, i % 2], px[:, i % 2], spread(xs[:, 3, c], T), ALU.mult)\
                       .then_inc(xnorm, 1)

                def output(i):
                    dve.wait_ge(acthi_ready, KD * VERSION[stage] + 2 * i + 2)
                    both = slice(2 * i, 2 * i + 2)
                    dve.tensor_tensor(flat(act_lo[:, both]), bank[7][:], f(flat(act_hi[:, both])),
                                      ALU.subtract).then_inc(actlo_ready, 2)

                dve.wait_ge(norm_ready, NORMS[f"turn_x{l}"] + 1)
                for n in range(4):
                    ahead(uq + n)
                maximum(0)
                normalize(0)
                maximum(1)
                normalize(1)
                maximum(2)
                output(0)
                normalize(2)
                maximum(3)
                output(1)
                normalize(3)
                ahead(uo)
                output(2)
                ahead(uo + 1)
                output(3)
                ahead(uo + 2)
                onto_h(f"xo{l}", uo + 3, f"turn_m{l}")

            def mlp(l):
                def hidden(j, buf, unit):
                    for i in range(2):
                        if l or not isinstance(j, int) or j:
                            dve.wait_ge(hidlo_ready, 2 * j + (2 * NJ * l + i - 1))
                        dve.wait_ge(relu_ready, 2 * j + (2 * NJ * l + i + 1))
                        dve.scalar_tensor_tensor(out=hid[:, i], in0=bank[hidden_bank(j) + i][:], scalar=0.0, in1=relu[:, i],
                                                 op0=ALU.max, op1=ALU.mult).then_inc(hid_ready, 1)
                    for i in range(2):
                        dve.wait_ge(hidhi_ready, 2 * j + (2 * NJ * l + i + 1))
                        dve.tensor_tensor(flat(hid_lo[:, buf, 2 * i:2 * i + 2]), hid[:, i],
                                          f(flat(hid_hi[:, buf, 2 * i:2 * i + 2])), ALU.subtract)\
                           .then_inc(hidlo_ready, 1)
                mlp_walk(dve, l, split, ahead, hidden)

            cross(0)
            mlp(0)

            ahead(UNITS["mlp0"] + 4 * NJ - 2)
            onto_h("mlp0", UNITS["mlp0"] + 4 * NJ - 1, "turn_mix1", True)
            dve.wait_ge(norm_ready, NORMS["turn_mix1"] + 1)
            ahead(UNITS["in1"])
            for m in range(MT):
                dve.tensor_scalar(diag[:, m], ident[:], rs[:, 0, m:m + 1], None, ALU.mult).then_inc(diag_ready, 1)
            ahead(UNITS["in1"] + 1)

            def gates1():
                wait_full(dve, "gate1", 4)
                then(dve.tensor_copy(rows1[0:HC, 2], bank[4][0:HC, T:2 * T]))
                dve.tensor_tensor(rows1[0:HC, 2], bank[4][0:HC, 0:T], rows1[0:HC, 2], ALU.mult).then_inc(gate_ready, 1)
                in1(0)
                log_sigmoid_sum(rows1, HC, bias_c, rows1[0:HC, 2], 2)
                parts(forget_hi[0:HC], forget_lo[0:HC], rows1[0:HC, 3], ((0, 0, P), (P, 0, T))).then_inc(rows_ready, 1)

            def in1(c):
                name, n = IN1[c]
                for m in range(MT):
                    b = 2 * (c % 2) + m
                    part = slice(n * BANK, (n + 1) * BANK)
                    dve.wait_ge(in_done[b], IN_DONE0[b] + c // 2 + 1)
                    dve.tensor_reduce(st[:, 5, HC * m + HM * n:HC * m + HM * (n + 1)], heads(u[:, m, part]), AX.X,
                                      ALU.add).then_inc(squares_used, 1)
                if n == 1:
                    dve.wait_ge(squares_used, 2 * (c + 1))
                    root(name, MT * HC, st[:, 5, 0:MT * HC], P)
                    z = qc if name == "q" else kc
                    for m in range(MT):
                        zm = heads(z[:, m], HC)
                        dve.tensor_tensor(zm, zm, spread(st[:, 6, HC * m:HC * (m + 1)], P), ALU.mult)\
                           .then_inc(cnormed, 1)

            def fox_maximum(i):
                wait_full(dve, "fox", 4 + i % 2, i // 2)
                for m in range(MT):
                    ins = dve.tensor_reduce(csum[:, 0, 2 * i + m:2 * i + m + 1],
                                            bank[4 + i % 2][:, m * P:(1 + 2 * m) * P], AX.X, ALU.max)
                then(ins)
                dve.tensor_scalar(csum[:, 1, 2 * i:2 * i + 2], csum[:, 0, 2 * i:2 * i + 2], -1.0, None, ALU.mult)\
                   .then_inc(cmax, 1)

            def fox_output(hp):
                c = slice(4 * hp, 4 * hp + 4)
                dve.wait_ge(cexp, 2 * hp + 2)
                then(dve.reciprocal(csum[:, 3, c], csum[:, 2, c]))
                wait_full(dve, "fox", 7, 2 * hp + 1)
                for m in range(MT):
                    gate_chunk = IN1.index(("g", hp // 2))
                    b = 2 * (gate_chunk % 2) + m
                    dve.wait_ge(in_done[b], IN_DONE0[b] + gate_chunk // 2 + 1)
                    for hd in (2 * hp, 2 * hp + 1):
                        part, at = slice(hd * P, (hd + 1) * P), (hd % 2) * T + m * P
                        ins = dve.scalar_tensor_tensor(out=u[:, m, part], in0=bank[7][:, at:at + P],
                                                       scalar=csum[:, 3, 2 * hd + m:2 * hd + m + 1],
                                                       in1=gc[:, m, part], op0=ALU.mult, op1=ALU.mult)
                ins.then_inc(oc_done, 1)

            for n in range(2, 16):
                if n >= FOX_AT:
                    fox_maximum(n - FOX_AT + 2)
                if n == FOX_AT + 2:
                    fox_output(0)
                if n == FOX_AT - 2:
                    for k in range(HC):
                        if k % 2 == 0:
                            wait_full(dve, "turn_k", 4 + k // 2)
                        dve.tensor_scalar(kcT[:, k], bank[4 + k // 2][:, (k % 2) * T:(k % 2 + 1) * T],
                                          par[:, PROW["kn"]:PROW["kn"] + 1], None, ALU.mult).then_inc(kT_ready, 1)
                if n == FOX_AT - 1:
                    fox_maximum(0)
                    fox_maximum(1)
                ahead(UNITS["in1"] + n)
                if n == FOX_AT + 3:
                    fox_output(1)
                if n == 15:
                    turn("turn_y1", 0)
                if n == 2:
                    gates1()
                for c in range(1, 4):
                    if n == (2 + c if crossed("in1", c) else 2 * c + 1):
                        in1(c)
            fox_output(2)
            ahead(UNITS["out1"])
            ahead(UNITS["out1"] + 1)
            fox_output(3)
            turn("turn_y1", 1)
            ahead(UNITS["out1"] + 2)
            onto_h("out1", UNITS["out1"] + 3, "turn_x1")
            cross(1)
            mlp(1)
            add_to_h("mlp1", 0, True)
            dve.wait_ge(gain_in, 16)
            dve.wait_ge(sum_done, 4 * SUM_BEFORE["final"] - 2)
            for m in range(MT):
                dve.tensor_tensor(u[:, m, 0:BANK], h[:, m, 0:BANK], final_g[:, 0:BANK], ALU.mult)
            add_to_h("mlp1", 1, True)
            norm("final")
            dve.wait_ge(norm_ready, NORMS["final"] + 1)
            for m in range(MT):
                dve.scalar_tensor_tensor(out=u[:, m, BANK:D], in0=h[:, m, BANK:D], scalar=rs[:, 0, m:m + 1],
                                         in1=final_g[:, BANK:D], op0=ALU.mult, op1=ALU.mult)\
                   .then_inc(fin_ready[MT + m], 1)

        @block.tensor
        def _(pe):
            def three(o, a_hi, a_lo, b_hi, b_lo, start, stop, mark=False):
                pe.matmul(o, a_hi, b_hi, start=start, stop=False, skip_group_check=True)
                pe.matmul(o, a_hi, b_lo, start=False, stop=False, skip_group_check=True)
                return pe.matmul(o, a_lo, b_hi, start=False, stop=stop, skip_group_check=True)

            def unit(i, slot, k0, banks, transposed, first, last, x_hi, x_lo, between=None, version=None):
                pe.wait_ge(lo_ready, i + 1)
                for g in range(2):
                    if g and between is not None:
                        between()
                    for k in range(KU):
                        begin, end = first and k == 0, last and k == KU - 1
                        if g == 0 and version is not None:
                            pe.wait_ge(actlo_ready, KD * version + k0 + k + 1)
                        if transposed:
                            for q in range(2):
                                cut = slice((2 * g + q) * P, (2 * g + q + 1) * P)
                                ins = three(bank[banks + g][:, q * T:(q + 1) * T], w_hi[:, slot, k, cut],
                                            w_lo[:, slot, k, cut], x_hi[:, k0 + k], x_lo[:, k0 + k],
                                            begin and q == 0, end)
                        else:
                            cut = slice(g * P, (g + 1) * P)
                            ins = three(bank[banks + g][:], x_hi[:, k0 + k, cut], x_lo[:, k0 + k, cut],
                                        w_hi[:, slot, k], w_lo[:, slot, k], begin, end)
                    if g == 0 and last:
                        ins.then_inc(full[banks], 1)
                ins.then_inc(unit_used, 1)

            def turn(stage, half, src, scale=None):
                for j in (2 * half, 2 * half + 1):
                    b = turn_bank(stage, j)[0]
                    for m in range(MT):
                        for k in (2 * j, 2 * j + 1):
                            o = bank[b][:, (k % 2) * T + m * P:(k % 2) * T + (m + 1) * P]
                            if scale is None:
                                ins = pe.transpose(o, src[:, m, k * P:(k + 1) * P], ident[:])
                            else:
                                ins = pe.matmul(o, src[:, m, k * P:(k + 1) * P], scale[:, m], start=True, stop=True)
                    ins.then_inc(full[b], 1)

            def turn_h(stage, half):
                pe.wait_ge(sum_done, 4 * (SUM_BEFORE[stage] - 1) + 2 * (half + 1))
                turn(stage, half, h)

            def project(stage, n, transposed, version, between=None):
                c, half = unit_order(stage, 8)[n]
                i = UNITS[stage] + n
                unit(i, i % RING, KU * half, 2 * (c % 2), transposed, half == 0, half == 1, act_hi, act_lo,
                     between=between, version=version)

            pe.wait_ge(consts, 1)
            pe.wait_ge(par_in, 16 * 10)
            pe.transpose(bank[7][:, 0:NPAR], par_rows[:], ident[0:NPAR, 0:NPAR]).then_inc(full[7], 1)
            pe.wait_ge(par_ready, 1)
            for m in range(MT):
                pe.wait_ge(diag_ready, m + 1)
                pe.wait_ge(x_in[m], 16)
            turn("turn_mix0", 0, h, diag)
            turn("turn_mix0", 1, h, diag)
            v = VERSION["turn_mix0"]

            def gate(l, v):
                pe.wait_ge(gatelo_ready, 1)
                pe.wait_ge(actlo_ready, KD * (v + 1))
                if l:
                    pe.wait_ge(diag_ready, 2 * MT)
                    for m in range(MT):
                        pe.matmul(bank[4][0:8, T + m * P:T + (m + 1) * P], ones[:], diag[:, m], start=True, stop=True)
                for k in range(KD):
                    ins = three(bank[4][0:8, 0:T], gate_hi[:, l, k], gate_lo[:, l, k], act_hi[:, k], act_lo[:, k],
                                k == 0, k == KD - 1)
                ins.then_inc(full[4], 1)

            def diagonals(b):
                return b[:].rearrange("p (a b) -> p a b", a=2)[:, :, 0:P]

            def twice(mask):
                return mask[:].unsqueeze(1).to_broadcast([P, 2, P])

            def mlstm_scores(hd):
                if hd == 0:
                    pe.wait_ge(rows_ready, 1)
                    pe.wait_ge(consts, 4)
                    for q, r in enumerate((4, 6)):
                        for m in range(MT):
                            at = (MT * q + m) * HM
                            ins = pe.transpose(bank[6][:, at:at + HM], rows[0:HM, r, m * P:(m + 1) * P],
                                               ident[0:HM, 0:HM])
                    ins.then_inc(full[6], 1)
                    pe.wait_ge(conv_silu, 4)
                else:
                    pe.wait_ge(weight_ready, hd)
                for part in (max_hi, max_lo):
                    pe.matmul(bank[4][:, 0:3 * P], select[0:HM, hd], part[0:HM], start=(part is max_hi), stop=False,
                              skip_group_check=True)
                pe.matmul(diagonals(bank[4]), ident_r[:], twice(after_T), start=False, stop=True,
                          skip_group_check=True).then_inc(full[4], 1)
                pe.matmul(bank[5][:, 0:T], qkT[:, HM + hd, 0:P], qkT[:, hd], start=True, stop=True)
                pe.matmul(bank[5][:, T:3 * P], qkT[:, HM + hd, P:T], qkT[:, hd, P:T], start=True, stop=True)\
                  .then_inc(full[5], 1)

            def mlstm_values(hd):
                pe.wait_ge(weight_ready, hd + 1)
                if hd == 0:
                    pe.wait_ge(cols_ready, 1)
                    pe.wait_ge(in_done[2], 1)
                    pe.wait_ge(in_done[3], 1)
                if hd == 2:
                    pe.wait_ge(half_ready, MT)
                for m in range(MT):
                    o = bank[6 + m][:, (hd % 2) * (P + 1):(hd % 2 + 1) * (P + 1)]
                    for s in range(m + 1):
                        ins = pe.matmul(o, weight[:, hd % 2, (m + s) * P:(m + s + 1) * P], va[:, s, hd],
                                        start=(s == 0), stop=(s == m))
                    if hd % 2:
                        ins.then_inc(full[6 + m], 1)

            def mlstm_step(n):
                if n == 0:
                    mlstm_scores(0)
                if n == 2:
                    mlstm_scores(1)
                if n in (4, 6):
                    mlstm_values(n // 2 - 2)
                    mlstm_scores(n // 2)
                if n in (9, 10):
                    mlstm_values(n - 7)

            for c, (name, _, transposed) in enumerate(IN0):
                for half in range(2):
                    i = UNITS["in0"] + 2 * c + half
                    if half == 0 and c >= 2:
                        for b in (2 * (c % 2), 2 * (c % 2) + 1):
                            if IN0[c - 2][0] in CONV0:
                                pe.wait_ge(conv_done, CONV0[IN0[c - 2][0]] // 2 + b % 2 + 1)
                            else:
                                done = len([1 for q in range(c % 2, c, 2) if IN0[q][0] not in CONV0])
                                pe.wait_ge(in_done[b], done)
                    step = 4 * (c - MLSTM_AT) + 2 * half
                    mlstm_step(step)
                    if i == UNITS["in0"] + 15:
                        pe.wait_ge(y_ready, 2)
                        pe.wait_ge(memory_ready, MT)
                        turn("turn_mem", 0, mem_v)
                        turn("turn_mem", 1, mem_v)
                    between = (lambda: mlstm_step(step + 1)) if c else None
                    project("in0", 2 * c + half, transposed, v, between=between)
                    if i == UNITS["in0"]:
                        gate(0, v)
                    if i == UNITS["in0"] + 1:
                        pe.wait_ge(gate_ready, 1)
                        pe.matmul(bank[5][0:HM, 0:T], ident[0:2 * HM, HM:2 * HM], rows[0:2 * HM, 5], start=True,
                                  stop=True).then_inc(full[5], 1)

            def hgrn_level(n):
                level = LEVELS[n]
                if n:
                    pe.wait_ge(scaled_ready, n)
                else:
                    pe.wait_ge(keep_ready, 2)
                    for b in range(4):
                        pe.wait_ge(in_done[b], IN_DONE0[b])
                if n >= 2:
                    pe.wait_ge(selected, n)
                kk, qq = (kb[:], qb[:]) if n == 0 else (kd[:, n % 2], qd[:, n % 2])
                b = 2 + 2 * (n % 2)
                for tile in range(1 if level == 128 else MT):
                    to = 1 if level == 128 else tile
                    for hd in range(HM):
                        k, q = kk[:, hd, tile * P:(tile + 1) * P], qq[:, hd, to * P:(to + 1) * P]
                        if level in (0, 128):
                            ins = pe.matmul(bank[b + tile][:, hd * P:(hd + 1) * P], k, q, start=True, stop=True)
                        else:
                            at = (tile * HM + hd) * P // 2
                            o = bank[b][:, at:at + P // 2].rearrange("p (b l) -> p b l", l=level)
                            ins = pe.matmul(o, k, second_halves(q, level), start=True, stop=True)
                    if level == 0:
                        ins.then_inc(full[b + tile], 1)
                if level:
                    ins.then_inc(full[b], 1)

            v = VERSION["turn_mem"]
            for n in range(1, len(LEVELS)):
                c, half = (n - 1) // 2, (n - 1) % 2
                if half == 0 and c:
                    pe.wait_ge(kv_done, 2 * c)
                if n == 8:
                    pe.wait_ge(y_normed, MT)
                    turn("turn_y0", 0, u)
                i = UNITS["kv"] + n - 1
                unit(i, i % RING, KU * half, 0, c < 2, half == 0, half == 1, act_hi, act_lo, version=v)
                if n == 1:
                    hgrn_level(0)
                    pe.wait_ge(actlo_ready, KD * v + KD)
                hgrn_level(n)
            v = VERSION["turn_y0"]
            pe.wait_ge(selected, len(LEVELS))
            for m in range(MT):
                if m:
                    pe.wait_ge(pairx_ready, 1)
                for hd in range(HM):
                    o, part = bank[4 + m][:, hd * P:(hd + 1) * P], slice(hd * P, (hd + 1) * P)
                    if m:
                        pe.matmul(o, pair_x[:, hd], vb[:, 0, part], start=True, stop=False)
                    ins = pe.matmul(o, pair_w[:, m, hd], vb[:, m, part], start=(m == 0), stop=True)
                ins.then_inc(full[4 + m], 1)
                if m == 0:
                    pe.wait_ge(kv_done, 8)
                    project("out0", 0, False, v)
            project("out0", 1, False, v)
            pe.wait_ge(y_scaled, MT)
            turn("turn_y0", 1, u)
            project("out0", 2, False, v)
            project("out0", 3, False, v, between=lambda: turn_h("turn_x0", 0))

            def cross(l):
                stage, q, o = f"xattn{l}", f"xq{l}", f"xo{l}"
                v = VERSION[f"turn_x{l}"]

                def scores(i):
                    pe.wait_ge(xq_done, 4 * l + i // 2 * 2 + 2)
                    if i >= 2:
                        pe.wait_ge(xexp, HX * l + i - 1)
                    for m in range(MT):
                        for k in range(2):
                            ins = pe.matmul(bank[4 + i % 2][:, m * T:(m + 1) * T],
                                            xqT[:, 2 * i + k, m * P:(m + 1) * P], mem_kT[:, 2 * i + k],
                                            start=(k == 0), stop=(k == 1))
                    ins.then_inc(full[4 + i % 2], 1)

                def turned(i):
                    pe.wait_ge(xnorm, HX * l + i + 1)
                    if i:
                        pe.wait_ge(xturned, HX * l + i)
                    for m in range(MT):
                        for j in range(MT):
                            ins = pe.transpose(bank[6][:, j * T + m * P:j * T + (m + 1) * P],
                                               px[:, i % 2, m, j * P:(j + 1) * P], ident[:])
                    ins.then_inc(full[6], 1)

                def output(i):
                    pe.wait_ge(xturned, HX * l + i + 1)
                    if i:
                        pe.wait_ge(actlo_ready, KD * VERSION[stage] + 2 * i)
                    for k in range(2):
                        at = XD * i + P * k
                        for j in range(MT):
                            ins = pe.matmul(bank[7][:, k * T:(k + 1) * T], mem_v[:, j, at:at + P], pxT[:, i % 2, j],
                                            start=(j == 0), stop=(j == MT - 1))
                    ins.then_inc(full[7], 1)

                project(q, 0, True, v)
                turn_h(f"turn_x{l}", 1)
                pe.wait_ge(sum_done, 4 * SUM_BEFORE[f"turn_x{l}"])
                for n in (1, 2):
                    project(q, n, True, v)
                project(q, 3, True, v, between=lambda: scores(0))
                scores(1)
                turned(0)
                scores(2)
                output(0)
                turned(1)
                scores(3)
                output(1)
                turned(2)
                v = VERSION[stage]
                project(o, 0, False, v)
                output(2)
                turned(3)
                project(o, 1, False, v, between=lambda: output(3))
                project(o, 2, False, v)
                project(o, 3, False, v, between=lambda: turn_h(f"turn_m{l}", 0))

            def mlp(l):
                stage = f"mlp{l}"

                def w1(i, slot, j):
                    pe.wait_ge(hid_ready, 2 * j + 2 * NJ * l)
                    for half in range(2):
                        unit(i + half, (slot + half) % RING, KU * half, 4, True, half == 0, half == 1, act_hi, act_lo)

                def w2(i, slot, j, buf, first, last):
                    pe.wait_ge(hidlo_ready, 2 * j + (2 * NJ * l + 2))
                    for n in range(2):
                        unit(i + n, (slot + n) % RING, 0, 2 * n, False, first, last, hid_hi[:, buf], hid_lo[:, buf],
                             between=(lambda: turn_h("turn_mix1", 0)) if last and n and l == 0 else None)

                u0 = UNITS[stage]
                v = VERSION[f"turn_m{l}"]
                pe.wait_ge(actlo_ready, KD * v + KU)
                for half in range(2):
                    for j in range(2):
                        i = u0 + 2 * half + j
                        unit(i, i % RING, KU * half, hidden_bank(j), True, half == 0, half == 1, act_hi, act_lo,
                             version=v)
                        if i == u0:
                            turn_h(f"turn_m{l}", 1)
                w2(u0 + 4, (u0 + 4) % RING, 0, 0, True, False)
                with pe.Fori(0, (NJ - 2) // 2) as it:
                    for n, (which, j, buf) in enumerate(in_order(it)):
                        i, slot = 8 * it + (u0 + 6 + 2 * n), (u0 + 6 + 2 * n) % RING
                        if which == 1:
                            w1(i, slot, j)
                        else:
                            w2(i, slot, j, buf, False, False)
                w2(u0 + 4 * NJ - 2, (u0 + 4 * NJ - 2) % RING, NJ - 1, (NJ - 1) % 2, False, True)

            cross(0)
            mlp(0)

            v = VERSION["turn_mix1"]

            def fox_scores(i):
                pe.wait_ge(kT_ready, min(2 * (i + 1), HC))
                if i >= 2:
                    pe.wait_ge(cexp, i - 1)
                b = 4 + i % 2
                for m in range(MT):
                    w = (m + 1) * P
                    pe.matmul(bank[b][:, m * P:m * P + w], qcT[:, i, m * P:(m + 1) * P], kcT[:, i, 0:w],
                              start=(m == 0), stop=False, skip_group_check=True)
                for part in (forget_hi, forget_lo):
                    pe.matmul(bank[b][:, 0:3 * P], select[0:HC, i], part[0:HC], start=False, stop=False,
                              skip_group_check=True)
                pe.matmul(diagonals(bank[b]), ident_r[:], twice(after), start=False, stop=True,
                          skip_group_check=True).then_inc(full[b], 1)

            def fox_turned(i):
                pe.wait_ge(cexp, i + 1)
                if i:
                    pe.wait_ge(cturned, i)
                for n in range(3):
                    ins = pe.transpose(bank[6][:, n * P:(n + 1) * P], pc[:, i % 2, n * P:(n + 1) * P], ident[:])
                ins.then_inc(full[6], 1)

            def fox_output(i):
                pe.wait_ge(cturned, i + 1)
                if i % 2 == 0 and i:
                    pe.wait_ge(oc_done, i // 2)
                for m in range(MT):
                    at = (i % 2) * T + m * P
                    for t in range(m + 1):
                        ins = pe.matmul(bank[7][:, at:at + P], pcT[:, i % 2, (m + t) * P:(m + t + 1) * P],
                                        vc[:, t, i * P:(i + 1) * P], start=(t == 0), stop=(t == m))
                ins.then_inc(full[7], 1)

            def fox_first():
                fox_scores(0)
                fox_scores(1)

            for n in range(16):
                c = unit_order("in1", 8)[n][0]
                if n == 1:
                    pe.wait_ge(sum_done, 4 * SUM_BEFORE["turn_mix1"])
                if n >= 4 and n % 2 == 0:
                    for b in (2 * (c % 2), 2 * (c % 2) + 1):
                        pe.wait_ge(in_done[b], IN_DONE0[b] + c // 2)
                between = None
                if n == FOX_AT - 1:
                    pe.wait_ge(qT_ready, HC)
                    pe.wait_ge(cnormed, 2 * MT)
                    for half in range(2):
                        turn("turn_k", half, kc)
                    between = fox_first
                if n >= FOX_AT:
                    i = n - FOX_AT
                    if i == 0:
                        pe.wait_ge(kT_ready, HC)
                    fox_turned(i)
                    fox_scores(i + 2)
                    between = lambda: fox_output(i)
                    if n == 15:
                        def between():
                            for b in range(2):
                                pe.wait_ge(in_done[b], IN_DONE0[b] + 4)
                            pe.wait_ge(oc_done, 2)
                            turn("turn_y1", 0, u)
                            fox_output(i)
                project("in1", n, False, v, between=between)
                if n == 0:
                    turn_h("turn_mix1", 1)
                if n == 2:
                    gate(1, v)
                if n == 6:
                    pe.wait_ge(rows_ready, 2)
                    pe.wait_ge(cnormed, MT)
                    for half in range(2):
                        turn("turn_q", half, qc)
            v = VERSION["turn_y1"]
            for n in range(2):
                i = 16 - FOX_AT + n
                fox_turned(i)
                if n == 0:
                    pe.wait_ge(actlo_ready, KD * v + KU)
                if n:
                    for b in (2, 3):
                        pe.wait_ge(in_done[b], IN_DONE0[b] + 4)
                project("out1", n, False, v, between=lambda: fox_output(i))
            pe.wait_ge(oc_done, HC // 2)
            turn("turn_y1", 1, u)
            project("out1", 2, False, v)
            project("out1", 3, False, v, between=lambda: turn_h("turn_x1", 0))
            cross(1)
            mlp(1)


_INS = ["x", "mem", "norm_mix_g", "norm_xattn_g", "norm_mlp_g", "final_norm_g", "ab_w_in", "ab_conv_w",
        "ab_gate_b", "hgrn_lb_logits", "mlstm_norm_g", "hgrn_norm_g", "ab_w_out", "c_w_in", "c_fgate_b",
        "c_qnorm_g", "c_knorm_g", "c_w_out", "mem_norm_g", "mem_w_kv", "xa_w_q", "xa_w_o", "mlp_w1", "mlp_w2"]


def kernel(**inputs):
    import numpy as _np
    import concourse.bacc as _bacc
    from concourse import mybir as _mybir
    from concourse.bass_utils import run_bass_kernel_spmd as _run

    nc = _bacc.Bacc("TRN2", target_bir_lowering=False, num_devices=1)
    arrays, args = {}, []
    for name in _INS:
        a = _np.ascontiguousarray(inputs[name])
        arrays[f"in_{name}_dram"] = a
        args.append(nc.dram_tensor(f"in_{name}_dram", a.shape, _mybir.dt.from_np(a.dtype), kind="ExternalInput").ap())
    args.append(nc.dram_tensor("out_dram", (1, T, D), F32, kind="ExternalOutput").ap())
    trunk(nc, *args)
    r = _run(nc, [arrays], core_ids=[0])
    return r.results[0]["out_dram"]
```
